# Optimizing a Trainium2 kernel written in Bass

```python
import jax, jax.numpy as jnp
from jax import lax
import numpy as np

D_MODEL = 1024
BATCH = 1
SEQ = 128
DEPTH = 4
DEC_BATCH = 1
DEC_SEQ = 256
PAST_LEN = 128

GRID_W = 64
N_MIXERS = 3
N_A = (DEPTH + 2) // 3
N_B = (DEPTH + 1) // 3
N_C = DEPTH // 3
CHUNK = 64
EPS = 1e-6

A_INNER = 2 * D_MODEL
A_HEADS = 4
A_DH = A_INNER // A_HEADS
A_CONV = 3
A_BLK = 4
A_NBLK = A_INNER // A_BLK

B_HEADS = 4
B_DK = D_MODEL // 2
B_DV = D_MODEL
B_DKH = B_DK // B_HEADS
B_DVH = B_DV // B_HEADS
B_RANK = 16
B_TAU = 16.0

C_HEADS = 16
C_DH = D_MODEL // C_HEADS
C_WIN_H = 8
C_WIN_W = 16

kernel_name = 'bidir_mlstm_gla_natten_prefix_step'

F32 = jnp.float32

def _rmsnorm(x, g):
    xf = x.astype(F32)
    y = xf * lax.rsqrt(jnp.mean(xf * xf, axis=-1, keepdims=True) + EPS)
    return (y * g.astype(F32)).astype(x.dtype)

def _layernorm(x, g):
    xf = x.astype(F32)
    mu = jnp.mean(xf, axis=-1, keepdims=True)
    xc = xf - mu
    y = xc * lax.rsqrt(jnp.mean(xc * xc, axis=-1, keepdims=True) + EPS)
    return (y * g.astype(F32)).astype(x.dtype)

def _modulate(x, g, mod):
    shift, scale, gate = jnp.split(mod, 3, axis=-1)
    return _rmsnorm(x, g) * (1 + scale) + shift, gate

def _heads(x, n, dh):
    b, t, _ = x.shape
    return x.reshape(b, t, n, dh).transpose(0, 2, 1, 3)

def _flip(a, d):
    return jnp.flip(a, axis=2) if d == 1 else a

def _to_chunks(a):
    b, h, t = a.shape[:3]
    a = a.reshape((b, h, t // CHUNK, CHUNK) + a.shape[3:])
    return jnp.moveaxis(a, 2, 0)

def _from_chunks(a):
    a = jnp.moveaxis(a, 0, 2)
    return a.reshape(a.shape[:2] + (a.shape[2] * a.shape[3],) + a.shape[4:])

def _conv_centred(x, w, b):
    y = lax.conv_general_dilated(x, w[:, None, :].astype(x.dtype), window_strides=(1,), padding='SAME',
                                 dimension_numbers=('NWC', 'WIO', 'NWC'), feature_group_count=x.shape[-1])
    return y + b

def _headwise(x, w):
    b, t, _ = x.shape
    return jnp.einsum('btni,nio->btno', x.reshape(b, t, A_NBLK, A_BLK), w).reshape(b, t, A_INNER)

def _mlstm_scan(q, k, v, ig, lf, C0, n0, m0):
    dt = q.dtype
    mask = jnp.tril(jnp.ones((CHUNK, CHUNK), bool))

    def step(carry, inp):
        C, n, m = carry
        qc, kc, vc, igc, lfc = inp
        b = jnp.cumsum(lfc, axis=-1)
        dmat = jnp.where(mask, b[..., :, None] - b[..., None, :] + igc[..., None, :], -jnp.inf)
        inter = b + m[..., None]
        m_t = jnp.maximum(inter, jnp.max(dmat, axis=-1))
        s = jnp.einsum('bhtd,bhsd->bhts', qc, kc) * jnp.exp(dmat - m_t[..., None])
        w_inter = jnp.exp(inter - m_t)
        num = jnp.einsum('bhts,bhsv->bhtv', s, vc) + w_inter[..., None] * jnp.einsum('bhtd,bhdv->bhtv', qc, C)
        den = jnp.sum(s, axis=-1) + w_inter * jnp.einsum('bhtd,bhd->bht', qc, n)
        h = num / jnp.maximum(jnp.abs(den), jnp.exp(-m_t))[..., None]
        bL = b[..., -1]
        w_state = bL[..., None] - b + igc
        m_new = jnp.maximum(bL + m, jnp.max(w_state, axis=-1))
        decay = jnp.exp(bL + m - m_new)
        ws = jnp.exp(w_state - m_new[..., None])
        C_new = decay[..., None, None] * C + jnp.einsum('bhsd,bhsv->bhdv', kc * ws[..., None], vc)
        n_new = decay[..., None] * n + jnp.einsum('bhs,bhsd->bhd', ws, kc)
        return (C_new, n_new, m_new), h

    xs = tuple(_to_chunks(a.astype(F32)) for a in (q, k, v, ig, lf))
    (C, n, m), h = lax.scan(step, (C0.astype(F32), n0.astype(F32), m0.astype(F32)), xs)
    return (C.astype(dt), n.astype(dt), m.astype(dt)), _from_chunks(h).astype(dt)

def _mlstm_mixer(h, C0, n0, m0, w_in, conv_w, conv_b, wq, wk, wv, w_ig, b_ig, w_fg, b_fg, out_g, skip, w_out):
    bsz, t, _ = h.shape
    xm, z = jnp.split(h @ w_in, 2, axis=-1)
    xc = jax.nn.silu(_conv_centred(xm, conv_w, conv_b))
    q = _headwise(xc, wq)
    k = _headwise(xc, wk)
    v = _headwise(xm, wv)
    gin = jnp.concatenate([q, k, v], axis=-1)
    ipre = (jnp.einsum('btc,dch->dbht', gin, w_ig) + b_ig[:, None, :, None]).astype(F32)
    lf = jax.nn.log_sigmoid((jnp.einsum('btc,dch->dbht', gin, w_fg) + b_fg[:, None, :, None]).astype(F32))
    qh = _heads(q, A_HEADS, A_DH) * (A_DH ** -0.5)
    kh = _heads(k, A_HEADS, A_DH)
    vh = _heads(v, A_HEADS, A_DH)
    outs, Cs, ns, ms = [], [], [], []
    for d in range(2):
        (Cd, nd, md), hd = _mlstm_scan(_flip(qh, d), _flip(kh, d), _flip(vh, d), _flip(ipre[d], d),
                                       _flip(lf[d], d), C0[:, d], n0[:, d], m0[:, d])
        outs.append(_flip(hd, d))
        Cs.append(Cd)
        ns.append(nd)
        ms.append(md)
    hsum = (outs[0] + outs[1]).transpose(0, 2, 1, 3)
    hn = _layernorm(hsum, out_g.reshape(A_HEADS, A_DH)).reshape(bsz, t, A_INNER)
    y = ((hn + skip * xc) * jax.nn.silu(z)) @ w_out
    return y, jnp.stack(Cs, axis=1), jnp.stack(ns, axis=1), jnp.stack(ms, axis=1)

def _gla_scan(q, k, v, la, S0):
    dt = q.dtype
    mask = jnp.tril(jnp.ones((CHUNK, CHUNK), bool))

    def step(S, inp):
        qc, kc, vc, lac = inp
        b = jnp.cumsum(lac, axis=2)
        diff = jnp.where(mask[:, :, None], b[:, :, :, None, :] - b[:, :, None, :, :], -jnp.inf)
        att = jnp.einsum('bhtd,bhsd,bhtsd->bhts', qc, kc, jnp.exp(diff))
        o = jnp.einsum('bhts,bhsv->bhtv', att, vc) + jnp.einsum('bhtd,bhdv->bhtv', qc * jnp.exp(b), S)
        bL = b[:, :, -1:, :]
        S_new = jnp.exp(bL[:, :, 0, :])[..., None] * S + jnp.einsum('bhsd,bhsv->bhdv', kc * jnp.exp(bL - b), vc)
        return S_new, o

    xs = tuple(_to_chunks(a.astype(F32)) for a in (q, k, v, la))
    S, o = lax.scan(step, S0.astype(F32), xs)
    return S.astype(dt), _from_chunks(o).astype(dt)

def _gla_mixer(h, S0, w_in, w_a1, w_a2, b_a, out_g, w_out):
    bsz, t, _ = h.shape
    q, k, v, r = jnp.split(h @ w_in, [B_DK, 2 * B_DK, 2 * B_DK + B_DV], axis=-1)
    qh = _heads(q, B_HEADS, B_DKH) * (B_DKH ** -0.5)
    kh = _heads(k, B_HEADS, B_DKH)
    vh = _heads(v, B_HEADS, B_DVH)
    outs, Ss = [], []
    for d in range(2):
        la = jax.nn.log_sigmoid(((h @ w_a1[d]) @ w_a2[d] + b_a[d]).astype(F32)) / B_TAU
        la = _heads(la, B_HEADS, B_DKH)
        Sd, od = _gla_scan(_flip(qh, d), _flip(kh, d), _flip(vh, d), _flip(la, d), S0[:, d])
        outs.append(_flip(od, d))
        Ss.append(Sd)
    o = (outs[0] + outs[1]).transpose(0, 2, 1, 3)
    o = _rmsnorm(o, out_g.reshape(B_HEADS, B_DVH)).reshape(bsz, t, B_DV)
    return (o * jax.nn.silu(r)) @ w_out, jnp.stack(Ss, axis=1)

def _na_project(h, w_in, q_g, k_g):
    q, k, v, g = jnp.split(h @ w_in, 4, axis=-1)
    q = _rmsnorm(_heads(q, C_HEADS, C_DH), q_g)
    k = _rmsnorm(_heads(k, C_HEADS, C_DH), k_g)
    return q, k, _heads(v, C_HEADS, C_DH), g

def _na_context(h, w_in, q_g, k_g, w_out):
    bsz, t, _ = h.shape
    q, k, v, g = _na_project(h, w_in, q_g, k_g)
    s = jnp.einsum('bhqd,bhkd->bhqk', q, k).astype(F32) * (C_DH ** -0.5)
    p = jax.nn.softmax(s, axis=-1).astype(v.dtype)
    o = jnp.einsum('bhqk,bhkd->bhqd', p, v).transpose(0, 2, 1, 3).reshape(bsz, t, D_MODEL)
    return (o * jax.nn.silu(g)) @ w_out, k, v

def _na_latent(h, k_ctx, v_ctx, w_in, q_g, k_g, rpb, w_out):
    bsz, t, _ = h.shape
    rows = t // GRID_W
    win_h = min(C_WIN_H, rows)
    q, k, v, g = _na_project(h, w_in, q_g, k_g)
    qg = q.reshape(bsz, C_HEADS, rows, GRID_W, C_DH)
    kg = k.reshape(bsz, C_HEADS, rows, GRID_W, C_DH)
    vg = v.reshape(bsz, C_HEADS, rows, GRID_W, C_DH)
    cols = jnp.arange(GRID_W)
    col_start = jnp.clip(cols - C_WIN_W // 2, 0, GRID_W - C_WIN_W)
    col_idx = col_start[:, None] + jnp.arange(C_WIN_W)[None, :]
    col_rel = col_idx - cols[:, None] + (C_WIN_W - 1)
    rpb_c = rpb[:, :, col_rel]
    scale = C_DH ** -0.5
    n_loc = win_h * C_WIN_W

    def row_block(r):
        r0 = jnp.clip(r - win_h // 2, 0, rows - win_h)
        q_r = lax.dynamic_index_in_dim(qg, r, axis=2, keepdims=False)
        k_r = lax.dynamic_slice_in_dim(kg, r0, win_h, axis=2)
        v_r = lax.dynamic_slice_in_dim(vg, r0, win_h, axis=2)
        k_w = k_r[:, :, :, col_idx]
        v_w = v_r[:, :, :, col_idx]
        row_rel = r0 + jnp.arange(win_h) - r + (C_WIN_H - 1)
        bias = rpb_c[:, row_rel].transpose(0, 2, 1, 3).astype(F32)
        s_loc = jnp.einsum('bhqd,bhrqwd->bhqrw', q_r, k_w).astype(F32) * scale + bias[None]
        s_ctx = jnp.einsum('bhqd,bhcd->bhqc', q_r, k_ctx).astype(F32) * scale
        s = jnp.concatenate([s_loc.reshape(bsz, C_HEADS, GRID_W, n_loc), s_ctx], axis=-1)
        p = jax.nn.softmax(s, axis=-1).astype(v.dtype)
        p_loc = p[..., :n_loc].reshape(bsz, C_HEADS, GRID_W, win_h, C_WIN_W)
        return (jnp.einsum('bhqrw,bhrqwd->bhqd', p_loc, v_w)
                + jnp.einsum('bhqc,bhcd->bhqd', p[..., n_loc:], v_ctx))

    o = lax.map(row_block, jnp.arange(rows))
    o = o.transpose(1, 0, 3, 2, 4).reshape(bsz, t, D_MODEL)
    return (o * jax.nn.silu(g)) @ w_out

def setup_inputs(seed: int = 0) -> dict:
    key = jax.random.key(seed)
    ks = iter(jax.random.split(key, 48))

    def nrm(shape, scale):
        return jax.random.normal(next(ks), shape, F32) * scale

    def gain(shape):
        return 1.0 + nrm(shape, 0.01)

    D = D_MODEL
    return {
        'x_prompt': nrm((BATCH, SEQ, D), 1.0),
        'x_sample': nrm((DEC_BATCH, DEC_SEQ, D), 1.0),
        'state_mlstm_C': nrm((DEC_BATCH, N_A, 2, A_HEADS, A_DH, A_DH), 0.1),
        'state_mlstm_n': nrm((DEC_BATCH, N_A, 2, A_HEADS, A_DH), 0.1),
        'state_mlstm_m': jax.random.uniform(next(ks), (DEC_BATCH, N_A, 2, A_HEADS), F32, -1.0, 1.0),
        'state_gla_S': nrm((DEC_BATCH, N_B, 2, B_HEADS, B_DKH, B_DVH), 1.0),
        'cache_na_k': nrm((DEC_BATCH, N_C, C_HEADS, PAST_LEN, C_DH), 1.0),
        'cache_na_v': nrm((DEC_BATCH, N_C, C_HEADS, PAST_LEN, C_DH), 1.0),
        'c': nrm((DEC_BATCH, D), 1.0),
        'c_ctx': nrm((D,), 1.0),
        'norm_g': gain((DEPTH, D)),
        'w_mod': nrm((DEPTH, D, 3 * D), 0.5 * D ** -0.5),
        'b_mod': nrm((DEPTH, 3 * D), 0.02),
        'a_w_in': nrm((N_A, D, 2 * A_INNER), D ** -0.5),
        'a_conv_w': nrm((N_A, A_CONV, A_INNER), A_CONV ** -0.5),
        'a_conv_b': nrm((N_A, A_INNER), 0.02),
        'a_wq': nrm((N_A, A_NBLK, A_BLK, A_BLK), A_BLK ** -0.5),
        'a_wk': nrm((N_A, A_NBLK, A_BLK, A_BLK), A_BLK ** -0.5),
        'a_wv': nrm((N_A, A_NBLK, A_BLK, A_BLK), A_BLK ** -0.5),
        'a_w_ig': nrm((N_A, 2, 3 * A_INNER, A_HEADS), (3 * A_INNER) ** -0.5),
        'a_b_ig': nrm((N_A, 2, A_HEADS), 0.1),
        'a_w_fg': nrm((N_A, 2, 3 * A_INNER, A_HEADS), (3 * A_INNER) ** -0.5),
        'a_b_fg': jnp.linspace(3.0, 6.0, A_HEADS, dtype=F32) + nrm((N_A, 2, A_HEADS), 0.1),
        'a_out_g': gain((N_A, A_INNER)),
        'a_skip': gain((N_A, A_INNER)),
        'a_w_out': nrm((N_A, A_INNER, D), A_INNER ** -0.5),
        'b_w_in': nrm((N_B, D, 2 * B_DK + 2 * B_DV), D ** -0.5),
        'b_w_a1': nrm((N_B, 2, D, B_RANK), D ** -0.5),
        'b_w_a2': nrm((N_B, 2, B_RANK, B_DK), B_RANK ** -0.5),
        'b_b_a': nrm((N_B, 2, B_DK), 0.1),
        'b_out_g': gain((N_B, B_DV)),
        'b_w_out': nrm((N_B, B_DV, D), B_DV ** -0.5),
        'c_w_in': nrm((N_C, D, 4 * D), D ** -0.5),
        'c_q_g': gain((N_C, C_DH)),
        'c_k_g': gain((N_C, C_DH)),
        'c_rpb': nrm((N_C, C_HEADS, 2 * C_WIN_H - 1, 2 * C_WIN_W - 1), 0.1),
        'c_w_out': nrm((N_C, D, D), D ** -0.5),
    }

def reference(x_prompt, x_sample, state_mlstm_C, state_mlstm_n, state_mlstm_m, state_gla_S, cache_na_k,
              cache_na_v, c, c_ctx, norm_g, w_mod, b_mod, a_w_in, a_conv_w, a_conv_b, a_wq, a_wk, a_wv,
              a_w_ig, a_b_ig, a_w_fg, a_b_fg, a_out_g, a_skip, a_w_out, b_w_in, b_w_a1, b_w_a2, b_b_a,
              b_out_g, b_w_out, c_w_in, c_q_g, c_k_g, c_rpb, c_w_out):
    sc = jax.nn.silu(c)
    scc = jax.nn.silu(c_ctx)
    yp, ys = x_prompt, x_sample
    bp = x_prompt.shape[0]
    new_C, new_n, new_m, new_S, new_k, new_v = [], [], [], [], [], []
    for l in range(DEPTH):
        kind, j = l % N_MIXERS, l // N_MIXERS
        mod_p = (scc @ w_mod[l] + b_mod[l])[None, None, :]
        mod_s = (sc @ w_mod[l] + b_mod[l])[:, None, :]
        hp, gp = _modulate(yp, norm_g[l], mod_p)
        hs, gs = _modulate(ys, norm_g[l], mod_s)
        if kind == 0:
            pa = (a_w_in[j], a_conv_w[j], a_conv_b[j], a_wq[j], a_wk[j], a_wv[j], a_w_ig[j], a_b_ig[j],
                  a_w_fg[j], a_b_fg[j], a_out_g[j], a_skip[j], a_w_out[j])
            zC = jnp.zeros((bp, 2, A_HEADS, A_DH, A_DH), yp.dtype)
            zn = jnp.zeros((bp, 2, A_HEADS, A_DH), yp.dtype)
            zm = jnp.zeros((bp, 2, A_HEADS), yp.dtype)
            op, Cf, nf, mf = _mlstm_mixer(hp, zC, zn, zm, *pa)
            os_, _, _, _ = _mlstm_mixer(hs, state_mlstm_C[:, j], state_mlstm_n[:, j], state_mlstm_m[:, j], *pa)
            new_C.append(Cf)
            new_n.append(nf)
            new_m.append(mf)
        elif kind == 1:
            pb = (b_w_in[j], b_w_a1[j], b_w_a2[j], b_b_a[j], b_out_g[j], b_w_out[j])
            zS = jnp.zeros((bp, 2, B_HEADS, B_DKH, B_DVH), yp.dtype)
            op, Sf = _gla_mixer(hp, zS, *pb)
            os_, _ = _gla_mixer(hs, state_gla_S[:, j], *pb)
            new_S.append(Sf)
        else:
            op, kc, vc = _na_context(hp, c_w_in[j], c_q_g[j], c_k_g[j], c_w_out[j])
            os_ = _na_latent(hs, cache_na_k[:, j], cache_na_v[:, j], c_w_in[j], c_q_g[j], c_k_g[j],
                             c_rpb[j], c_w_out[j])
            new_k.append(kc)
            new_v.append(vc)
        yp = yp + gp * op
        ys = ys + gs * os_
    return (yp, ys, jnp.stack(new_C, axis=1), jnp.stack(new_n, axis=1), jnp.stack(new_m, axis=1),
            jnp.stack(new_S, axis=1), jnp.stack(new_k, axis=1), jnp.stack(new_v, axis=1))


_drawn_inputs = setup_inputs


def setup_inputs(seed=0):
    import zlib

    import numpy as np

    out = dict(_drawn_inputs(seed))
    spreads = {}
    factors = {'state_mlstm_C': 8.0,
     'state_mlstm_n': 8.0,
     'state_mlstm_m': 8.0,
     'state_gla_S': 19.005,
     'cache_na_k': 3.646,
     'cache_na_v': 2.886,
     'norm_g': 3.845,
     'a_out_g': 35.402,
     'a_skip': 8.0,
     'b_out_g': 43.61,
     'c_q_g': 23.439,
     'c_k_g': 69.008,
     'c_rpb': 22.266,
     'a_b_ig': 3.096}
    for name, (base, spread) in spreads.items():
        noise = np.random.default_rng([zlib.crc32(name.encode()), seed]).standard_normal(out[name].shape)
        drawn = base * np.exp(spread * noise) if base else spread * noise
        out[name] = __import__('jax').numpy.asarray(drawn.astype(out[name].dtype))
    for name, factor in factors.items():
        out[name] = (out[name] * factor).astype(out[name].dtype)
    return out
```

```python
from contextlib import ExitStack

import concourse.bass as bass
from concourse import mybir
from concourse.alu_op_type import AluOpType as ALU

ACT = mybir.ActivationFunctionType
F32 = mybir.dt.float32
I32 = mybir.dt.int32
AX = mybir.AxisListType.X

P = 128
D = 1024
CONSTS = 1
SMALL = 25
FOLD_IN = 7
KD = D // P
NCTX, NLAT = 128, 256
W = NCTX + 1 + NLAT
LAT = NCTX + 1
TOK = (0, LAT, LAT + P)
NT = len(TOK)
TC = NT * P
HALVES = ((0, 256), (256, W))
EPS = 1e-6
KINDS = (0, 1, 2, 0)
DEPTH = len(KINDS)
AH, ADH, AI = 4, 512, 2048
AT_ = AI // P
HT = ADH // P
BH, BDK, BDV, RANK = 4, 128, 256, 16
CH, CDH = 16, 64
GW, ROWS, WINW = 64, 4, 16
B_TAU = 16.0
BIG = 1.0e30
LEVELS = 7
MOD_CHUNKS = 8
MC = 3 * D // MOD_CHUNKS
SLOTS = 2
CHUNK = 4096

def plan():
    chunk0, tile0, last_use, c, t = {}, {}, [], 0, 0
    phases = [("vec", 0, 0, 2), ("load", 0, 0, 6)]

    def mod(l, *parts):
        out = []
        for n in parts if l < DEPTH else ():
            out += [(f"modcol{n - 1}", l, 0, 1)] if n else []
            out += [(f"modrow{n}", l, 1, 1)] + ([(f"modcol{n}", l, 0, 1)] if n == MOD_CHUNKS - 1 else [])
        return out

    fold = [[("fold", 0, 2)]] + [[(f"fold{h}", 0, 4)] for h in range(AH)]
    for l, kind in enumerate(KINDS):
        folds = [[(name, l, *counts) for name, *counts in part] for part in fold]
        if l == 0:
            phases += mod(0, 0, 1) + folds[0] + folds[1] + mod(0, 2, 3) + folds[2] + mod(0, 4, 5) + folds[3]
            phases += mod(0, 6, 7) + folds[4]
        phases += [("norm", l, 0, 2)]
        if kind == 0:
            if l:
                phases += sum(folds, [])
            phases += [("xm", l, 4, 16), ("z", l, 4, 16), ("gate", l, 0, 3), ("pre", l, 0, 12), ("cols", l, 0, 1)]
            for h in range(AH):
                first, second = mod(l + 1, 2 * h), mod(l + 1, 2 * h + 1)
                phases += [(f"first{h}", l, 0, 1)] + first + [(f"c0_{h}", l, 1, 0), (f"state{h}", l, 0, 9)] + second
                phases += [(f"rest{h}", l, 0, 14 if h < AH - 1 else 2)]
            phases += [("out", l, 4, 8)]
        elif kind == 1:
            phases += [("q", l, 1, 4), ("k", l, 1, 4), ("v", l, 2, 6), ("g", l, 2, 8), ("la", l, 0, 10)]
            phases += mod(l + 1, 0, 1, 2, 3, 4, 5) + [("state", l, 0, 6), ("rms", l, 0, 3)] + mod(l + 1, 6, 7)
            phases += [("rms3", l, 0, 1), ("out", l, 2, 8)]
        else:
            phases += [("q", l, 2, 8), ("k", l, 2, 8), ("v", l, 2, 6), ("g", l, 2, 8),
                       ("turn", l, 0, 2), ("qk", l, 0, 20), ("knew", l, 0, 2)]
            for k in range(KD):
                phases += [(f"attn{k}", l, 0, 1)] + mod(l + 1, k)
            phases += [("out", l, 2, 8)]
    phases += [("store", 0, 0, 6)]
    for name, l, chunks, tiles in phases:
        if name in ("xm", "z", "v", "g", "out") or name in ("q", "k") and KINDS[l] == 2:
            assert c % 2 == 0 and t % 2 == 0
        chunk0[name, l], tile0[name, l] = c, t
        for n in range(chunks):
            last_use.append(t + tiles // chunks * (n + 1) - 1)
        if name[:4] == "rest":
            last_use[chunk0[f"c0_{name[4]}", l]] = t
        c, t = c + chunks, t + tiles
    return chunk0, tile0, last_use


CHUNK0, TILE0, LAST_USE = plan()


def trunk(nc, i, o):
    with ExitStack() as ctx:
        def sb(name, cols, dt=F32, rows=P, stack=ctx):
            return stack.enter_context(nc.sbuf_tensor(name, [rows, cols], dt))[:, :]

        def sem(name):
            return ctx.enter_context(nc.semaphore(name))

        acc = [ctx.enter_context(nc.psum_tensor(f"acc{b}", [P, 512], F32))[:, :] for b in range(2)]
        mix = ctx.enter_context(nc.psum_tensor("mix", [P, 6 * 512], F32))[:, :]

        y = sb("y", KD * W)
        hT = sb("hT", KD * W)
        ring = [sb(f"ring{s}", CHUNK) for s in range(SLOTS)]
        ident = sb("ident", P)
        ones = sb("ones", P)
        ones_d = sb("ones_d", P)
        ones_h = sb("ones_h", P)
        vec = sb("vec", 4 * P)
        sc = sb("sc", 2 * KD)
        modv = sb("modv", 3 * KD * 2)
        modr = sb("modr", 3 * KD * 2)
        mst = sb("mst", 2 * MC, rows=2)
        rstd = sb("rstd", W)
        eps = sb("eps", 1)
        m0_all = sb("m0_all", 16)
        rowp = sb("rowp", 6, rows=64)

        V_NORM, V_BMOD = 0, 32
        V_CW, V_CB = P, P + 96
        V_OG, V_SKIP, V_BOG, V_CTX, V_C, V_BA, V_QG, V_KG = (2 * P + x for x in (0, 32, 64, 72, 80, 88, 96, 97))
        V_N0 = 3 * P

        def v3(t, n, w=W):
            return t[:, 0:n * w].rearrange("p (n w) -> p n w", w=w)

        y3, h3 = v3(y, KD), v3(hT, KD)

        def mod_col(part, k, r):
            n = (part * KD + k) * 2 + r
            return modv[:, n:n + 1]

        with ExitStack() as st:
            xm = sb("xm", AT_ * (W + 2), stack=st)
            xc = sb("xc", AT_ * W, stack=st)
            z = sb("z", AT_ * W, stack=st)
            aq = sb("aq", HT * W, stack=st)
            ak = sb("ak", HT * W, stack=st)
            vtok = sb("vtok", NT * ADH, stack=st)
            ktok = sb("ktok", ADH, stack=st)
            kw = [sb(f"kw{d}", ADH, stack=st) for d in range(2)]
            bd = sb("bd", 3 * HT * P, stack=st)
            qs = [sb(f"qs{d}", HT * NLAT, stack=st) for d in range(2)]
            cst = [sb(f"cst{s}", 2 * ADH, stack=st) for s in range(2)]
            pm = [sb(f"pm{d}", 640, stack=st) for d in range(2)]
            fl = [sb(f"fl{d}", TC, stack=st) for d in range(2)]
            rd = [sb(f"rd{d}", TC, stack=st) for d in range(2)]
            wi = [sb(f"wi{d}", NLAT, stack=st) for d in range(2)]
            mask_f = sb("mask_f", TC, stack=st)
            mask_b = sb("mask_b", TC, stack=st)
            mask4 = sb("mask4", 32, stack=st)
            wt4 = sb("wt4", 3 * 4 * AT_, stack=st)
            cols = sb("cols", 4 * 64, stack=st)
            r_ab = sb("r_ab", 2 * TC, rows=64, stack=st)
            r_m = sb("r_m", TC, rows=64, stack=st)
            r_fl = sb("r_fl", TC, rows=64, stack=st)
        r_a, r_b = r_ab[:, 0:TC], r_ab[:, TC:2 * TC]
        nst = r_ab[0:2, 0:ADH]
        gfold = kw[0]
        grow = kw[1][0:16, 0:TC]
        gsel = kw[1][0:16, TC:TC + P]
        vrow = cst[0][:, 0:4 * P]
        r_ig, r_x, r_t = (t[0:64, 0:TC] for t in (pm[0], pm[1], fl[0]))
        r_keep, r_ones, r_ws = (t[0:64, 0:TC] for t in (fl[1], rd[0], rd[1]))
        wg_rows = z[0:48, 0:2048]
        wt_rows = z[0:16, 2048:3584]
        bdt4 = z[:, 3584:5120].rearrange("p (m e c) -> p m e c", m=3, e=HT)
        wg3 = z[:, 5120:5120 + 768].rearrange("p (f n) -> p f n", n=16)
        bd4 = bd.rearrange("p (m e c) -> p m e c", m=3, e=HT)
        g4 = gfold.rearrange("p (f s n) -> p f s n", s=2, n=16)
        qs3 = [v3(t, HT, NLAT) for t in qs]
        vtok3 = v3(vtok, NT, ADH)
        XIN = [xc[:, n * D:(n + 1) * D] for n in range(NT)]
        xm3, xc3, z3 = v3(xm, AT_, W + 2), v3(xc, AT_), v3(z, AT_)
        aq3, ak3 = v3(aq, HT), v3(ak, HT)

        with ExitStack() as st:
            gq = sb("gq", BH * TC, stack=st)
            gk = sb("gk", BH * TC, stack=st)
            gv = sb("gv", NT * D, stack=st)
            gr = sb("gr", KD * W, stack=st)
            dx = [sb(f"dx{s}", 2 * BH * TC, stack=st) for s in range(2)]
            gb = sb("gb", 2 * BH * TC, stack=st)
            fqk = [sb(f"fqk{s}", 2 * BH * TC, stack=st) for s in range(2)]
            gat = sb("gat", BH * TC, stack=st)
            gax = sb("gax", 2 * BH * P, stack=st)
            gs0 = sb("gs0", 2 * BH * BDV, stack=st)
            kf = sb("kf", 2 * BH * P, stack=st)
            kft = sb("kft", 2 * BH * P, stack=st)
            keep = [sb(f"keep{d}", TC, stack=st) for d in range(2)]
            gxor = sb("gxor", P, I32, stack=st)
            gxs = sb("gxs", P, I32, stack=st)
            gmask = sb("gmask", LEVELS * P, I32, stack=st)
            ga1 = sb("ga1", KD * 2 * RANK, stack=st)
            ga2 = sb("ga2", 2 * BH * BDK, rows=RANK, stack=st)
            gha = sb("gha", 2 * W, rows=RANK, stack=st)
        gq3, gk3, gv3, gr3 = v3(gq, BH, TC), v3(gk, BH, TC), v3(gv, NT, D), v3(gr, KD)
        gb4 = gb.rearrange("p (d h t) -> p d h t", d=2, h=BH)
        ga14 = ga1.rearrange("p (k d n) -> p k d n", k=KD, d=2)
        gs03, kft3 = v3(gs0, 2 * BH, BDV), v3(kft, 2 * BH, P)
        gq0 = dx[0][:, 0:2 * BH * NLAT].rearrange("p (d h t) -> p d h t", d=2, h=BH)
        gst = hT[:, 0:2 * BH * BDV]
        go3 = fqk[1][:, 0:KD * TC].rearrange("p (n t) -> p n t", n=KD)
        gsq = hT[:, 0:KD * TC].rearrange("p (n t) -> p n t", n=KD)

        with ExitStack() as st:
            cq = sb("cq", KD * W, stack=st)
            ck = sb("ck", KD * W, stack=st)
            cv = sb("cv", NT * D, stack=st)
            cg = sb("cg", KD * W, stack=st)
            csq = sb("csq", KD * W, stack=st)
            cb = sb("cb", 2 * CH * NLAT, stack=st)
            cwin = sb("cwin", GW, stack=st)
            ckr = sb("ckr", D, stack=st)
            ckc = sb("ckc", D, stack=st)
            cvc = sb("cvc", D, stack=st)
            knt = sb("knt", D, stack=st)
            cp = [sb(f"cp{s}", 896, stack=st) for s in range(2)]
            cpt = [sb(f"cpt{s}", 896, stack=st) for s in range(2)]
            cst_ = [sb(f"cstat{s}", 6, stack=st) for s in range(2)]
            crms = [sb(f"crms{s}", 3 * CH, stack=st) for s in range(2)]
            cqg = sb("cqg", 1, stack=st)
            csel = sb("csel", 2, stack=st)
            zrow = sb("zrow", P, rows=112, stack=st)
            crt = sb("crt", TC, rows=CH, stack=st)
            chead = sb("chead", D, rows=CH, stack=st)
        cq3, ck3, cv3, cg3, csq3 = v3(cq, KD), v3(ck, KD), v3(cv, NT, D), v3(cg, KD), v3(csq, KD)
        cb4 = cb.rearrange("p (q h k) -> p q h k", q=2, h=CH)
        rpb_rows = nc.dram_tensor("rpb_rows", (112, P), F32, kind="Internal").ap()

        small_in = sem("small_in")
        const_made = sem("const_made")
        const_dve = sem("const_dve")
        ring_full = [sem(f"ring_full{s}") for s in range(SLOTS)]
        acc_ready = sem("acc_ready")
        acc_moved = [sem(f"acc_moved{b}") for b in range(2)]
        mod_ready = sem("mod_ready")
        gsel_ready = sem("gsel_ready")
        sq_ready = sem("sq_ready")
        hraw_ready = sem("hraw_ready")
        h_ctx, h_lat = sem("h_ctx"), sem("h_lat")
        act_step, dve_step, pool_step = sem("act_step"), sem("dve_step"), sem("pool_step")
        fold_in = sem("fold_in")
        mask_ready = sem("mask_ready")
        bd_ready = sem("bd_ready")
        conv_step = sem("conv_step")
        xc_ready = sem("xc_ready")
        lse_ready = sem("lse_ready")
        rows_ready = sem("rows_ready")
        rows_exp = sem("rows_exp")
        m_out = sem("m_out")
        cols_ready = sem("cols_ready")
        bcast_ready = sem("bcast_ready")
        s_ready = sem("s_ready")
        e_ready = sem("e_ready")
        x_ready = sem("x_ready")
        w_ready = sem("w_ready")
        p_ready = sem("p_ready")
        den_ready = sem("den_ready")
        a_ready = sem("a_ready")
        qs_ready = sem("qs_ready")
        kw_ready = sem("kw_ready")
        cst_out = [sem(f"cst_out{s}") for s in range(2)]
        nst_out = sem("nst_out")
        num_ready = sem("num_ready")
        hs_moved = sem("hs_moved")
        cen_ready = sem("cen_ready")
        lnsq_ready = sem("lnsq_ready")
        sk_ready = sem("sk_ready")
        u_ready = sem("u_ready")
        y_out = sem("y_out")
        b_in, gmask_ready = sem("b_in"), sem("gmask_ready")
        xla_ready = sem("xla_ready")
        dist_ready = sem("dist_ready")
        fac_ready = sem("fac_ready")
        lq_ready, lk_ready = sem("lq_ready"), sem("lk_ready")
        q2_ready = sem("q2_ready")
        att_ready = sem("att_ready")
        att_moved = sem("att_moved")
        kd_ready, ke_ready, kf_ready = sem("kd_ready"), sem("ke_ready"), sem("kf_ready")
        q0e_ready, q0_ready = sem("q0e_ready"), sem("q0_ready")
        gst_out = sem("gst_out")
        o_ready, o_moved, osq_ready, ub_ready = sem("o_ready"), sem("o_moved"), sem("osq_ready"), sem("ub_ready")
        c_in, rpb_in, rpb_out, bias_in, bias_ready = (sem("c_in"), sem("rpb_in"), sem("rpb_out"), sem("bias_in"),
                                                      sem("bias_ready"))
        csel_ready, chead_ready = sem("csel_ready"), sem("chead_ready")
        csq_ready = sem("csq_ready")
        rms_ready = sem("rms_ready")
        kv_out = sem("kv_out")
        cs_ready = sem("cs_ready")
        mx_ready, cx_ready, cpn_ready = sem("mx_ready"), sem("cx_ready"), sem("cpn_ready")
        ct_ready, cpt_ready = sem("ct_ready"), sem("cpt_ready")

        def tile(name, l, k=0):
            return TILE0[name, l] + k

        def moved(eng, n):
            eng.wait_ge(acc_moved[n % 2], n // 2 + 1)

        def moved_all(eng, name, l, count):
            for n in (tile(name, l, count - 1), tile(name, l, count - 2)):
                moved(eng, n)

        def done_before(eng, l):
            if l < 0:
                return
            moved_all(eng, "out", l, 8)
            if KINDS[l] == 0:
                n = AH * (A_BEFORE[l] + 1)
                eng.wait_ge(cst_out[0], 32 * n)
                eng.wait_ge(cst_out[1], 32 * n)
                eng.wait_ge(nst_out, 16 * n)
                eng.wait_ge(m_out, 32 * (A_BEFORE[l] + 1))
            elif KINDS[l] == 1:
                eng.wait_ge(gst_out, 16)
            else:
                eng.wait_ge(kv_out, 32)

        A_BEFORE = [sum(k == 0 for k in KINDS[:l]) for l in range(DEPTH)]
        N_QN, N_ST, N_N, N_MEAN, N_Q, N_SQ, N_K = 0, 1, 9, 10, 11, 15, 16

        def headtile(l, h, k):
            if k < N_ST:
                return tile(f"first{h}", l)
            return tile(f"state{h}", l, k - N_ST) if k < N_MEAN else tile(f"rest{h}", l, k - N_MEAN)

        def qkv_tiles(l, h):
            if h == 0:
                return [tile("pre", l, n) for n in range(12)]
            return [headtile(l, h - 1, n) for n in (*range(N_Q, N_Q + 4), *range(N_K, N_K + 8))]

        def sqtile(l, h):
            return headtile(l, h, N_SQ if h < AH - 1 else N_MEAN + 1)

        def rmstile(l, h):
            return tile("rms", l, h) if h < BH - 1 else tile("rms3", l)

        def seg(col0, n=None):
            return slice(col0, col0 + n)

        block = ctx.enter_context(nc.Block())

        @block.sync
        def _(sp):
            def halves(slot, dst, src):
                n = len(dst) if isinstance(dst, list) else None
                for e in range(2):
                    if n:
                        sp.dma_start(dst[e], src[e]).then_inc(ring_full[slot], 16)
                    else:
                        k = slice(e * dst.shape[1] // 2, (e + 1) * dst.shape[1] // 2)
                        sp.dma_start(dst[:, k], src[:, k]).then_inc(ring_full[slot], 16)

            def chunk(g, dst, src):
                if g >= 2:
                    sp.wait_ge(acc_ready, LAST_USE[g - 2] + 1)
                halves(g % 2, dst, src)

            def stream(name, l, n, w, cols_, k):
                g0 = CHUNK0[name, l]
                src = w.rearrange("(k p) n -> p k n", p=P)
                dst = [ring[s][:, 0:k * cols_].rearrange("p (k n) -> p k n", k=k) for s in range(2)]
                for s in range(min(n, 2)):
                    chunk(g0 + s, dst[(g0 + s) % 2], src[:, :, s * cols_:(s + 1) * cols_])
                if n > 2:
                    per = LAST_USE[g0 + 1] - LAST_USE[g0]
                    with sp.Fori(0, n // 2 - 1) as it:
                        for s in range(2):
                            sp.wait_ge(acc_ready, it * (2 * per) + (LAST_USE[g0 + s] + 1))
                            halves(s, dst[s], src[:, :, bass.ds(it * (2 * cols_) + (2 + s) * cols_, cols_)])

            def mod_chunk(l, n):
                if l < DEPTH:
                    g = CHUNK0[f"modrow{n}", l]
                    chunk(g, ring[g % 2][:, 0:KD * MC].rearrange("p (k n) -> p k n", k=KD),
                          i["w_mod"][l].rearrange("(k p) n -> p k n", p=P)[:, :, n * MC:(n + 1) * MC])

            for n in range(NT):
                src = i["x_prompt"][0] if n == 0 else i["x_sample"][0, (n - 1) * P:n * P]
                sp.dma_start(XIN[n], src).then_inc(small_in, 16)
            for l, kind in enumerate(KINDS):
                if l == 0:
                    for n in range(MOD_CHUNKS):
                        mod_chunk(0, n)
                if kind == 0:
                    j = A_BEFORE[l]
                    stream("xm", l, 4, i["a_w_in"][j, :, 0:AI], 512, KD)
                    stream("z", l, 4, i["a_w_in"][j, :, AI:2 * AI], 512, KD)
                    for h in range(AH):
                        mod_chunk(l + 1, 2 * h)
                        g = CHUNK0[f"c0_{h}", l]
                        chunk(g, [ring[g % 2][:, seg(d * 2048, 2048)].rearrange("p (k n) -> p k n", k=HT)
                                  for d in range(2)],
                              [i["state_mlstm_C"][0, j, d, h].rearrange("(k p) n -> p k n", p=P) for d in range(2)])
                        mod_chunk(l + 1, 2 * h + 1)
                    stream("out", l, 4, i["a_w_out"][j], 256, AT_)
                elif kind == 1:
                    w = i["b_w_in"][0]
                    stream("q", l, 1, w[:, 0:512], 512, KD)
                    stream("k", l, 1, w[:, 512:1024], 512, KD)
                    stream("v", l, 2, w[:, 1024:2048], 512, KD)
                    stream("g", l, 2, w[:, 2048:3072], 512, KD)
                    for n in range(MOD_CHUNKS):
                        mod_chunk(l + 1, n)
                    stream("out", l, 2, i["b_w_out"][0], 512, KD)
                else:
                    w = i["c_w_in"][0]
                    for n, name in enumerate("qkvg"):
                        stream(name, l, 2, w[:, n * D:(n + 1) * D], 512, KD)
                    for n in range(MOD_CHUNKS):
                        mod_chunk(l + 1, n)
                    stream("out", l, 2, i["c_w_out"][0], 512, KD)
            for n in range(NT):
                for half in range(2):
                    moved(sp, tile("store", 0, 2 * n + half))
                dst = o["y_prompt"][0] if n == 0 else o["y_sample"][0, (n - 1) * P:n * P]
                sp.dma_start(dst, XIN[n]).then_inc(y_out, 16)
            sp.wait_ge(y_out, 16 * NT)

        @block.tensor
        def _(pe):
            def bank(n):
                if n >= 2:
                    pe.wait_ge(acc_moved[n % 2], n // 2)
                return acc[n % 2]

            def mm(out, lhsT, rhs, start, stop):
                return nc.tensor.matmul(out, lhsT=lhsT, rhs=rhs, start=start, stop=stop)

            def group(out, pairs):
                for n, (a, b) in enumerate(pairs):
                    ins = mm(out, a, b, n == 0, n == len(pairs) - 1)
                return ins

            def linear(name, l, n, k, m, rhs, width, tokens=False):
                g0, t0 = CHUNK0[name, l], TILE0[name, l]
                per = NT if tokens else m
                cols_ = m * P

                def body(turn, slots):
                    for s, slot in enumerate(slots):
                        w3 = ring[slot][:, 0:k * cols_].rearrange("p (k n) -> p k n", k=k)
                        pe.wait_ge(ring_full[slot], turn * 32 + 32 * ((g0 + s) // 2 + 1))
                        for e in range(per):
                            t = s * per + e
                            if t0 + t >= 2 or not isinstance(turn, int):
                                pe.wait_ge(acc_moved[(t0 + t) % 2], turn * per + (t0 + t) // 2)
                            ps = acc[(t0 + t) % 2]
                            for kk in range(k):
                                if tokens:
                                    ins = mm(ps[:, 0:cols_], rhs[:, kk, seg(TOK[e], P)], w3[:, kk, :], kk == 0, kk == k - 1)
                                else:
                                    ins = mm(ps[:, 0:width], w3[:, kk, e * P:(e + 1) * P], rhs[:, kk, :], kk == 0, kk == k - 1)
                            ins.then_inc(acc_ready, 1)

                if n == 1:
                    body(0, [g0 % 2])
                else:
                    with pe.Fori(0, n // 2) as it:
                        body(it, [0, 1])

            def transposes(n, parts):
                ps = bank(n)
                for out, src in parts:
                    ins = nc.tensor.transpose(out(ps), src, ident[0:src.shape[0], 0:src.shape[0]])
                ins.then_inc(acc_ready, 1)

            pe.wait_ge(const_made, CONSTS)
            pe.wait_ge(const_dve, 1)
            pe.wait_ge(small_in, 16 * SMALL)
            transposes(tile("vec", 0, 0), [(lambda ps, n=n: ps[:, n * P:(n + 1) * P], vrow[:, n * P:(n + 1) * P])
                                           for n in range(4)])
            transposes(tile("vec", 0, 1), [(lambda ps: ps[:, 0:P], vrow[:, 2 * P:3 * P])])
            for n in range(2 * NT):
                transposes(tile("load", 0, n), [
                    (lambda ps, e=e: ps[:, e * P:(e + 1) * P],
                     XIN[n // 2][:, (4 * (n % 2) + e) * P:(4 * (n % 2) + e + 1) * P]) for e in range(4)])

            def mod_columns(l, n):
                t = tile(f"modrow{n}", l)
                moved(pe, t)
                transposes(tile(f"modcol{n}", l), [
                    (lambda ps, e=e: ps[:, 2 * e:2 * e + 2], mst[:, seg(n % 2 * MC + e * P, P)])
                    for e in range(MC // P)])

            def mod_part(l, n):
                if l == DEPTH:
                    return
                if n:
                    mod_columns(l, n - 1)
                g = CHUNK0[f"modrow{n}", l]
                ps = bank(tile(f"modrow{n}", l))
                pe.wait_ge(ring_full[g % 2], 32 * (g // 2 + 1))
                w3 = ring[g % 2][:, 0:KD * MC].rearrange("p (k n) -> p k n", k=KD)
                group(ps[0:2, 0:MC], [(sc[:, 2 * k:2 * k + 2], w3[:, k, :]) for k in range(KD)]
                      ).then_inc(acc_ready, 1)
                if n == MOD_CHUNKS - 1:
                    mod_columns(l, n)

            def norm(l):
                ps = [bank(tile("norm", l, n)) for n in range(2)]
                for k in range(KD):
                    pe.wait_ge(sq_ready, KD * l + k + 1)
                    for n, (c0, c1) in enumerate(HALVES):
                        ins = mm(ps[n][:, 0:c1 - c0], ones_d[:, :], h3[:, k, c0:c1], k == 0, k == KD - 1)
                        if k == KD - 1:
                            ins.then_inc(acc_ready, 1)

            def fold_start(l):
                ia = A_BEFORE[l]
                pe.wait_ge(fold_in, 16 * FOLD_IN * (ia + 1))
                for t in range(2):
                    parts = [(lambda ps, n=n: ps[:, n * 48:(n + 1) * 48],
                              wg_rows[:, (2 * t + n // 4) * 512 + n % 4:(2 * t + n // 4 + 1) * 512:4])
                             for n in range(8)]
                    parts += [(lambda ps, n=n: ps[:, 384 + n * 16:384 + (n + 1) * 16], wt_rows[:, (6 * t + n) // 4 * 512 + (6 * t + n) % 4:((6 * t + n) // 4 + 1) * 512:4])
                              for n in range(6)]
                    transposes(tile("fold", l, t), parts)

            def fold(l, h):
                pe.wait_ge(bd_ready, 8 * A_BEFORE[l] + h + 1)
                for m in range(3):
                    transposes(tile(f"fold{h}", l, m),
                               [(lambda ps, e=e: ps[:, e * P:(e + 1) * P], bd4[:, m, e, :]) for e in range(HT)])
                ps = bank(tile(f"fold{h}", l, 3))
                for m in range(3):
                    moved(pe, tile(f"fold{h}", l, m))
                for e in range(HT):
                    f = h * HT + e
                    mm(ps[:, e * 32:e * 32 + 16], bdt4[:, 0, e, :], wg3[:, f, :], e == 0, False)
                    mm(ps[:, e * 32:e * 32 + 16], bdt4[:, 1, e, :], wg3[:, AT_ + f, :], False, False)
                    ins = mm(ps[:, e * 32 + 16:e * 32 + 32], bdt4[:, 2, e, :], wg3[:, 2 * AT_ + f, :],
                             False, e == HT - 1)
                ins.then_inc(acc_ready, 1)

            def qkv(l, h, part):
                ia = A_BEFORE[l]
                tiles = qkv_tiles(l, h)
                if part != 1:
                    pe.wait_ge(bd_ready, 8 * ia + 4 + h + 1)
                    for e in range(HT):
                        mm(bank(tiles[e])[:, 0:W], bd4[:, 0, e, :], xc3[:, HT * h + e, :], True, True
                           ).then_inc(acc_ready, 1)
                if part != 0:
                    for e in range(HT):
                        mm(bank(tiles[4 + e])[:, 0:W], bd4[:, 1, e, :], xc3[:, HT * h + e, :], True, True
                           ).then_inc(acc_ready, 1)
                    for t in range(NT):
                        ps = bank(tiles[8 + t])
                        for e in range(HT):
                            ins = mm(ps[:, e * P:(e + 1) * P], xm3[:, HT * h + e, seg(1 + TOK[t], P)],
                                     bd4[:, 2, e, :], e == 0, e == HT - 1)
                        ins.then_inc(acc_ready, 1)
                    ps = bank(tiles[11])
                    for e in range(HT):
                        ins = mm(ps[:, e * P:(e + 1) * P], xc3[:, HT * h + e, 0:P], bd4[:, 1, e, :],
                                 e == 0, e == HT - 1)
                    ins.then_inc(acc_ready, 1)

            def head(l, h):
                ia = A_BEFORE[l]
                H = AH * ia + h
                for n in qkv_tiles(l, h):
                    moved(pe, n)
                if H >= 1:
                    pe.wait_ge(hs_moved, H)
                for n in range(4):
                    d = n % 2
                    src = r_m if n < 2 else r_fl
                    ins = mm(mix[:, seg((2 + n) * 512, TC)],
                             ident[0:64, 32 * d + h:32 * d + h + 1].to_broadcast([64, P]), src[:, :], True, True)
                ins.then_inc(bcast_ready, 1)
                if H >= 1:
                    pe.wait_ge(p_ready, 2 * H)
                group(mix[:, 0:P], [(ak3[:, k, 0:P], aq3[:, k, 0:P]) for k in range(HT)])
                for k in range(HT):
                    mm(mix[:, P:P + NLAT], ak3[:, k, seg(TOK[1], P)], aq3[:, k, LAT:W], k == 0, k == HT - 1)
                group(mix[:, 512:512 + NLAT], [(ak3[:, k, seg(TOK[2], P)], aq3[:, k, LAT:W]) for k in range(HT)]
                      ).then_inc(s_ready, 1)
                ps = bank(headtile(l, h, N_QN))
                for d in range(2):
                    ins = group(ps[:, d * NLAT:(d + 1) * NLAT],
                                [(vec[:, seg(V_N0 + ((ia * 2 + d) * AH + h) * HT + k, 1)].to_broadcast([P, P]),
                                  aq3[:, k, LAT:W]) for k in range(HT)])
                ins.then_inc(acc_ready, 1)

                def state(d):
                    pe.wait_ge(kw_ready, 2 * H + d + 1)
                    for k in range(HT):
                        mm(bank(headtile(l, h, N_ST + 4 * d + k))[:, :], kw[d][:, k * P:(k + 1) * P],
                           vtok[:, 0:ADH], True, True).then_inc(acc_ready, 1)

                mod_part(l + 1, 2 * h)
                for d in range(2):
                    pe.wait_ge(p_ready, 2 * H + d + 1)
                    pe.wait_ge(w_ready, 2 * H + d + 1)
                    ps = mix[:, seg((2 + d) * 512, TC)]
                    mm(ps[:, 0:P], ones[:, :], pm[d][:, 0:P], True, True)
                    mm(ps[:, P:TC], ones[:, :], pm[d][:, P:TC], True, False)
                    mm(ps[:, P:TC], ones[:, :], pm[d][:, TC:640], False, True).then_inc(den_ready, 1)
                state(0)
                state(1)
                mm(bank(headtile(l, h, N_N))[0:2, :], cols[:, 3 * 64 + h:4 * 64:32], ktok[:, :], True, True
                   ).then_inc(acc_ready, 1)
                mod_part(l + 1, 2 * h + 1)
                g = CHUNK0[f"c0_{h}", l]
                pe.wait_ge(ring_full[g % 2], 32 * (g // 2 + 1))
                pe.wait_ge(a_ready, H + 1)
                pe.wait_ge(qs_ready, 2 * H + 2)
                c04 = ring[g % 2].rearrange("p (d k n) -> p d k n", d=2, k=HT)
                for e in range(HT):
                    ps = mix[:, seg((2 + e) * 512, W)]
                    v = slice(e * P, (e + 1) * P)
                    pairs = [(c04[:, d, k, v], qs3[d][:, k, :]) for d in range(2) for k in range(HT)]
                    pairs += [(vtok3[:, t, v], pm[0][:, t * 256 - P:t * 256 + P]) for t in (1, 2)]
                    group(ps[:, LAT:W], pairs)
                    ins = mm(ps[:, 0:P], vtok3[:, 0, v], pm[0][:, 0:P], True, True)
                ins.then_inc(num_ready, 1)

            def head_mean(l, h):
                H = AH * A_BEFORE[l] + h
                pe.wait_ge(hs_moved, H + 1)
                group(bank(headtile(l, h, N_MEAN))[:, 0:W], [(ones_h[:, :], h3[:, k, :]) for k in range(HT)]
                      ).then_inc(acc_ready, 1)

            def head_square(l, h):
                pe.wait_ge(lnsq_ready, AH * A_BEFORE[l] + h + 1)
                group(bank(sqtile(l, h))[:, 0:W], [(ones_h[:, :], h3[:, HT + k, :]) for k in range(HT)]
                      ).then_inc(acc_ready, 1)

            def mlstm(l):
                ia = A_BEFORE[l]
                linear("xm", l, 4, KD, 4, h3, W)
                linear("z", l, 4, KD, 4, h3, W)
                t = tile("gate", l, 0)
                moved(pe, tile("fold3", l, 3))
                pairs = [(g4[:, f, 1, :], xm3[:, f, 1:1 + W]) for f in range(AT_)]
                pairs += [(g4[:, f, 0, :], xc3[:, f, :]) for f in range(AT_)]
                ps = bank(t)
                for n, (a, b) in enumerate(pairs):
                    if n == AT_:
                        pe.wait_ge(xc_ready, AT_ * (ia + 1))
                    ins = mm(ps[0:16, 0:W], a, b, n == 0, n == len(pairs) - 1)
                ins.then_inc(acc_ready, 1)
                moved(pe, t)
                pe.wait_ge(gsel_ready, ia + 1)
                for kind in range(2):
                    mm(bank(tile("gate", l, 1 + kind))[0:64, 0:TC], gsel[:, seg(64 * kind, 64)], grow, True, True
                       ).then_inc(acc_ready, 1)
                qkv(l, 0, 2)
                pe.wait_ge(rows_ready, ia + 1)
                pe.wait_ge(rows_exp, ia + 1)
                transposes(tile("cols", l, 0),
                           [(lambda ps, e=e: ps[:, e * 64:(e + 1) * 64],
                             (r_a[:, e * P:(e + 1) * P] if e < 3 else r_ws[:, 0:P])) for e in range(4)])
                for h in range(AH):
                    head(l, h)
                    head_mean(l, h)
                    if h < AH - 1:
                        qkv(l, h + 1, 0)
                    head_square(l, h)
                    if h < AH - 1:
                        qkv(l, h + 1, 1)
                pe.wait_ge(u_ready, AH * (ia + 1))
                linear("out", l, 4, AT_, 2, z3, W)

            def gla(l):
                linear("q", l, 1, KD, 4, h3, W)
                linear("k", l, 1, KD, 4, h3, W)
                linear("v", l, 2, KD, 4, h3, W, tokens=True)
                linear("g", l, 2, KD, 4, h3, W)
                pe.wait_ge(b_in, 16 * 5)
                for d in range(2):
                    group(bank(tile("la", l, d))[0:RANK, 0:W], [(ga14[:, k, d, :], h3[:, k, :]) for k in range(KD)]
                          ).then_inc(acc_ready, 1)
                for d in range(2):
                    moved(pe, tile("la", l, d))
                    for h in range(BH):
                        n = d * BH + h
                        mm(bank(tile("la", l, 2 + n))[:, 0:W], ga2[:, n * BDK:(n + 1) * BDK],
                           gha[:, d * W:(d + 1) * W], True, True).then_inc(acc_ready, 1)
                for n in range(MOD_CHUNKS - 2):
                    mod_part(l + 1, n)
                pe.wait_ge(kf_ready, 1)
                for n in range(2):
                    transposes(tile("state", l, n), [
                        (lambda ps, e=e: ps[:, e * P:(e + 1) * P], kf[:, (4 * n + e) * P:(4 * n + e + 1) * P])
                        for e in range(4)])
                moved_all(pe, "state", l, 2)
                for n in range(4):
                    ps = bank(tile("state", l, 2 + n))
                    for e in range(2):
                        m = 2 * n + e
                        ins = mm(ps[:, e * BDV:(e + 1) * BDV], kft3[:, m, :],
                                 gv3[:, 0, seg((m % BH) * BDV, BDV)], True, True)
                    ins.then_inc(acc_ready, 1)
                for n, level in enumerate(range(LEVELS + 1, -1, -1)):
                    fq, fk = (fqk[level % 2][:, e * BH * TC:(e + 1) * BH * TC] for e in range(2))
                    half = (level % 2) * 3 * 512
                    if level:
                        pe.wait_ge(lq_ready, n + 1)
                        pe.wait_ge(lk_ready, n + 1)
                    else:
                        pe.wait_ge(q2_ready, 1)
                    if n >= 2:
                        pe.wait_ge(att_moved, n - 1)
                    if level > LEVELS:
                        for m in range(2 * BH):
                            h, back = divmod(m, 2)
                            ins = mm(mix[:, seg(half + m * P, P)], fk[:, seg(h * NLAT + back * P, P)],
                                     fq[:, seg(h * NLAT + (1 - back) * P, P)], True, True)
                    else:
                        for m in range(BH * NT):
                            ins = mm(mix[:, seg(half + m * P, P)], (fk if level else gk)[:, seg(m * P, P)],
                                     fq[:, seg(m * P, P)], True, True)
                    ins.then_inc(att_ready, 1)
                pe.wait_ge(att_moved, LEVELS + 2)
                pe.wait_ge(q0_ready, 1)
                for n in range(2 * BH):
                    h = n // 2
                    if n >= 6:
                        pe.wait_ge(o_moved, n - 5)
                    ps = mix[:, seg((3 + n) % 6 * 512, TC)]
                    v = slice(n * P, (n + 1) * P)
                    for d in range(2):
                        mm(ps[:, P:TC], gs03[:, d * BH + h, (n % 2) * P:(n % 2 + 1) * P], gq0[:, d, h, :], d == 0, False)
                    for t in (1, 2):
                        mm(ps[:, t * P:(t + 1) * P], gv3[:, t, v], gat[:, seg((h * NT + t) * P, P)], False, False)
                        mm(ps[:, t * P:(t + 1) * P], gv3[:, 3 - t, v], gax[:, seg((2 * h + 2 - t) * P, P)],
                           False, t == 2)
                    mm(ps[:, 0:P], gv3[:, 0, v], gat[:, seg(h * NT * P, P)], True, True).then_inc(o_ready, 1)
                    if n % 2 and h:
                        gla_rms(l, h - 1)
                for n in range(MOD_CHUNKS - 2, MOD_CHUNKS):
                    mod_part(l + 1, n)
                gla_rms(l, BH - 1)
                pe.wait_ge(ub_ready, BH)
                linear("out", l, 2, KD, 4, gr3, W)

            def gla_rms(l, h):
                pe.wait_ge(osq_ready, h + 1)
                group(bank(rmstile(l, h))[:, 0:TC], [(ones[:, :], gsq[:, 2 * h + e, :]) for e in range(2)]
                      ).then_inc(acc_ready, 1)

            def natten(l):
                for name in "qk":
                    linear(name, l, 2, KD, 4, h3, W)
                linear("v", l, 2, KD, 4, h3, W, tokens=True)
                linear("g", l, 2, KD, 4, h3, W)
                pe.wait_ge(c_in, 32)
                for n in range(2):
                    transposes(tile("turn", l, n), [
                        (lambda ps, e=e: ps[:, e * P:(e + 1) * P], ckr[:, (4 * n + e) * P:(4 * n + e + 1) * P])
                        for e in range(4)])
                pe.wait_ge(csel_ready, 1)
                for s, x3 in enumerate((cq3, ck3)):
                    pe.wait_ge(csq_ready, s + 1)
                    ps = bank(tile("qk", l, 10 * s))
                    for t in range(NT):
                        for k in range(KD):
                            ins = mm(ps[:, t * CH + 2 * k:t * CH + 2 * k + 2], csq3[:, k, seg(TOK[t], P)], csel[:, :],
                                     True, True)
                    ins.then_inc(acc_ready, 1)
                    pe.wait_ge(rms_ready, s + 1)
                    t = tile("qk", l, 10 * s + 1)
                    transposes(t, [(lambda ps, e=e: ps[0:CH, e * P:(e + 1) * P], crms[s][:, e * CH:(e + 1) * CH])
                                   for e in range(NT)])
                    moved(pe, t)
                    for k in range(KD):
                        mm(bank(tile("qk", l, 10 * s + 2 + k))[:, 0:TC], chead[:, k * P:(k + 1) * P], crt[:, :], True, True
                           ).then_inc(acc_ready, 1)
                moved_all(pe, "qk", l, 20)
                for n in range(2):
                    transposes(tile("knew", l, n), [
                        (lambda ps, e=e: ps[:, e * P:(e + 1) * P], ck3[:, 4 * n + e, 0:P]) for e in range(4)])

                def scores(h):
                    k, r = h // 2, slice(64 * (h % 2), 64 * (h % 2) + 64)
                    if h:
                        pe.wait_ge(cx_ready, h)
                    mm(mix[:, 0:P], cq3[r, k, 0:P], ck3[r, k, 0:P], True, True)
                    for q in (1, 2):
                        ps = mix[:, seg(q * 512, TC)]
                        qt = cq3[r, k, seg(TOK[q], P)]
                        mm(ps[:, 0:NLAT], qt, ck3[r, k, LAT:W], True, False)
                        mm(ps[:, 0:NLAT], ident[:, :], cb4[:, q - 1, h, :], False, True)
                        ins = mm(ps[:, NLAT:TC], qt, ckc[r, k * P:(k + 1) * P], True, True)
                    ins.then_inc(cs_ready, 1)

                def turn(h):
                    pe.wait_ge(cpn_ready, h + 1)
                    if h:
                        pe.wait_ge(cpt_ready, h)
                    for b in range(7):
                        ins = nc.tensor.transpose(mix[:, seg(3 * 512 + b * P, P)], cp[h % 2][:, b * P:(b + 1) * P],
                                                  ident[:, :])
                    ins.then_inc(ct_ready, 1)

                def values(h):
                    pe.wait_ge(cpt_ready, h + 1)
                    k, r = h // 2, slice(64 * (h % 2), 64 * (h % 2) + 64)
                    t = tile(f"attn{k}", l)
                    ps = acc[t % 2]
                    if h % 2 == 0:
                        bank(t)
                    hv = slice(h * CDH, (h + 1) * CDH)
                    pt = cpt[h % 2]
                    mm(ps[r, 0:P], cv3[:, 0, hv], pt[:, 0:P], True, True)
                    for b, v in enumerate((cv3[:, 1, hv], cv3[:, 2, hv], cvc[:, hv])):
                        both = pt[:, P:896].rearrange("p (q b t) -> p q b t", q=2, b=3)[:, :, b, :]
                        ins = mm(ps[r, P:TC].rearrange("p (q t) -> p q t", q=2), v, both, b == 0, b == 2)
                    if h % 2:
                        ins.then_inc(acc_ready, 1)

                moved_all(pe, "turn", l, 2)
                pe.wait_ge(bias_ready, 1)
                scores(0)
                for h in range(CH):
                    if h + 1 < CH:
                        scores(h + 1)
                    turn(h)
                    if h:
                        values(h - 1)
                    if h and h % 2 == 0:
                        mod_part(l + 1, h // 2 - 1)
                values(CH - 1)
                mod_part(l + 1, KD - 1)
                moved(pe, tile(f"attn{KD - 1}", l))
                moved(pe, tile(f"attn{KD - 2}", l))
                linear("out", l, 2, KD, 4, cg3, W)

            moved(pe, tile("vec", 0, 1))
            for l, kind in enumerate(KINDS):
                if l == 0:
                    mod_part(0, 0)
                    mod_part(0, 1)
                    fold_start(0)
                    for h in range(AH):
                        fold(0, h)
                        if h < AH - 1:
                            mod_part(0, 2 * h + 2)
                            mod_part(0, 2 * h + 3)
                norm(l)
                if kind == 0 and l:
                    fold_start(l)
                    for h in range(AH):
                        fold(l, h)
                pe.wait_ge(h_ctx, l + 1)
                pe.wait_ge(h_lat, l + 1)
                [mlstm, gla, natten][kind](l)
            moved_all(pe, "out", DEPTH - 1, 8)
            for n in range(2 * NT):
                transposes(tile("store", 0, n), [
                    (lambda ps, e=e: ps[:, e * P:(e + 1) * P],
                     y3[:, 4 * (n % 2) + e, seg(TOK[n // 2], P)]) for e in range(4)])

        @block.scalar
        def _(act):
            steps = [0]

            def link(ins):
                steps[0] += 1
                ins.then_inc(act_step, 1)
                act.wait_ge(act_step, steps[0])

            def ready(n):
                act.wait_ge(acc_ready, n + 1)
                return acc[n % 2]

            def move(n, out, src=lambda ps: ps, func=ACT.Copy, **kw_):
                nc.scalar.activation(out, src(ready(n)), func, **kw_).then_inc(acc_moved[n % 2], 1)

            def pair_loop(t0, count, step):
                with act.Fori(0, count // 2) as it:
                    for e in range(2):
                        act.wait_ge(acc_ready, it * 2 + (t0 + e + 1))
                        step(it, e, acc[(t0 + e) % 2]).then_inc(acc_moved[(t0 + e) % 2], 1)

            act.wait_ge(const_dve, 1)

            def rows(r0, w, block=None):
                n = 1
                for x in w.shape:
                    n *= x
                b, r = divmod(r0, P)
                flat = w.rearrange(" ".join("abcde"[:len(w.shape)]) + " -> (" + " ".join("abcde"[:len(w.shape)]) + ")")
                act.dma_start(vrow[r:r + n // P, b * P:(b + 1) * P], flat.rearrange("(r c) -> r c", c=P)
                              ).then_inc(small_in, 16)

            rows(V_NORM, i["norm_g"])
            rows(V_BMOD, i["b_mod"])
            rows(V_CW, i["a_conv_w"])
            rows(V_CB, i["a_conv_b"])
            rows(V_OG, i["a_out_g"])
            rows(V_SKIP, i["a_skip"])
            rows(V_BOG, i["b_out_g"])
            rows(V_CTX, i["c_ctx"])
            rows(V_C, i["c"])
            rows(V_BA, i["b_b_a"])
            rows(V_N0, i["state_mlstm_n"])
            for r0, g in ((V_QG, i["c_q_g"]), (V_KG, i["c_k_g"])):
                for half in range(2):
                    act.dma_start(vrow[r0 - 2 * P:r0 - 2 * P + 1, seg(2 * P + half * CDH, CDH)], g).then_inc(small_in, 16)
            act.dma_start(m0_all[:, :], i["state_mlstm_m"].rearrange("a j d h -> a (j d h)").to_broadcast([P, 16])
                          ).then_inc(small_in, 16)
            for n, w in enumerate((i["a_b_ig"], i["a_b_fg"], i["state_mlstm_m"][0])):
                for d in range(2):
                    act.dma_start(rowp[32 * d:32 * d + AH, 2 * n:2 * n + 2], w[:, d].rearrange("j h -> h j"),
                                  allow_slow_non_contiguous=True).then_inc(small_in, 16)

            move(tile("vec", 0, 0), vec[:, :])
            move(tile("vec", 0, 1), sc.rearrange("p (k r) -> p r k", r=2),
                 lambda ps: ps[:, V_CTX - 2 * P:V_CTX - 2 * P + 16].rearrange("p (r k) -> p r k", r=2), ACT.Silu)
            for n in range(2 * NT):
                k0 = 4 * (n % 2)
                move(tile("load", 0, n), y3[:, k0:k0 + 4, seg(TOK[n // 2], P)],
                     lambda ps: ps[:, :].rearrange("p (e t) -> p e t", e=4))

            def fold_start(l):
                for t in range(2):
                    ps = ready(tile("fold", l, t))
                    nc.scalar.copy(wg3[:, :, 8 * t:8 * t + 8].rearrange("p f n -> p n f"),
                                   ps[:, 0:384].rearrange("p (n f) -> p n f", n=8))
                    move(tile("fold", l, t), wt4[:, 96 * t:96 * t + 96], lambda ps: ps[:, 384:480])

            def fold(l, h):
                for m in range(3):
                    move(tile(f"fold{h}", l, m), bdt4[:, m], lambda ps: ps[:, :].rearrange("p (e c) -> p e c", e=HT))
                move(tile(f"fold{h}", l, 3), gfold[:, h * P:(h + 1) * P], lambda ps: ps[:, 0:P])

            def mod_part(l, n):
                if l == DEPTH:
                    return
                for m, last in ((n - 1, False), (n, True)):
                    if m >= 0 and (not last or n == MOD_CHUNKS - 1):
                        if last:
                            mod_row(l, n)
                        move(tile(f"modcol{m}", l), modr[:, seg(6 * m, 6)], lambda ps: ps[:, 0:6])
                if n < MOD_CHUNKS - 1:
                    mod_row(l, n)

            def mod_row(l, n):
                move(tile(f"modrow{n}", l), mst[:, seg(n % 2 * MC, MC)], lambda ps: ps[0:2, 0:MC])

            def norm(l):
                if l:
                    t0 = tile("out", l - 1)
                    with act.Fori(0, KD // 2) as it:
                        for e in range(2):
                            act.wait_ge(acc_moved[(t0 + e) % 2], it + ((t0 + e) // 2 + 1))
                            nc.scalar.activation(hT[:, bass.ds(it * (2 * W) + e * W, W)],
                                                 y[:, bass.ds(it * (2 * W) + e * W, W)], ACT.Square
                                                 ).then_inc(sq_ready, 1)
                else:
                    moved_all(act, "load", 0, 6)
                    for k in range(KD):
                        nc.scalar.activation(h3[:, k, :], y3[:, k, :], ACT.Square).then_inc(sq_ready, 1)
                for n, (c0, c1) in enumerate(HALVES):
                    move(tile("norm", l, n), rstd[:, c0:c1], lambda ps: ps[:, 0:c1 - c0], ACT.Sqrt, bias=eps[:, 0:1])
                act.wait_ge(mod_ready, l + 1)
                for k in range(KD):
                    act.wait_ge(hraw_ready, KD * l + k + 1)
                    ins = nc.scalar.activation(h3[:, k, LAT:W], h3[:, k, LAT:W], ACT.Identity,
                                               scale=mod_col(1, k, 1), bias=mod_col(0, k, 1))
                ins.then_inc(h_lat, 1)

            def qkv(l, h, part):
                tiles = qkv_tiles(l, h)
                if part != 1:
                    for e in range(HT):
                        move(tiles[e], aq3[:, e, :], lambda ps: ps[:, 0:W], scale=ADH ** -0.5)
                if part != 0:
                    for e in range(HT):
                        move(tiles[4 + e], ak3[:, e, :], lambda ps: ps[:, 0:W])
                    for e in range(NT):
                        move(tiles[8 + e], vtok3[:, e, :])
                    move(tiles[11], ktok[:, :])

            def head(l, h):
                ia = A_BEFORE[l]
                H = AH * ia + h
                act.wait_ge(bcast_ready, H + 1)
                for d in range(2):
                    nc.scalar.activation(wi[d][:, :], mix[:, seg((2 + d) * 512 + P, NLAT)], ACT.Exp, scale=-1.0,
                                         bias=m0_all[:, (ia * 2 + d) * AH + h:(ia * 2 + d) * AH + h + 1])
                    nc.scalar.copy(fl[d][:, :], mix[:, seg((4 + d) * 512, TC)]).then_inc(w_ready, 1)
                for d in range(2):
                    act.wait_ge(e_ready, 2 * H + d + 1)
                    nc.scalar.activation(pm[d][:, :], pm[d][:, :], ACT.Exp, scale=-1.0).then_inc(x_ready, 1)
                mod_part(l + 1, 2 * h)
                for q in range(4):
                    if 2 * H + q // 2:
                        act.wait_ge(cst_out[q % 2], 16 * (2 * H + q // 2))
                    for e in range(2):
                        move(headtile(l, h, N_ST + 2 * q + e), cst[q % 2][:, e * ADH:(e + 1) * ADH])
                if h:
                    act.wait_ge(nst_out, 16 * H)
                else:
                    act.wait_ge(m_out, 32 * (ia + 1))
                move(headtile(l, h, N_N), nst[:, :], lambda ps: ps[0:2, :])
                mod_part(l + 1, 2 * h + 1)
                act.wait_ge(num_ready, H + 1)
                if H:
                    act.wait_ge(u_ready, H)
                banks = mix[:, 2 * 512:6 * 512].rearrange("p (e c) -> p e c", e=HT)
                nc.scalar.copy(h3[:, 0:HT, 0:P], banks[:, :, 0:P])
                nc.scalar.copy(h3[:, 0:HT, LAT:W], banks[:, :, LAT:W]).then_inc(hs_moved, 1)

            def head_norm(l, h):
                moved(act, headtile(l, h, N_MEAN))
                nc.scalar.activation(h3[:, HT:2 * HT, :], h3[:, 0:HT, :], ACT.Square).then_inc(lnsq_ready, 1)
                move(sqtile(l, h), rstd[:, :], lambda ps: ps[:, 0:W], ACT.Sqrt, bias=eps[:, 0:1])
                for e in range(HT):
                    v = V_SKIP + A_BEFORE[l] * AT_ + HT * h + e
                    ins = nc.scalar.mul(h3[:, HT + e, :], xc3[:, HT * h + e, :], vec[:, v:v + 1])
                ins.then_inc(sk_ready, 1)

            def mlstm(l):
                ia = A_BEFORE[l]
                pair_loop(tile("xm", l), AT_, lambda it, e, ps: nc.scalar.copy(
                    xm[:, bass.ds(it * (2 * (W + 2)) + (e * (W + 2) + 1), W)], ps[:, 0:W]))
                t0 = tile("z", l)
                with act.Fori(0, AT_ // 2) as it:
                    for e in range(2):
                        act.wait_ge(acc_ready, it * 2 + (t0 + e + 1))
                        nc.scalar.activation(z[:, bass.ds(it * (2 * W) + e * W, W)], acc[(t0 + e) % 2][:, 0:W],
                                             ACT.Silu).then_inc(acc_moved[(t0 + e) % 2], 1)
                        act.wait_ge(conv_step, it * 6 + 3 * (AT_ * ia + e + 1))
                        tmp = xc[:, bass.ds(it * (2 * W) + e * W, W)]
                        nc.scalar.activation(tmp, tmp, ACT.Silu).then_inc(xc_ready, 1)
                ps = ready(tile("gate", l, 0))
                nc.scalar.copy(grow[:, 0:P], ps[0:16, 0:P])
                move(tile("gate", l, 0), grow[:, P:TC], lambda ps: ps[0:16, LAT:W])
                move(tile("gate", l, 1), r_ig, lambda ps: ps[0:64, 0:TC], ACT.Identity, bias=rowp[:, ia:ia + 1])
                move(tile("gate", l, 2), r_x, lambda ps: ps[0:64, 0:TC], ACT.Identity, bias=rowp[:, 2 + ia:3 + ia])
                moved(act, tile("gate", l, 2))
                link(nc.scalar.activation(r_t, r_x, ACT.Abs))
                link(nc.scalar.activation(r_t, r_t, ACT.Exp, scale=-1.0))
                nc.scalar.activation(r_t, r_t, ACT.Ln, bias=1.0).then_inc(lse_ready, 1)
                qkv(l, 0, 2)
                act.wait_ge(rows_ready, ia + 1)
                nc.scalar.activation(r_fl[:, :], r_b[:, :], ACT.Exp, scale=-1.0)
                nc.scalar.activation(r_ws[:, 0:P], r_ws[:, 0:P], ACT.Exp).then_inc(rows_exp, 1)
                move(tile("cols", l), cols[:, :], lambda ps: ps[:, 0:256])
                for h in range(AH):
                    head(l, h)
                    if h < AH - 1:
                        qkv(l, h + 1, 0)
                    head_norm(l, h)
                    if h < AH - 1:
                        qkv(l, h + 1, 1)

            def both_sequences(n, out, **kw_):
                ps = ready(n)
                nc.scalar.activation(out[:, 0:P], ps[:, 0:P], ACT.Identity, **kw_)
                move(n, out[:, P:TC], lambda ps: ps[:, LAT:W], ACT.Identity, **kw_)

            def token_values(l, v3_):
                for n in range(6):
                    move(tile("v", l, n), v3_[:, n % NT, (n // NT) * 512:(n // NT + 1) * 512])

            def gate_path(l, t):
                pair_loop(tile("g", l), KD, lambda it, e, ps: nc.scalar.activation(
                    t[:, bass.ds(it * (2 * W) + e * W, W)], ps[:, 0:W], ACT.Silu))

            def gla(l):
                for h in range(BH):
                    both_sequences(tile("q", l, h), gq3[:, h, :], scale=BDK ** -0.5)
                for h in range(BH):
                    both_sequences(tile("k", l, h), gk3[:, h, :])
                token_values(l, gv3)
                gate_path(l, gr)
                for d in range(2):
                    move(tile("la", l, d), gha[:, d * W:(d + 1) * W], lambda ps: ps[0:RANK, 0:W])
                for n in range(2 * BH):
                    both_sequences(tile("la", l, 2 + n), dx[0][:, n * TC:(n + 1) * TC], bias=vec[:, V_BA + n:V_BA + n + 1])
                for n in range(2):
                    mod_part(l + 1, n)
                moved_all(act, "la", l, 10)
                link(nc.scalar.activation(dx[1][:, :], dx[0][:, :], ACT.Abs))
                link(nc.scalar.activation(dx[1][:, :], dx[1][:, :], ACT.Exp, scale=-1.0))
                nc.scalar.activation(dx[1][:, :], dx[1][:, :], ACT.Ln, bias=1.0).then_inc(xla_ready, 1)
                for n in range(2, MOD_CHUNKS - 2):
                    mod_part(l + 1, n)
                act.wait_ge(kd_ready, 1)
                nc.scalar.activation(kf[:, :], kf[:, :], ACT.Exp, scale=1.0 / B_TAU).then_inc(ke_ready, 1)

                def states():
                    for n in range(2):
                        move(tile("state", l, n), kft[:, n * 512:(n + 1) * 512])
                    for n in range(4):
                        move(tile("state", l, 2 + n), gst[:, n * 512:(n + 1) * 512])

                for n, level in enumerate(range(LEVELS + 1, 0, -1)):
                    tc = BH * (NLAT if level > LEVELS else TC)
                    half = 2 ** (level - 1)
                    fq, fk, df, db = (t[level % 2][:, e * BH * TC:e * BH * TC + tc].rearrange(
                        "p (b s t) -> p b s t", s=2, t=half) for t in (fqk, dx) for e in range(2))
                    act.wait_ge(dist_ready, n + 1)
                    if n >= 2:
                        act.wait_ge(att_ready, n - 1)
                    nc.scalar.activation(fq[:, :, 1], df[:, :, 1], ACT.Exp, scale=1.0 / B_TAU)
                    nc.scalar.activation(fq[:, :, 0], db[:, :, 0], ACT.Exp, scale=1.0 / B_TAU)
                    nc.scalar.activation(fk[:, :, 0], df[:, :, 0], ACT.Exp, scale=-1.0 / B_TAU)
                    nc.scalar.activation(fk[:, :, 1], db[:, :, 1], ACT.Exp, scale=-1.0 / B_TAU).then_inc(fac_ready, 1)
                    if n == 1:
                        states()
                act.wait_ge(att_ready, LEVELS)
                nc.scalar.mul(fqk[0][:, 0:BH * TC], gq[:, :], 2.0).then_inc(q2_ready, 1)
                nc.scalar.activation(gq0, gb4[:, :, :, P:TC], ACT.Exp, scale=1.0 / B_TAU).then_inc(q0e_ready, 1)
                act.wait_ge(gst_out, 16)
                for n in range(2 * BH):
                    act.wait_ge(o_ready, n + 1)
                    nc.scalar.copy(go3[:, n, :], mix[:, seg((3 + n) % 6 * 512, TC)]).then_inc(o_moved, 1)
                    if n % 2:
                        h = n // 2
                        act.wait_ge(o_moved, n + 1)
                        nc.scalar.activation(gsq[:, n - 1:n + 1, :], go3[:, n - 1:n + 1, :], ACT.Square,
                                             scale=BDV ** -0.5).then_inc(osq_ready, 1)
                        if h:
                            rms(l, h - 1)
                for n in range(MOD_CHUNKS - 2, MOD_CHUNKS):
                    mod_part(l + 1, n)
                rms(l, BH - 1)

            def rms(l, h):
                if h:
                    act.wait_ge(ub_ready, h)
                move(rmstile(l, h), rstd[:, 0:TC], lambda ps: ps[:, 0:TC], ACT.Sqrt, bias=eps[:, 0:1])

            def natten(l):
                def query_tile(it, e, ps):
                    nc.scalar.copy(cq[:, bass.ds(it * (2 * W) + e * W, LAT)], ps[:, 0:LAT])
                    return nc.scalar.copy(
                        cq[:, bass.ds(it * (2 * W) + (e * W + LAT), NLAT)].rearrange("p (q t) -> p q t", q=2),
                        ps[:, LAT:W].rearrange("p (q t) -> p q t", q=2)[:, :, ::-1])

                for s, (name, x) in enumerate((("q", cq), ("k", ck))):
                    pair_loop(tile(name, l), KD, query_tile if s == 0 else lambda it, e, ps: nc.scalar.copy(
                        ck[:, bass.ds(it * (2 * W) + e * W, W)], ps[:, 0:W]))
                    if s == 0:
                        moved_all(act, name, l, KD)
                        nc.scalar.activation(csq[:, :], x, ACT.Square).then_inc(csq_ready, 1)
                token_values(l, cv3)
                gate_path(l, cg)
                for n in range(2):
                    move(tile("turn", l, n), ckc[:, n * 512:(n + 1) * 512])
                move(tile("qk", l, 0), crms[0], lambda ps: ps[:, 0:3 * CH], ACT.Sqrt, bias=eps[:, 0:1])
                move(tile("qk", l, 1), crt, lambda ps: ps[0:CH, 0:TC])
                moved_all(act, "k", l, KD)
                nc.scalar.activation(csq[:, :], ck, ACT.Square).then_inc(csq_ready, 1)
                move(tile("qk", l, 10), crms[1], lambda ps: ps[:, 0:3 * CH], ACT.Sqrt, bias=eps[:, 0:1])
                move(tile("qk", l, 11), crt, lambda ps: ps[0:CH, 0:TC])
                for n in range(2):
                    move(tile("knew", l, n), knt[:, n * 512:(n + 1) * 512])

                def exps(h):
                    s = h % 2
                    act.wait_ge(mx_ready, h + 1)
                    if h >= 2:
                        act.wait_ge(ct_ready, h - 1)
                    for q, (c, n) in enumerate(((0, P), (P, TC), (P + TC, TC))):
                        ins = nc.scalar.activation(cp[s][:, seg(c, n)], mix[:, seg(q * 512, n)], ACT.Exp,
                                                   bias=cst_[s][:, q:q + 1], accum_out=cst_[s][:, 3 + q:4 + q])
                    ins.then_inc(cx_ready, 1)

                def turned(h):
                    act.wait_ge(ct_ready, h + 1)
                    nc.scalar.copy(cpt[h % 2], mix[:, seg(3 * 512, 896)]).then_inc(cpt_ready, 1)

                for h in range(CH):
                    exps(h)
                    if h:
                        turned(h - 1)
                    if h >= 3 and h % 2:
                        mod_part(l + 1, h // 2 - 1)
                turned(CH - 1)
                mod_part(l + 1, KD - 1)

            for l, kind in enumerate(KINDS):
                if l == 0:
                    mod_part(0, 0)
                    mod_part(0, 1)
                    fold_start(0)
                    for h in range(AH):
                        fold(0, h)
                        if h < AH - 1:
                            mod_part(0, 2 * h + 2)
                            mod_part(0, 2 * h + 3)
                norm(l)
                if kind == 0 and l:
                    fold_start(l)
                    for h in range(AH):
                        fold(l, h)
                [mlstm, gla, natten][kind](l)
            done_before(act, DEPTH - 1)
            for n in range(2 * NT):
                move(tile("store", 0, n), XIN[n // 2][:, (n % 2) * 512:(n % 2 + 1) * 512])

        @block.vector
        def _(dve):
            steps = [0]

            def link(ins):
                steps[0] += 1
                ins.then_inc(dve_step, 1)
                dve.wait_ge(dve_step, steps[0])

            tt = nc.vector.tensor_tensor
            stt = nc.vector.scalar_tensor_tensor

            for t, x in ((vrow[:, :], 0.0), (rowp[:, :], 0.0), (eps[:, :], EPS), (ones[:, :], 1.0),
                         (ones_d[:, :], 1.0 / D), (ones_h[:, :], 1.0 / ADH),
                         (y3[:, :, NCTX:LAT], 0.0)):
                ins = nc.vector.memset(t, x)
            ins.then_inc(const_dve, 1)

            def mod_vectors(l):
                for n in (MOD_CHUNKS - 2, MOD_CHUNKS - 1):
                    moved(dve, tile(f"modcol{n}", l))
                if l:
                    dve.wait_ge(h_lat, l)
                    moved_all(dve, "out", l - 1, 8)
                link(tt(modv.rearrange("p (c r) -> p c r", r=2), modr.rearrange("p (c r) -> p c r", r=2),
                        vec[:, V_BMOD + 24 * l:V_BMOD + 24 * l + 24].unsqueeze(2).to_broadcast([P, 24, 2]), ALU.add))
                scale = modv[:, 16:32].rearrange("p (k r) -> p k r", r=2)
                stt(scale, scale, 1.0, vec[:, V_NORM + 8 * l:V_NORM + 8 * l + 8].unsqueeze(2).to_broadcast([P, KD, 2]),
                    ALU.add, ALU.mult).then_inc(mod_ready, 1)

            def norm(l):
                for n in range(2):
                    moved(dve, tile("norm", l, n))
                inv = mix[:, 0:W]
                link(nc.vector.reciprocal(inv, rstd[:, :]))
                dve.wait_ge(mod_ready, l + 1)
                for k in range(KD):
                    tt(h3[:, k, :], y3[:, k, :], inv, ALU.mult).then_inc(hraw_ready, 1)
                for k in range(KD):
                    dve.wait_ge(hraw_ready, KD * l + k + 1)
                    ins = nc.vector.tensor_scalar(h3[:, k, 0:P], h3[:, k, 0:P], mod_col(1, k, 0), mod_col(0, k, 0),
                                                  ALU.mult, ALU.add)
                ins.then_inc(h_ctx, 1)

            def residual(l):
                t0 = tile("out", l)
                with dve.Fori(0, KD // 2) as it:
                    for e in range(2):
                        ps = acc[(t0 + e) % 2]
                        dve.wait_ge(acc_ready, it * 2 + (t0 + e + 1))
                        for r, (c, n) in enumerate(((0, NCTX), (LAT, NLAT))):
                            yc = y[:, bass.ds(it * (2 * W) + (e * W + c), n)]
                            ins = stt(yc, ps[:, seg(c, n)], modv[:, bass.ds(it * 4 + (2 * (2 * KD + e) + r), 1)], yc,
                                      ALU.mult, ALU.add)
                        ins.then_inc(acc_moved[(t0 + e) % 2], 1)

            def block_diagonal(l, h):
                w5 = wt4.rearrange("p (m o f) -> p m f o", m=3, o=4)
                for m in range(3):
                    ins = tt(bd4[:, m].rearrange("p e (b o) -> p e b o", o=4),
                             w5[:, m, HT * h:HT * h + HT, :].unsqueeze(2).to_broadcast([P, HT, 32, 4]),
                             mask4.unsqueeze(1).unsqueeze(3).to_broadcast([P, HT, 32, 4]), ALU.mult)
                ins.then_inc(bd_ready, 1)

            def prepare(l):
                done_before(dve, l - 1)
                for t in (xm3[:, :, 0:1], xm3[:, :, W + 1:W + 2], gsel, r_ab[:, :], r_m[:, :]):
                    ins = nc.vector.memset(t, 0.0)
                link(ins)
                dve.wait_ge(const_made, CONSTS)
                nc.vector.tensor_copy(gsel.rearrange("p (n c) -> p n c", c=32)[:, :, 0:AH],
                                      ident[0:16, 0:16].rearrange("p (n c) -> p n c", c=AH)).then_inc(gsel_ready, 1)
                dve.wait_ge(mask_ready, A_BEFORE[l] + 1)
                for t in range(2):
                    moved(dve, tile("fold", l, t))
                for h in range(AH):
                    if h:
                        dve.wait_ge(acc_ready, tile(f"fold{h - 1}", l, 2) + 1)
                    block_diagonal(l, h)

            def conv(l):
                ia = A_BEFORE[l]
                t0 = tile("xm", l)
                with dve.Fori(0, AT_ // 2) as it:
                    for e in range(2):
                        def x(shift):
                            return xm[:, bass.ds(it * (2 * (W + 2)) + (e * (W + 2) + shift), W)]

                        def w(row):
                            return vec[:, bass.ds(it * 2 + (row + e), 1)]

                        out = xc[:, bass.ds(it * (2 * W) + e * W, W)]
                        n = 3 * (AT_ * ia + e)
                        dve.wait_ge(acc_moved[(t0 + e) % 2], it + ((t0 + e) // 2 + 1))
                        nc.vector.tensor_scalar(out, x(1), w(V_CW + (3 * ia + 1) * AT_), w(V_CB + ia * AT_),
                                                ALU.mult, ALU.add).then_inc(conv_step, 1)
                        dve.wait_ge(conv_step, it * 6 + (n + 1))
                        stt(out, x(0), w(V_CW + 3 * ia * AT_), out, ALU.mult, ALU.add).then_inc(conv_step, 1)
                        dve.wait_ge(conv_step, it * 6 + (n + 2))
                        stt(out, x(2), w(V_CW + (3 * ia + 2) * AT_), out, ALU.mult, ALU.add).then_inc(conv_step, 1)

            DIRS = ((0, slice(0, AH)), (1, slice(32, 32 + AH)))

            def gate_rows(l):
                ia = A_BEFORE[l]
                for t_, x in ((r_keep, 1.0), (r_ones, 1.0), (r_ws, 0.0)):
                    ins = nc.vector.memset(t_, x)
                link(ins)
                nc.vector.memset(r_keep[0:AH, P:P + 1], 0.0)
                nc.vector.memset(r_keep[32:32 + AH, P - 1:P], 0.0)
                dve.wait_ge(lse_ready, ia + 1)
                link(stt(r_x, r_x, 0.0, r_t, ALU.min, ALU.subtract))
                for d, r in DIRS:
                    way = slice(None, None, -1) if d else slice(None)
                    ins = nc.vector.tensor_tensor_scan(r_b[r, way], r_keep[r, way], r_x[r, way], 0.0, ALU.mult, ALU.add)
                link(ins)
                for d, r in DIRS:
                    ins = tt(r_a[r, :], r_ig[r, :], r_b[r, :], ALU.subtract)
                link(ins)
                for d, r in DIRS:
                    for first, n, start in ((0, NCTX, 0.0), (NCTX, NLAT, rowp[r, 4 + ia:5 + ia])):
                        way = slice(first + n - 1, first - 1 if first else None, -1) if d else seg(first, n)
                        ins = nc.vector.tensor_tensor_scan(r_m[r, way], r_ones[r, way], r_a[r, way], start,
                                                           ALU.mult, ALU.max)
                link(ins)
                for d, r in DIRS:
                    tt(r_b[r, :], r_b[r, :], r_m[r, :], ALU.add)
                    end = 0 if d else P - 1
                    ins = nc.vector.tensor_scalar(r_ws[r, 0:P], r_a[r, 0:P], r_m[r, end:end + 1], None, ALU.subtract)
                ins.then_inc(rows_ready, 1)

            def head(l, h):
                ia = A_BEFORE[l]
                H = AH * ia + h
                moved(dve, tile("cols", l))
                dve.wait_ge(bcast_ready, H + 1)
                for d, mask in enumerate((mask_f, mask_b)):
                    dve.wait_ge(w_ready, 2 * H + d + 1)
                    m = mix[:, seg((2 + d) * 512, TC)]
                    for t, (c, n, m0) in enumerate(((0, P, P), (P, NLAT, P), (P, NLAT, 0))):
                        a = cols[:, t * 64 + 32 * d + h:t * 64 + 32 * d + h + 1]
                        ins = stt(pm[d][:, seg((0, P, TC)[t], n)], m[:, seg(c, n)], a, mask[:, seg(m0, n)],
                                  ALU.subtract, ALU.max)
                    ins.then_inc(e_ready, 1)
                t = headtile(l, h, N_QN)
                dve.wait_ge(acc_ready, t + 1)
                for d in range(2):
                    ins = tt(rd[d][:, P:TC], wi[d][:, :], acc[t % 2][:, d * NLAT:(d + 1) * NLAT], ALU.mult)
                ins.then_inc(acc_moved[t % 2], 1)
                dve.wait_ge(s_ready, H + 1)
                for d in range(2):
                    dve.wait_ge(x_ready, 2 * H + d + 1)
                    tt(pm[d][:, 0:TC], pm[d][:, 0:TC], mix[:, 0:TC], ALU.mult)
                    tt(pm[d][:, TC:640], pm[d][:, TC:640], mix[:, 512:512 + NLAT], ALU.mult).then_inc(p_ready, 1)
                if h < AH - 1:
                    block_diagonal(l, h + 1)
                for d in range(2):
                    den = mix[:, seg((2 + d) * 512, TC)]
                    dve.wait_ge(den_ready, 2 * H + d + 1)
                    stt(fl[d][:, 0:P], den[:, 0:P], -1.0, fl[d][:, 0:P], ALU.mult, ALU.max)
                    ins = tt(rd[d][:, P:TC], den[:, P:TC], rd[d][:, P:TC], ALU.add)
                link(ins)
                for d in range(2):
                    ins = stt(fl[d][:, P:TC], rd[d][:, P:TC], -1.0, fl[d][:, P:TC], ALU.mult, ALU.max)
                link(ins)
                for d in range(2):
                    tt(rd[d][:, 0:P], mix[:, seg((2 + d) * 512, P)], fl[d][:, 0:P], ALU.max)
                    ins = tt(rd[d][:, P:TC], rd[d][:, P:TC], fl[d][:, P:TC], ALU.max)
                link(ins)
                for d in range(2):
                    ins = nc.vector.reciprocal(rd[d][:, :], rd[d][:, :])
                link(ins)
                dve.wait_ge(p_ready, 2 * H + 2)
                for d in range(2):
                    tt(wi[d][:, :], wi[d][:, :], rd[d][:, P:TC], ALU.mult)
                    tt(pm[d][:, 0:P], pm[d][:, 0:P], rd[d][:, 0:P], ALU.mult)
                    both = pm[d][:, P:640].rearrange("p (s t) -> p s t", s=2)
                    ins = tt(both, both, rd[d][:, P:TC].unsqueeze(1).to_broadcast([P, 2, NLAT]), ALU.mult)
                link(ins)
                tt(pm[0][:, :], pm[0][:, :], pm[1][:, :], ALU.add).then_inc(a_ready, 1)
                for d in range(2):
                    tt(qs3[d], aq3[:, :, LAT:W], wi[d].unsqueeze(1).to_broadcast([P, HT, NLAT]), ALU.mult
                       ).then_inc(qs_ready, 1)
                hs = h3[:, 0:HT, :]
                t = headtile(l, h, N_MEAN)
                dve.wait_ge(acc_ready, t + 1)
                tt(hs, hs, acc[t % 2][:, 0:W].unsqueeze(1).to_broadcast([P, HT, W]), ALU.subtract
                   ).then_inc(acc_moved[t % 2], 1)
                moved(dve, t)
                moved(dve, sqtile(l, h))
                link(nc.vector.reciprocal(rstd[:, :], rstd[:, :]))
                link(tt(hs, hs, rstd.unsqueeze(1).to_broadcast([P, HT, W]), ALU.mult))
                dve.wait_ge(sk_ready, H + 1)
                for e in range(HT):
                    v = V_OG + ia * AT_ + HT * h + e
                    ins = stt(h3[:, e, :], h3[:, e, :], vec[:, v:v + 1], h3[:, HT + e, :], ALU.mult, ALU.add)
                link(ins)
                zh = z3[:, HT * h:HT * h + HT, :]
                tt(zh, zh, hs, ALU.mult).then_inc(u_ready, 1)

            def mlstm(l):
                conv(l)
                block_diagonal(l, 0)
                gate_rows(l)
                for h in range(AH):
                    head(l, h)

            def gla(l):
                copy = nc.vector.tensor_copy
                done_before(dve, l - 1)
                for d in range(2):
                    ins = nc.vector.memset(keep[d], 1.0)
                link(ins)
                nc.vector.memset(keep[0][:, P:P + 1], 0.0)
                nc.vector.memset(keep[1][:, P - 1:P], 0.0)
                dve.wait_ge(gmask_ready, 1)
                link(tt(gxor, gxor, gxs, ALU.bitwise_xor))
                for level in range(LEVELS):
                    ins = nc.vector.tensor_scalar(gmask[:, level * P:(level + 1) * P], gxor, float(2 ** level), None,
                                                  ALU.is_lt)
                link(ins)
                dve.wait_ge(xla_ready, 1)
                link(stt(dx[0], dx[0], 0.0, dx[1], ALU.min, ALU.subtract))
                for n in range(2 * BH):
                    d = n // BH
                    c = n * TC
                    way = slice(c + TC - 1, c - 1 if c else None, -1) if d else seg(c, TC)
                    ins = nc.vector.tensor_tensor_scan(gb[:, way], keep[d][:, ::-1] if d else keep[d],
                                                       dx[0][:, way], 0.0, ALU.mult, ALU.add)
                link(ins)
                for d in range(2):
                    end = 0 if d else P - 1
                    ins = tt(kf[:, d * 512:(d + 1) * 512].rearrange("p (h t) -> p h t", h=BH),
                             gb4[:, d, :, end:end + 1].to_broadcast([P, BH, P]), gb4[:, d, :, 0:P], ALU.subtract)
                ins.then_inc(kd_ready, 1)

                def distance(n, level):
                    if n >= 2:
                        dve.wait_ge(fac_ready, n - 1)
                    size = 2 ** level
                    for d in range(2):
                        if level > LEVELS:
                            src = gb4[:, d, :, P:TC]
                            tc = BH * NLAT
                        else:
                            src = gb[:, d * BH * TC:(d + 1) * BH * TC].rearrange("p (b t) -> p b t", t=size)
                            tc = BH * TC
                        mid = size // 2 - 1 + d
                        ins = tt(dx[level % 2][:, d * BH * TC:d * BH * TC + tc].rearrange("p (b t) -> p b t", t=size),
                                 src, src[:, :, mid:mid + 1].to_broadcast([P, tc // size, size]), ALU.subtract)
                    ins.then_inc(dist_ready, 1)

                def attention(n, level):
                    dve.wait_ge(att_ready, n + 1)
                    if n:
                        dve.wait_ge(att_moved, n)
                    half = (level % 2) * 3 * 512
                    if level > LEVELS:
                        ins = copy(gax, mix[:, seg(half, 2 * BH * P)])
                    elif level == LEVELS:
                        ins = copy(gat, mix[:, seg(half, BH * TC)])
                    else:
                        ins = nc.vector.copy_predicated(
                            gat.rearrange("p (n t) -> p n t", t=P),
                            gmask[:, level * P:(level + 1) * P].unsqueeze(1).to_broadcast([P, BH * NT, P]),
                            mix[:, seg(half, BH * TC)].rearrange("p (n t) -> p n t", t=P))
                    ins.then_inc(att_moved, 1)

                distance(0, LEVELS + 1)
                dve.wait_ge(ke_ready, 1)
                for d in range(2):
                    kd = kf[:, d * 512:(d + 1) * 512].rearrange("p (h t) -> p h t", h=BH)
                    ins = tt(kd, kd, gk3[:, :, 0:P], ALU.mult)
                ins.then_inc(kf_ready, 1)
                for n, level in enumerate(range(LEVELS + 1, 0, -1)):
                    if level > 1:
                        distance(n + 1, level - 1)
                    dve.wait_ge(fac_ready, n + 1)
                    if level > LEVELS:
                        f = fqk[level % 2][:, 0:BH * NLAT].rearrange("p (h t) -> p h t", h=BH)
                        tt(f, f, gq3[:, :, P:TC], ALU.mult).then_inc(lq_ready, 1)
                    else:
                        f = fqk[level % 2][:, 0:BH * TC]
                        tt(f, f, gq, ALU.mult).then_inc(lq_ready, 1)
                    if n:
                        attention(n - 1, level + 1)
                attention(LEVELS, 1)
                attention(LEVELS + 1, 0)
                dve.wait_ge(q0e_ready, 1)
                for d in range(2):
                    ins = tt(gq0[:, d], gq0[:, d], gq3[:, :, P:TC], ALU.mult)
                ins.then_inc(q0_ready, 1)
                for h in range(BH):
                    moved(dve, rmstile(l, h))
                    link(nc.vector.reciprocal(rstd[:, 0:TC], rstd[:, 0:TC]))
                    for e in range(2):
                        n = 2 * h + e
                        ins = stt(go3[:, n, :], go3[:, n, :], vec[:, V_BOG + n:V_BOG + n + 1], rstd[:, 0:TC],
                                  ALU.mult, ALU.mult)
                    link(ins)
                    for c, w, g in ((0, P, 0), (P, NLAT, LAT)):
                        r_ = gr3[:, 2 * h:2 * h + 2, seg(g, w)]
                        ins = tt(r_, r_, go3[:, 2 * h:2 * h + 2, seg(c, w)], ALU.mult)
                    ins.then_inc(ub_ready, 1)

            def natten(l):
                done_before(dve, l - 1)
                dve.wait_ge(chead_ready, 1)
                for t, x in ((csel, 0.0), (csel[0:CDH, 0:1], 1.0 / CDH), (csel[CDH:P, 1:2], 1.0 / CDH)):
                    ins = nc.vector.memset(t, x)
                    if x == 0.0:
                        link(ins)
                ins.then_inc(csel_ready, 1)
                link(nc.vector.tensor_scalar(cqg, vec[:, V_QG:V_QG + 1], CDH ** -0.5, None, ALU.mult))
                for s, (x3, gain) in enumerate(((cq3, cqg), (ck3, vec[:, V_KG:V_KG + 1]))):
                    moved(dve, tile("qk", l, 10 * s))
                    nc.vector.reciprocal(crms[s], crms[s]).then_inc(rms_ready, 1)
                    for k in range(KD):
                        t = tile("qk", l, 10 * s + 2 + k)
                        dve.wait_ge(acc_ready, t + 1)
                        for c, w, g in ((0, P, 0), (P, NLAT, LAT)):
                            ins = stt(x3[:, k, seg(g, w)], x3[:, k, seg(g, w)], gain, acc[t % 2][:, seg(c, w)],
                                      ALU.mult, ALU.mult)
                        ins.then_inc(acc_moved[t % 2], 1)

                def maxima(h):
                    st_ = cst_[h % 2]
                    dve.wait_ge(cs_ready, h + 1)
                    for q, n in enumerate((P, TC, TC)):
                        ins = nc.vector.tensor_reduce(st_[:, q:q + 1], mix[:, seg(q * 512, n)], AX, ALU.max)
                    link(ins)
                    nc.vector.tensor_scalar(st_[:, 0:3], st_[:, 0:3], -1.0, None, ALU.mult).then_inc(mx_ready, 1)

                def normalise(h):
                    st_ = cst_[h % 2]
                    dve.wait_ge(cx_ready, h + 1)
                    link(nc.vector.reciprocal(st_[:, 3:6], st_[:, 3:6]))
                    for q, (c, n) in enumerate(((0, P), (P, TC), (P + TC, TC))):
                        ins = nc.vector.tensor_scalar(cp[h % 2][:, seg(c, n)], cp[h % 2][:, seg(c, n)],
                                                      st_[:, 3 + q:4 + q], None, ALU.mult)
                    ins.then_inc(cpn_ready, 1)

                def gated(k):
                    t = tile(f"attn{k}", l)
                    dve.wait_ge(acc_ready, t + 1)
                    g_ = cg3[:, k, 0:P]
                    tt(g_, g_, acc[t % 2][:, 0:P], ALU.mult)
                    g_ = cg3[:, k, LAT:W].rearrange("p (q t) -> p q t", q=2)
                    ins = tt(g_, g_, acc[t % 2][:, P:TC].rearrange("p (q t) -> p q t", q=2)[:, :, ::-1], ALU.mult)
                    ins.then_inc(acc_moved[t % 2], 1)

                maxima(0)
                for h in range(CH):
                    normalise(h)
                    if h + 1 < CH:
                        maxima(h + 1)
                    if h and h % 2 == 0:
                        gated(h // 2 - 1)
                gated(KD - 1)

            for l, kind in enumerate(KINDS):
                if l == 0:
                    prepare(0)
                mod_vectors(l)
                norm(l)
                if kind == 0 and l:
                    prepare(l)
                [mlstm, gla, natten][kind](l)
                residual(l)

        @block.gpsimd
        def _(pool):
            steps = [0]

            def link(ins):
                steps[0] += 1
                ins.then_inc(pool_step, 1)
                pool.wait_ge(pool_step, steps[0])

            def select(t, pattern, base, mult, fill, op=ALU.is_ge):
                return nc.gpsimd.affine_select(out=t, in_=t, pattern=pattern, compare_op=op, fill=fill,
                                               base=base, channel_multiplier=mult)

            link(nc.gpsimd.memset(ident[:, :], 0.0))
            select(ident[:, :], [[-1, P]], 0, 1, 1.0, ALU.not_equal).then_inc(const_made, 1)

            def mlstm(l):
                ia = A_BEFORE[l]
                j = ia
                done_before(pool, l - 1)
                for n, w in enumerate((i["a_w_ig"], i["a_w_fg"])):
                    for d in range(2):
                        pool.dma_start(wg_rows[:, seg((2 * n + d) * 512, 512)],
                                       w[j, d].rearrange("(f q) h -> f (q h)", q=P)).then_inc(fold_in, 16)
                for n, w in enumerate((i["a_wq"], i["a_wk"], i["a_wv"])):
                    pool.dma_start(wt_rows[:, seg(n * 512, 512)],
                                   w[j].rearrange("(f b) x o -> f (b x o)", b=32)).then_inc(fold_in, 16)
                for t, x in ((mask_f[:, 0:P], BIG), (mask_f[:, P:TC], 0.0), (mask_b[:, 0:2 * P], 0.0),
                             (mask_b[:, 2 * P:TC], BIG), (mask4[:, :], 1.0)):
                    ins = nc.gpsimd.memset(t, x)
                link(ins)
                select(mask_f[:, P:2 * P], [[1, P]], 0, -1, BIG)
                select(mask_b[:, P:2 * P], [[-1, P]], 0, 1, BIG)
                link(select(mask4[:, :], [[-4, 32]], 0, 1, 0.0))
                select(mask4[:, :], [[4, 32]], 3, -1, 0.0).then_inc(mask_ready, 1)
                pool.wait_ge(rows_ready, ia + 1)
                for d in range(2):
                    col = 0 if d else P - 1
                    pool.dma_start(o["new_m"][0, j, d].rearrange("(h x) -> h x", x=1),
                                   r_b[32 * d:32 * d + AH, col:col + 1]).then_inc(m_out, 16)
                moved(pool, tile("cols", l))
                for h in range(AH):
                    moved(pool, qkv_tiles(l, h)[11])
                    for d in range(2):
                        nc.gpsimd.tensor_scalar(kw[d][:, :], ktok[:, :], cols[:, seg(192 + 32 * d + h, 1)], None,
                                                ALU.mult).then_inc(kw_ready, 1)
                    for q in range(4):
                        for e in range(2):
                            moved(pool, headtile(l, h, N_ST + 2 * q + e))
                        dst = o["new_C"][0, j, q // 2, h].rearrange("(k p) n -> p k n", p=P)
                        pool.dma_start(dst[:, 2 * (q % 2):2 * (q % 2) + 2, :],
                                       cst[q % 2].rearrange("p (k n) -> p k n", k=2)).then_inc(cst_out[q % 2], 16)
                    moved(pool, headtile(l, h, N_N))
                    pool.dma_start(o["new_n"][0, j, :, h], nst[:, :]).then_inc(nst_out, 16)

            def gla(l):
                done_before(pool, l - 1)
                for d in range(2):
                    pool.dma_start(ga14[:, :, d, :], i["b_w_a1"][0, d].rearrange("(k p) n -> p k n", p=P)).then_inc(b_in, 16)
                    pool.dma_start(ga2[:, seg(d * BH * BDK, BH * BDK)], i["b_w_a2"][0, d]).then_inc(b_in, 16)
                pool.dma_start(gs03, i["state_gla_S"][0, 0].rearrange("d h k v -> k (d h) v")).then_inc(b_in, 16)
                nc.gpsimd.iota(gxor, [[1, P]], base=0, channel_multiplier=0)
                nc.gpsimd.iota(gxs, [[0, P]], base=0, channel_multiplier=1).then_inc(gmask_ready, 1)
                for n, level in enumerate(range(LEVELS + 1, 0, -1)):
                    pool.wait_ge(fac_ready, n + 1)
                    f = fqk[level % 2][:, BH * TC:2 * BH * TC]
                    if level > LEVELS:
                        f = f[:, 0:BH * NLAT].rearrange("p (h t) -> p h t", h=BH)
                        nc.gpsimd.tensor_tensor(f, f, gk3[:, :, P:TC], ALU.mult).then_inc(lk_ready, 1)
                    else:
                        nc.gpsimd.tensor_tensor(f, f, gk, ALU.mult).then_inc(lk_ready, 1)
                    if n == 2:
                        for m in range(2, 6):
                            moved(pool, tile("state", l, m))
                        pool.dma_start(o["new_S"][0, 0].rearrange("d h k v -> k (d h) v"),
                                       gst.rearrange("p (n v) -> p n v", v=BDV)).then_inc(gst_out, 16)

            def natten(l):
                done_before(pool, l - 1)
                for t, name in ((ckr, "cache_na_k"), (cvc, "cache_na_v")):
                    pool.dma_start(t.rearrange("p (h c) -> p h c", h=CH), i[name][0, 0].rearrange("h t c -> t h c")
                                   ).then_inc(c_in, 16)
                link(nc.gpsimd.memset(chead, 1.0))
                link(select(chead, [[1, D]], 0, -CDH, 0.0))
                select(chead, [[-1, D]], CDH - 1, CDH, 0.0).then_inc(chead_ready, 1)
                link(nc.gpsimd.memset(zrow, 0.0))
                for h in range(CH):
                    pool.dma_start(zrow[7 * h:7 * h + 7, GW - WINW:GW - WINW + 31], i["c_rpb"][0, h, 4:11, :]
                                   ).then_inc(rpb_in, 16)
                pool.wait_ge(rpb_in, 16 * CH)
                pool.dma_start(rpb_rows, zrow).then_inc(rpb_out, 16)
                pool.wait_ge(rpb_out, 16)
                for r in range(ROWS):
                    for kr in range(ROWS):
                        src = bass.AP(tensor=rpb_rows.tensor, offset=(kr - r + 3) * P,
                                      ap=[[1, GW], [7 * P, CH], [1, GW]])
                        pool.dma_start(cb4[seg(GW * (1 - r % 2), GW), r // 2, :, kr * GW:(kr + 1) * GW], src
                                       ).then_inc(bias_in, 16)
                link(nc.gpsimd.memset(cwin, 0.0))
                for half in range(2):
                    p = seg(GW * half, GW)
                    link(select(cwin[p, 0:GW - WINW], [[1, GW - WINW]], WINW // 2 - (GW - 1), 1, -BIG))
                    ins = select(cwin[p, WINW:GW], [[-1, GW - WINW]], GW - 1 + WINW // 2 - 1 - WINW, -1, -BIG)
                link(ins)
                pool.wait_ge(bias_in, 16 * ROWS * ROWS)
                both = cb.rearrange("p (n c) -> p n c", c=GW)
                nc.gpsimd.tensor_tensor(both, both, cwin.unsqueeze(1).to_broadcast([P, 2 * CH * ROWS, GW]), ALU.add
                                        ).then_inc(bias_ready, 1)
                moved_all(pool, "v", l, 6)
                pool.dma_start(o["new_v"][0, 0].rearrange("h t c -> t h c"),
                               cv3[:, 0, :].rearrange("p (h c) -> p h c", h=CH)).then_inc(kv_out, 16)
                moved_all(pool, "knew", l, 2)
                pool.dma_start(o["new_k"][0, 0].rearrange("h t c -> t h c"),
                               knt.rearrange("p (h c) -> p h c", h=CH)).then_inc(kv_out, 16)

            for l, kind in enumerate(KINDS):
                [mlstm, gla, natten][kind](l)
            done_before(pool, DEPTH - 1)


_INS = ["x_prompt", "x_sample", "state_mlstm_C", "state_mlstm_n", "state_mlstm_m", "state_gla_S", "cache_na_k",
        "cache_na_v", "c", "c_ctx", "norm_g", "w_mod", "b_mod", "a_w_in", "a_conv_w", "a_conv_b", "a_wq", "a_wk",
        "a_wv", "a_w_ig", "a_b_ig", "a_w_fg", "a_b_fg", "a_out_g", "a_skip", "a_w_out", "b_w_in", "b_w_a1",
        "b_w_a2", "b_b_a", "b_out_g", "b_w_out", "c_w_in", "c_q_g", "c_k_g", "c_rpb", "c_w_out"]
_OUTS = {"y_prompt": (1, 128, 1024), "y_sample": (1, 256, 1024), "new_C": (1, 2, 2, 4, 512, 512),
         "new_n": (1, 2, 2, 4, 512), "new_m": (1, 2, 2, 4), "new_S": (1, 1, 2, 4, 128, 256),
         "new_k": (1, 1, 16, 128, 64), "new_v": (1, 1, 16, 128, 64)}


def kernel(**inputs):
    import numpy as _np
    import concourse.bacc as _bacc
    from concourse import mybir as _mybir
    from concourse.bass_utils import run_bass_kernel_spmd as _run

    nc = _bacc.Bacc("TRN2", target_bir_lowering=False, num_devices=1)
    arrays, ins, outs = {}, {}, {}
    for name in _INS:
        a = _np.ascontiguousarray(inputs[name])
        arrays[f"in_{name}"] = a
        ins[name] = nc.dram_tensor(f"in_{name}", a.shape, _mybir.dt.from_np(a.dtype), kind="ExternalInput").ap()
    for name, shape in _OUTS.items():
        outs[name] = nc.dram_tensor(f"out_{name}", shape, _mybir.dt.float32, kind="ExternalOutput").ap()
    trunk(nc, ins, outs)
    r = _run(nc, [arrays], core_ids=[0])
    return tuple(r.results[0][f"out_{name}"] for name in _OUTS)
```

```python
from contextlib import ExitStack

import concourse.bass as bass
from concourse import mybir
from concourse.alu_op_type import AluOpType as ALU

ACT = mybir.ActivationFunctionType
F32 = mybir.dt.float32
I32 = mybir.dt.int32
AX = mybir.AxisListType.X

P = 128
D = 1024
CONSTS = 1
VECTORS = 15
LATE = 7
FOLD_IN = 7
KD = D // P
NCTX, NLAT = 128, 256
W = NCTX + 1 + NLAT
LAT = NCTX + 1
TOK = (0, LAT, LAT + P)
NT = len(TOK)
TC = NT * P
HALVES = ((0, 256), (256, W))
EPS = 1e-6
KINDS = (0, 1, 2, 0)
DEPTH = len(KINDS)
AH, ADH, AI = 4, 512, 2048
AT_ = AI // P
HT = ADH // P
BH, BDK, BDV, RANK = 4, 128, 256, 16
CH, CDH = 16, 64
GW, ROWS, WINW = 64, 4, 16
B_TAU = 16.0
BIG = 1.0e30
LEVELS = 7
MOD_CHUNKS = 8
MC = 3 * D // MOD_CHUNKS
SLOTS = 2
CHUNK = 4096

def plan():
    chunk0, tile0, last_use, c, t = {}, {}, [], 0, 0
    phases = [("vec", 0, 0, 2), ("load", 0, 0, 6)]

    def mod(l, *parts):
        out = []
        for n in parts if l < DEPTH else ():
            out += [(f"modrow{n}", l, 1, 1)] + ([(f"modcol{n - 1}", l, 0, 1)] if n else [])
            out += [(f"modcol{n}", l, 0, 1)] if n == MOD_CHUNKS - 1 else []
        return out

    fold = [[("fold", 0, 2)]] + [[(f"fold{x}", 0, 3)] for x in range(4)]
    for l, kind in enumerate(KINDS):
        folds = [[(name, l, *counts) for name, *counts in part] for part in fold]
        if l == 0:
            phases += mod(0, 0, 1) + folds[0] + folds[1] + mod(0, 2, 3) + folds[2] + mod(0, 4, 5) + folds[3]
            phases += mod(0, 6, 7) + folds[4]
        phases += [("norm", l, 0, 2)]
        if kind == 0:
            if l:
                phases += sum(folds, [])
            phases += [("xm", l, 4, 16), ("z", l, 4, 16), ("gate", l, 0, 3), ("pre", l, 0, 12), ("cols", l, 0, 1)]
            for h in range(AH):
                first, second = mod(l + 1, 2 * h), mod(l + 1, 2 * h + 1)
                phases += [(f"first{h}", l, 0, 1)] + first + [(f"c0_{h}", l, 1, 0), (f"state{h}", l, 0, 9)] + second
                phases += [(f"rest{h}", l, 0, 14 if h < AH - 1 else 2)]
            phases += [("out", l, 4, 8)]
        elif kind == 1:
            phases += [("q", l, 1, 4), ("k", l, 1, 4), ("la", l, 0, 10), ("v", l, 2, 6), ("g", l, 2, 8)]
            phases += [("state", l, 0, 6)] + mod(l + 1, 0, 1, 2, 3, 4, 5) + [("rms", l, 0, 3)] + mod(l + 1, 6, 7)
            phases += [("rms3", l, 0, 1), ("out", l, 2, 8)]
        else:
            phases += [("q", l, 2, 8), ("k", l, 2, 8), ("rmsq", l, 0, 8), ("v", l, 2, 6), ("rmsk", l, 0, 8),
                       ("g", l, 2, 8), ("turn", l, 0, 2), ("knew", l, 0, 2)]
            for k in range(KD):
                phases += [(f"attn{k}", l, 0, 1)] + mod(l + 1, k)
            phases += [("out", l, 2, 8)]
    phases += [("store", 0, 0, 6)]
    for name, l, chunks, tiles in phases:
        if name in ("xm", "z", "v", "g", "out") or name in ("q", "k") and KINDS[l] == 2:
            assert c % 2 == 0 and t % 2 == 0
        chunk0[name, l], tile0[name, l] = c, t
        for n in range(chunks):
            last_use.append(t + tiles // chunks * (n + 1) - 1)
        if name[:4] == "rest":
            last_use[chunk0[f"c0_{name[4]}", l]] = t
        c, t = c + chunks, t + tiles
    return chunk0, tile0, last_use


CHUNK0, TILE0, LAST_USE = plan()


def trunk(nc, i, o):
    with ExitStack() as ctx:
        def sb(name, cols, dt=F32, rows=P, stack=ctx):
            return stack.enter_context(nc.sbuf_tensor(name, [rows, cols], dt))[:, :]

        def sem(name):
            return ctx.enter_context(nc.semaphore(name))

        acc = [ctx.enter_context(nc.psum_tensor(f"acc{b}", [P, 512], F32))[:, :] for b in range(2)]
        mix = ctx.enter_context(nc.psum_tensor("mix", [P, 6 * 512], F32))[:, :]

        y = sb("y", KD * W)
        hT = sb("hT", KD * W)
        ring = [sb(f"ring{s}", CHUNK) for s in range(SLOTS)]
        ident = sb("ident", P)
        ones = sb("ones", P)
        ones_d = sb("ones_d", P)
        ones_h = sb("ones_h", P)
        vec = sb("vec", 4 * P)
        sc = sb("sc", 2 * KD)
        modv = sb("modv", 3 * KD * 2)
        modr = sb("modr", 3 * KD * 2)
        mst = sb("mst", 2 * MC, rows=2)
        rstd = sb("rstd", W)
        eps = sb("eps", 1)
        m0_all = sb("m0_all", 16)
        rowp = sb("rowp", 6, rows=64)

        V_NORM, V_BMOD = 0, 32
        V_CW, V_CB = P, P + 96
        V_OG, V_SKIP, V_BOG, V_CTX, V_C, V_BA, V_QG, V_KG = (2 * P + x for x in (0, 32, 64, 72, 80, 88, 96, 97))
        V_N0 = 3 * P

        def v3(t, n, w=W):
            return t[:, 0:n * w].rearrange("p (n w) -> p n w", w=w)

        y3, h3 = v3(y, KD), v3(hT, KD)

        def mod_col(part, k, r):
            n = (part * KD + k) * 2 + r
            return modv[:, n:n + 1]

        with ExitStack() as st:
            xm = sb("xm", AT_ * (W + 2), stack=st)
            xc = sb("xc", AT_ * W, stack=st)
            z = sb("z", AT_ * W, stack=st)
            aq = sb("aq", HT * W, stack=st)
            ak = sb("ak", HT * W, stack=st)
            vtok = sb("vtok", NT * ADH, stack=st)
            ktok = sb("ktok", ADH, stack=st)
            kw = [sb(f"kw{d}", ADH, stack=st) for d in range(2)]
            bd = sb("bd", 3 * HT * P, stack=st)
            qs = [sb(f"qs{d}", HT * NLAT, stack=st) for d in range(2)]
            cst = [sb(f"cst{s}", 2 * ADH, stack=st) for s in range(2)]
            pm = [sb(f"pm{d}", 640, stack=st) for d in range(2)]
            fl = [sb(f"fl{d}", TC, stack=st) for d in range(2)]
            rd = [sb(f"rd{d}", TC, stack=st) for d in range(2)]
            wi = [sb(f"wi{d}", NLAT, stack=st) for d in range(2)]
            mask_f = sb("mask_f", TC, stack=st)
            mask_b = sb("mask_b", TC, stack=st)
            mask4 = sb("mask4", 32, stack=st)
            wt4 = sb("wt4", 3 * 4 * AT_, stack=st)
            cols = sb("cols", 4 * 64, stack=st)
            r_ab = sb("r_ab", 2 * TC, rows=64, stack=st)
            r_m = sb("r_m", TC, rows=64, stack=st)
            r_fl = sb("r_fl", TC, rows=64, stack=st)
        r_a, r_b = r_ab[:, 0:TC], r_ab[:, TC:2 * TC]
        nst = r_ab[0:2, 0:ADH]
        gfold = kw[0]
        grow = kw[1][0:16, 0:TC]
        gsel = kw[1][0:16, TC:TC + P]
        vrow = cst[0][:, 0:4 * P]
        r_ig, r_x, r_t = (t[0:64, 0:TC] for t in (pm[0], pm[1], fl[0]))
        r_keep, r_ones, r_ws = (t[0:64, 0:TC] for t in (fl[1], rd[0], rd[1]))
        wg_rows = z[0:48, 0:2048]
        wt_rows = z[0:16, 2048:3584]
        gspread = z[:, 3584:3584 + 4 * P]
        wg_cols = z[:, 5120:5120 + 768]
        wg3 = wg_cols.rearrange("p (f n) -> p f n", n=16)
        bd4 = bd.rearrange("p (m e c) -> p m e c", m=3, e=HT)
        g4 = gfold.rearrange("p (f s n) -> p f s n", s=2, n=16)
        qs3 = [v3(t, HT, NLAT) for t in qs]
        vtok3 = v3(vtok, NT, ADH)
        XIN = [xc[:, n * D:(n + 1) * D] for n in range(NT)]
        xm3, xc3, z3 = v3(xm, AT_, W + 2), v3(xc, AT_), v3(z, AT_)
        aq3, ak3 = v3(aq, HT), v3(ak, HT)

        with ExitStack() as st:
            gq = sb("gq", BH * TC, stack=st)
            gk = sb("gk", BH * TC, stack=st)
            gv = sb("gv", NT * D, stack=st)
            gr = sb("gr", KD * W, stack=st)
            dx = [sb(f"dx{s}", 2 * BH * TC, stack=st) for s in range(2)]
            gb = sb("gb", 2 * BH * TC, stack=st)
            fqk = [sb(f"fqk{s}", 2 * BH * TC, stack=st) for s in range(2)]
            gat = sb("gat", BH * TC, stack=st)
            gax = sb("gax", 2 * BH * P, stack=st)
            gs0 = sb("gs0", 2 * BH * BDV, stack=st)
            kf = sb("kf", 2 * BH * P, stack=st)
            kft = sb("kft", 2 * BH * P, stack=st)
            keep = [sb(f"keep{d}", TC, stack=st) for d in range(2)]
            gxor = sb("gxor", P, I32, stack=st)
            gxs = sb("gxs", P, I32, stack=st)
            gmask = sb("gmask", LEVELS * P, I32, stack=st)
            ga1 = sb("ga1", KD * 2 * RANK, stack=st)
            ga2 = sb("ga2", 2 * BH * BDK, rows=RANK, stack=st)
            gha = sb("gha", 2 * W, rows=RANK, stack=st)
        gq3, gk3, gv3, gr3 = v3(gq, BH, TC), v3(gk, BH, TC), v3(gv, NT, D), v3(gr, KD)
        gb4 = gb.rearrange("p (d h t) -> p d h t", d=2, h=BH)
        ga14 = ga1.rearrange("p (k d n) -> p k d n", k=KD, d=2)
        gs03, kft3 = v3(gs0, 2 * BH, BDV), v3(kft, 2 * BH, P)
        gq0 = dx[0][:, 0:2 * BH * NLAT].rearrange("p (d h t) -> p d h t", d=2, h=BH)
        gst = hT[:, 0:2 * BH * BDV]
        go3 = fqk[1][:, 0:KD * TC].rearrange("p (n t) -> p n t", n=KD)
        gsq = hT[:, 0:KD * TC].rearrange("p (n t) -> p n t", n=KD)

        with ExitStack() as st:
            cq = sb("cq", KD * W, stack=st)
            ck = sb("ck", KD * W, stack=st)
            cv = sb("cv", NT * D, stack=st)
            cg = sb("cg", KD * W, stack=st)
            cqr = sb("cqr", KD * W, stack=st)
            ckrt = sb("ckrt", KD * W, stack=st)
            cb = sb("cb", 2 * CH * NLAT, stack=st)
            cwin = sb("cwin", GW, stack=st)
            ckr = sb("ckr", D, stack=st)
            ckc = sb("ckc", D, stack=st)
            cvc = sb("cvc", D, stack=st)
            knt = sb("knt", D, stack=st)
            cp = [sb(f"cp{s}", 896, stack=st) for s in range(2)]
            cpt = [sb(f"cpt{s}", 896, stack=st) for s in range(2)]
            cst_ = [sb(f"cstat{s}", 6, stack=st) for s in range(2)]
            cqg = sb("cqg", 1, stack=st)
            hones = sb("hones", P, stack=st)
            zrow = sb("zrow", P, rows=112, stack=st)
        cq3, ck3, cv3, cg3 = v3(cq, KD), v3(ck, KD), v3(cv, NT, D), v3(cg, KD)
        cqr3, ckr3 = v3(cqr, KD), v3(ckrt, KD)
        cb4 = cb.rearrange("p (q h k) -> p q h k", q=2, h=CH)
        rpb_rows = nc.dram_tensor("rpb_rows", (112, P), F32, kind="Internal").ap()

        vec_in, x_in = sem("vec_in"), sem("x_in")
        late_in = sem("late_in")
        const_made = sem("const_made")
        const_dve = sem("const_dve")
        ring_full = [sem(f"ring_full{s}") for s in range(SLOTS)]
        acc_ready = sem("acc_ready")
        acc_moved = [sem(f"acc_moved{b}") for b in range(2)]
        mod_ready = sem("mod_ready")
        gsel_ready = sem("gsel_ready")
        sq_ready = sem("sq_ready")
        hraw_ready = sem("hraw_ready")
        h_ctx, h_lat = sem("h_ctx"), sem("h_lat")
        act_step, dve_step, pool_step = sem("act_step"), sem("dve_step"), sem("pool_step")
        fold_in = sem("fold_in")
        mask_ready = sem("mask_ready")
        bd_ready = sem("bd_ready")
        spread_made, gfold_ready = sem("spread_made"), sem("gfold_ready")
        conv_step = sem("conv_step")
        xc_ready = sem("xc_ready")
        lse_ready = sem("lse_ready")
        rows_ready = sem("rows_ready")
        rows_exp = sem("rows_exp")
        m_out = sem("m_out")
        bcast_ready = sem("bcast_ready")
        s_ready = sem("s_ready")
        e_ready = sem("e_ready")
        x_ready = sem("x_ready")
        w_ready = sem("w_ready")
        p_ready = sem("p_ready")
        den_ready = sem("den_ready")
        a_ready = sem("a_ready")
        qs_ready = sem("qs_ready")
        kw_ready = sem("kw_ready")
        cst_out = [sem(f"cst_out{s}") for s in range(2)]
        nst_out = sem("nst_out")
        num_ready = sem("num_ready")
        hs_moved = sem("hs_moved")
        cen_ready = sem("cen_ready")
        lnsq_ready = sem("lnsq_ready")
        sk_ready = sem("sk_ready")
        u_ready = sem("u_ready")
        y_out = sem("y_out")
        b_in, gmask_ready = sem("b_in"), sem("gmask_ready")
        xla_ready = sem("xla_ready")
        dist_ready = sem("dist_ready")
        fac_ready = sem("fac_ready")
        lq_ready, lk_ready = sem("lq_ready"), sem("lk_ready")
        q2_ready = sem("q2_ready")
        att_ready = sem("att_ready")
        att_moved = sem("att_moved")
        kd_ready, ke_ready, kf_ready = sem("kd_ready"), sem("ke_ready"), sem("kf_ready")
        q0e_ready, q0_ready = sem("q0e_ready"), sem("q0_ready")
        gst_out = sem("gst_out")
        o_ready, o_moved, osq_ready, ub_ready = sem("o_ready"), sem("o_moved"), sem("osq_ready"), sem("ub_ready")
        c_in, rpb_in, rpb_out, bias_in, bias_ready = (sem("c_in"), sem("rpb_in"), sem("rpb_out"), sem("bias_in"),
                                                      sem("bias_ready"))
        hones_ready = sem("hones_ready")
        csq_ready = sem("csq_ready")
        qkn_ready = sem("qkn_ready")
        kv_out = sem("kv_out")
        cs_ready = sem("cs_ready")
        mx_ready, cx_ready, cpn_ready = sem("mx_ready"), sem("cx_ready"), sem("cpn_ready")
        ct_ready, cpt_ready = sem("ct_ready"), sem("cpt_ready")

        def tile(name, l, k=0):
            return TILE0[name, l] + k

        def moved(eng, n):
            eng.wait_ge(acc_moved[n % 2], n // 2 + 1)

        def moved_all(eng, name, l, count):
            for n in (tile(name, l, count - 1), tile(name, l, count - 2)):
                moved(eng, n)

        def done_before(eng, l):
            if l < 0:
                return
            moved_all(eng, "out", l, 8)
            if KINDS[l] == 0:
                n = AH * (A_BEFORE[l] + 1)
                eng.wait_ge(cst_out[0], 32 * n)
                eng.wait_ge(cst_out[1], 32 * n)
                eng.wait_ge(nst_out, 16 * n)
                eng.wait_ge(m_out, 32 * (A_BEFORE[l] + 1))
            elif KINDS[l] == 1:
                eng.wait_ge(gst_out, 16)
            else:
                eng.wait_ge(kv_out, 32)

        A_BEFORE = [sum(k == 0 for k in KINDS[:l]) for l in range(DEPTH)]
        N_QN, N_ST, N_N, N_MEAN, N_Q, N_SQ, N_K = 0, 1, 9, 10, 11, 15, 16

        def headtile(l, h, k):
            if k < N_ST:
                return tile(f"first{h}", l)
            return tile(f"state{h}", l, k - N_ST) if k < N_MEAN else tile(f"rest{h}", l, k - N_MEAN)

        def qkv_tiles(l, h):
            if h == 0:
                return [tile("pre", l, n) for n in range(12)]
            return [headtile(l, h - 1, n) for n in (*range(N_Q, N_Q + 4), *range(N_K, N_K + 8))]

        def sqtile(l, h):
            return headtile(l, h, N_SQ if h < AH - 1 else N_MEAN + 1)

        def rmstile(l, h):
            return tile("rms", l, h) if h < BH - 1 else tile("rms3", l)

        def seg(col0, n=None):
            return slice(col0, col0 + n)

        block = ctx.enter_context(nc.Block())

        def rows(eng, r0, w):
            n = 1
            for x in w.shape:
                n *= x
            b, r = divmod(r0, P)
            flat = w.rearrange(" ".join("abcde"[:len(w.shape)]) + " -> (" + " ".join("abcde"[:len(w.shape)]) + ")")
            eng.dma_start(vrow[r:r + n // P, b * P:(b + 1) * P], flat.rearrange("(r c) -> r c", c=P)
                          ).then_inc(vec_in, 16)

        @block.sync
        def _(sp):
            def halves(slot, dst, src):
                n = len(dst) if isinstance(dst, list) else None
                for e in range(2):
                    if n:
                        sp.dma_start(dst[e], src[e]).then_inc(ring_full[slot], 16)
                    else:
                        k = slice(e * dst.shape[1] // 2, (e + 1) * dst.shape[1] // 2)
                        sp.dma_start(dst[:, k], src[:, k]).then_inc(ring_full[slot], 16)

            def chunk(g, dst, src):
                if g >= 2:
                    sp.wait_ge(acc_ready, LAST_USE[g - 2] + 1)
                halves(g % 2, dst, src)

            def stream(name, l, n, w, cols_, k):
                g0 = CHUNK0[name, l]
                src = w.rearrange("(k p) n -> p k n", p=P)
                dst = [ring[s][:, 0:k * cols_].rearrange("p (k n) -> p k n", k=k) for s in range(2)]
                for s in range(min(n, 2)):
                    chunk(g0 + s, dst[(g0 + s) % 2], src[:, :, s * cols_:(s + 1) * cols_])
                if n > 2:
                    per = LAST_USE[g0 + 1] - LAST_USE[g0]
                    with sp.Fori(0, n // 2 - 1) as it:
                        for s in range(2):
                            sp.wait_ge(acc_ready, it * (2 * per) + (LAST_USE[g0 + s] + 1))
                            halves(s, dst[s], src[:, :, bass.ds(it * (2 * cols_) + (2 + s) * cols_, cols_)])

            def mod_chunk(l, n):
                if l < DEPTH:
                    g = CHUNK0[f"modrow{n}", l]
                    chunk(g, ring[g % 2][:, 0:KD * MC].rearrange("p (k n) -> p k n", k=KD),
                          i["w_mod"][l].rearrange("(k p) n -> p k n", p=P)[:, :, n * MC:(n + 1) * MC])

            for n in range(NT):
                src = i["x_prompt"][0] if n == 0 else i["x_sample"][0, (n - 1) * P:n * P]
                sp.dma_start(XIN[n], src).then_inc(x_in, 16)
            sp.wait_ge(const_dve, 1)
            rows(sp, V_SKIP, i["a_skip"])
            rows(sp, V_BOG, i["b_out_g"])
            rows(sp, V_BA, i["b_b_a"])
            rows(sp, V_N0, i["state_mlstm_n"])
            for r0, g in ((V_QG, i["c_q_g"]), (V_KG, i["c_k_g"])):
                for half in range(2):
                    sp.dma_start(vrow[r0 - 2 * P:r0 - 2 * P + 1, seg(2 * P + half * CDH, CDH)], g).then_inc(vec_in, 16)
            for l, kind in enumerate(KINDS):
                if l == 0:
                    for n in range(MOD_CHUNKS):
                        mod_chunk(0, n)
                if kind == 0:
                    j = A_BEFORE[l]
                    stream("xm", l, 4, i["a_w_in"][j, :, 0:AI], 512, KD)
                    stream("z", l, 4, i["a_w_in"][j, :, AI:2 * AI], 512, KD)
                    for h in range(AH):
                        mod_chunk(l + 1, 2 * h)
                        g = CHUNK0[f"c0_{h}", l]
                        chunk(g, [ring[g % 2][:, seg(d * 2048, 2048)].rearrange("p (k n) -> p k n", k=HT)
                                  for d in range(2)],
                              [i["state_mlstm_C"][0, j, d, h].rearrange("(k p) n -> p k n", p=P) for d in range(2)])
                        mod_chunk(l + 1, 2 * h + 1)
                    stream("out", l, 4, i["a_w_out"][j], 256, AT_)
                elif kind == 1:
                    w = i["b_w_in"][0]
                    stream("q", l, 1, w[:, 0:512], 512, KD)
                    stream("k", l, 1, w[:, 512:1024], 512, KD)
                    stream("v", l, 2, w[:, 1024:2048], 512, KD)
                    stream("g", l, 2, w[:, 2048:3072], 512, KD)
                    for n in range(MOD_CHUNKS):
                        mod_chunk(l + 1, n)
                    stream("out", l, 2, i["b_w_out"][0], 512, KD)
                else:
                    w = i["c_w_in"][0]
                    for n, name in enumerate("qkvg"):
                        stream(name, l, 2, w[:, n * D:(n + 1) * D], 512, KD)
                    for n in range(MOD_CHUNKS):
                        mod_chunk(l + 1, n)
                    stream("out", l, 2, i["c_w_out"][0], 512, KD)
            for n in range(NT):
                for half in range(2):
                    moved(sp, tile("store", 0, 2 * n + half))
                dst = o["y_prompt"][0] if n == 0 else o["y_sample"][0, (n - 1) * P:n * P]
                sp.dma_start(dst, XIN[n]).then_inc(y_out, 16)
            sp.wait_ge(y_out, 16 * NT)

        @block.tensor
        def _(pe):
            def bank(n):
                if n >= 2:
                    pe.wait_ge(acc_moved[n % 2], n // 2)
                return acc[n % 2]

            def mm(out, lhsT, rhs, start, stop):
                return nc.tensor.matmul(out, lhsT=lhsT, rhs=rhs, start=start, stop=stop)

            def group(out, pairs):
                for n, (a, b) in enumerate(pairs):
                    ins = mm(out, a, b, n == 0, n == len(pairs) - 1)
                return ins

            def linear(name, l, n, k, m, rhs, width, tokens=False, ready=None):
                g0, t0 = CHUNK0[name, l], TILE0[name, l]
                per = NT if tokens else m
                cols_ = m * P

                first = 1 if ready else 0

                def body(turn, slots, before=0):
                    for s, slot in enumerate(slots):
                        w3 = ring[slot][:, 0:k * cols_].rearrange("p (k n) -> p k n", k=k)
                        pe.wait_ge(ring_full[slot], turn * 32 + 32 * ((g0 + s) // 2 + 1 + before))
                        together = 2 if ready and not before and s == 0 else 0
                        if together:
                            ps = [bank(t0), bank(t0 + 1)]
                            for kk in range(k):
                                ready(kk)
                                for e in range(2):
                                    ins = mm(ps[e][:, 0:width], w3[:, kk, e * P:(e + 1) * P], rhs[:, kk, :],
                                             kk == 0, kk == k - 1)
                                    if kk == k - 1:
                                        ins.then_inc(acc_ready, 1)
                        for e in range(together, per):
                            t = s * per + e
                            if t0 + t >= 2:
                                pe.wait_ge(acc_moved[(t0 + t) % 2], turn * per + (before * per + (t0 + t) // 2))
                            ps = acc[(t0 + t) % 2]
                            for kk in range(k):
                                if tokens:
                                    ins = mm(ps[:, 0:cols_], rhs[:, kk, seg(TOK[e], P)], w3[:, kk, :], kk == 0, kk == k - 1)
                                else:
                                    ins = mm(ps[:, 0:width], w3[:, kk, e * P:(e + 1) * P], rhs[:, kk, :], kk == 0, kk == k - 1)
                            ins.then_inc(acc_ready, 1)

                if n == 1:
                    body(0, [g0 % 2])
                else:
                    if ready:
                        body(0, [0, 1])
                    if n > 2 * first:
                        with pe.Fori(0, n // 2 - first) as it:
                            body(it, [0, 1], before=first)

            def h_ready(l):
                def wait(kk):
                    pe.wait_ge(h_ctx, KD * l + kk + 1)
                    pe.wait_ge(h_lat, KD * l + kk + 1)
                return wait

            def transposes(n, parts):
                ps = bank(n)
                for out, src in parts:
                    ins = nc.tensor.transpose(out(ps), src, ident[0:src.shape[0], 0:src.shape[0]])
                ins.then_inc(acc_ready, 1)

            pe.wait_ge(const_made, CONSTS)
            pe.wait_ge(const_dve, 1)
            pe.wait_ge(vec_in, 16 * VECTORS)
            transposes(tile("vec", 0, 0), [(lambda ps, n=n: ps[:, n * P:(n + 1) * P], vrow[:, n * P:(n + 1) * P])
                                           for n in range(4)])
            transposes(tile("vec", 0, 1), [(lambda ps: ps[:, 0:P], vrow[:, 2 * P:3 * P])])
            pe.wait_ge(x_in, 16 * NT)
            for n in range(2 * NT):
                transposes(tile("load", 0, n), [
                    (lambda ps, e=e: ps[:, e * P:(e + 1) * P],
                     XIN[n // 2][:, (4 * (n % 2) + e) * P:(4 * (n % 2) + e + 1) * P]) for e in range(4)])

            def mod_columns(l, n):
                t = tile(f"modrow{n}", l)
                moved(pe, t)
                transposes(tile(f"modcol{n}", l), [
                    (lambda ps, e=e: ps[:, 2 * e:2 * e + 2], mst[:, seg(n % 2 * MC + e * P, P)])
                    for e in range(MC // P)])

            def mod_part(l, n):
                if l == DEPTH:
                    return
                g = CHUNK0[f"modrow{n}", l]
                ps = bank(tile(f"modrow{n}", l))
                pe.wait_ge(ring_full[g % 2], 32 * (g // 2 + 1))
                w3 = ring[g % 2][:, 0:KD * MC].rearrange("p (k n) -> p k n", k=KD)
                group(ps[0:2, 0:MC], [(sc[:, 2 * k:2 * k + 2], w3[:, k, :]) for k in range(KD)]
                      ).then_inc(acc_ready, 1)
                if n:
                    mod_columns(l, n - 1)
                if n == MOD_CHUNKS - 1:
                    mod_columns(l, n)

            def norm(l):
                ps = [bank(tile("norm", l, n)) for n in range(2)]
                for k in range(KD):
                    pe.wait_ge(sq_ready, KD * l + k + 1)
                    for n, (c0, c1) in enumerate(HALVES):
                        ins = mm(ps[n][:, 0:c1 - c0], ones_d[:, :], h3[:, k, c0:c1], k == 0, k == KD - 1)
                        if k == KD - 1:
                            ins.then_inc(acc_ready, 1)

            def fold_start(l):
                ia = A_BEFORE[l]
                pe.wait_ge(fold_in, 16 * FOLD_IN * (ia + 1))
                for t in range(2):
                    parts = [(lambda ps, n=n: ps[:, n * 48:(n + 1) * 48],
                              wg_rows[:, (2 * t + n // 4) * 512 + n % 4:(2 * t + n // 4 + 1) * 512:4])
                             for n in range(8)]
                    parts += [(lambda ps, n=n: ps[:, 384 + n * 16:384 + (n + 1) * 16], wt_rows[:, (6 * t + n) // 4 * 512 + (6 * t + n) % 4:((6 * t + n) // 4 + 1) * 512:4])
                              for n in range(6)]
                    transposes(tile("fold", l, t), parts)

            def fold(l, x):
                if x == 0:
                    pe.wait_ge(spread_made, A_BEFORE[l] + 1)
                    for t in range(2):
                        moved(pe, tile("fold", l, t))
                for m in range(3):
                    mm(bank(tile(f"fold{x}", l, m))[:, 0:256], gspread[:, x * P:(x + 1) * P],
                       wg_cols[:, m * 256:(m + 1) * 256], True, True).then_inc(acc_ready, 1)

            def qkv(l, h, part):
                ia = A_BEFORE[l]
                tiles = qkv_tiles(l, h)
                if part != 1:
                    pe.wait_ge(bd_ready, AH * ia + h + 1)
                    for e in range(HT):
                        mm(bank(tiles[e])[:, 0:W], bd4[:, 0, e, :], xc3[:, HT * h + e, :], True, True
                           ).then_inc(acc_ready, 1)
                if part != 0:
                    for e in range(HT):
                        mm(bank(tiles[4 + e])[:, 0:W], bd4[:, 1, e, :], xc3[:, HT * h + e, :], True, True
                           ).then_inc(acc_ready, 1)
                    for t in range(NT):
                        ps = bank(tiles[8 + t])
                        for e in range(HT):
                            ins = mm(ps[:, e * P:(e + 1) * P], xm3[:, HT * h + e, seg(1 + TOK[t], P)],
                                     bd4[:, 2, e, :], e == 0, e == HT - 1)
                        ins.then_inc(acc_ready, 1)
                    ps = bank(tiles[11])
                    for e in range(HT):
                        ins = mm(ps[:, e * P:(e + 1) * P], xc3[:, HT * h + e, 0:P], bd4[:, 1, e, :],
                                 e == 0, e == HT - 1)
                    ins.then_inc(acc_ready, 1)

            def head(l, h):
                ia = A_BEFORE[l]
                H = AH * ia + h
                if H >= 1:
                    pe.wait_ge(hs_moved, HT * H)
                for n in range(4):
                    d = n % 2
                    src = r_m if n < 2 else r_fl
                    ins = mm(mix[:, seg((2 + n) * 512, TC)],
                             ident[0:64, 32 * d + h:32 * d + h + 1].to_broadcast([64, P]), src[:, :], True, True)
                ins.then_inc(bcast_ready, 1)
                for n in qkv_tiles(l, h):
                    moved(pe, n)
                if H >= 1:
                    pe.wait_ge(p_ready, 2 * H)
                group(mix[:, 0:P], [(ak3[:, k, 0:P], aq3[:, k, 0:P]) for k in range(HT)])
                for k in range(HT):
                    mm(mix[:, P:P + NLAT], ak3[:, k, seg(TOK[1], P)], aq3[:, k, LAT:W], k == 0, k == HT - 1)
                group(mix[:, 512:512 + NLAT], [(ak3[:, k, seg(TOK[2], P)], aq3[:, k, LAT:W]) for k in range(HT)]
                      ).then_inc(s_ready, 1)
                ps = bank(headtile(l, h, N_QN))
                for d in range(2):
                    ins = group(ps[:, d * NLAT:(d + 1) * NLAT],
                                [(vec[:, seg(V_N0 + ((ia * 2 + d) * AH + h) * HT + k, 1)].to_broadcast([P, P]),
                                  aq3[:, k, LAT:W]) for k in range(HT)])
                ins.then_inc(acc_ready, 1)

                def state(d):
                    pe.wait_ge(kw_ready, 2 * H + d + 1)
                    for k in range(HT):
                        mm(bank(headtile(l, h, N_ST + 4 * d + k))[:, :], kw[d][:, k * P:(k + 1) * P],
                           vtok[:, 0:ADH], True, True).then_inc(acc_ready, 1)

                if l + 1 < DEPTH:
                    mod_part(l + 1, 2 * h)
                else:
                    state(0)
                for d in range(2):
                    pe.wait_ge(p_ready, 2 * H + d + 1)
                    pe.wait_ge(w_ready, 2 * H + d + 1)
                    ps = mix[:, seg((2 + d) * 512, TC)]
                    mm(ps[:, 0:P], ones[:, :], pm[d][:, 0:P], True, True)
                    mm(ps[:, P:TC], ones[:, :], pm[d][:, P:TC], True, False)
                    mm(ps[:, P:TC], ones[:, :], pm[d][:, TC:640], False, True).then_inc(den_ready, 1)
                if l + 1 < DEPTH:
                    state(0)
                state(1)
                mm(bank(headtile(l, h, N_N))[0:2, :], cols[:, 3 * 64 + h:4 * 64:32], ktok[:, :], True, True
                   ).then_inc(acc_ready, 1)
                mod_part(l + 1, 2 * h + 1)
                g = CHUNK0[f"c0_{h}", l]
                pe.wait_ge(ring_full[g % 2], 32 * (g // 2 + 1))
                c04 = ring[g % 2].rearrange("p (d k n) -> p d k n", d=2, k=HT)
                out = [mix[:, seg((2 + e) * 512, W)] for e in range(HT)]
                v = [slice(e * P, (e + 1) * P) for e in range(HT)]
                for d in range(2):
                    pe.wait_ge(qs_ready, 2 * H + d + 1)
                    for e in range(HT):
                        for k in range(HT):
                            mm(out[e][:, LAT:W], c04[:, d, k, v[e]], qs3[d][:, k, :], d == 0 and k == 0, False)
                pe.wait_ge(a_ready, H + 1)
                for e in range(HT):
                    for t in (1, 2):
                        mm(out[e][:, LAT:W], vtok3[:, t, v[e]], pm[0][:, t * 256 - P:t * 256 + P], False, t == 2)
                    mm(out[e][:, 0:P], vtok3[:, 0, v[e]], pm[0][:, 0:P], True, True).then_inc(num_ready, 1)

            def head_mean(l, h):
                H = AH * A_BEFORE[l] + h
                ps = bank(headtile(l, h, N_MEAN))
                for k in range(HT):
                    pe.wait_ge(hs_moved, HT * H + k + 1)
                    ins = mm(ps[:, 0:W], ones_h[:, :], h3[:, k, :], k == 0, k == HT - 1)
                ins.then_inc(acc_ready, 1)

            def head_square(l, h):
                H = AH * A_BEFORE[l] + h
                ps = bank(sqtile(l, h))
                for k in range(HT):
                    pe.wait_ge(lnsq_ready, HT * H + k + 1)
                    ins = mm(ps[:, 0:W], ones_h[:, :], h3[:, HT + k, :], k == 0, k == HT - 1)
                ins.then_inc(acc_ready, 1)

            def mlstm(l):
                ia = A_BEFORE[l]
                linear("xm", l, 4, KD, 4, h3, W, ready=h_ready(l))
                linear("z", l, 4, KD, 4, h3, W)
                t = tile("gate", l, 0)
                pe.wait_ge(gfold_ready, ia + 1)
                pairs = [(g4[:, f, 1, :], xm3[:, f, 1:1 + W]) for f in range(AT_)]
                pairs += [(g4[:, f, 0, :], xc3[:, f, :]) for f in range(AT_)]
                ps = bank(t)
                for n, (a, b) in enumerate(pairs):
                    if n == AT_:
                        pe.wait_ge(xc_ready, AT_ * (ia + 1))
                    ins = mm(ps[0:16, 0:W], a, b, n == 0, n == len(pairs) - 1)
                ins.then_inc(acc_ready, 1)
                moved(pe, t)
                pe.wait_ge(gsel_ready, ia + 1)
                for kind in range(2):
                    mm(bank(tile("gate", l, 1 + kind))[0:64, 0:TC], gsel[:, seg(64 * kind, 64)], grow, True, True
                       ).then_inc(acc_ready, 1)
                qkv(l, 0, 2)
                pe.wait_ge(rows_ready, ia + 1)
                pe.wait_ge(rows_exp, ia + 1)
                transposes(tile("cols", l, 0),
                           [(lambda ps, e=e: ps[:, e * 64:(e + 1) * 64],
                             (r_a[:, e * P:(e + 1) * P] if e < 3 else r_ws[:, 0:P])) for e in range(4)])
                for h in range(AH):
                    head(l, h)
                    head_mean(l, h)
                    if h < AH - 1:
                        qkv(l, h + 1, 0)
                    head_square(l, h)
                    if h < AH - 1:
                        qkv(l, h + 1, 1)
                linear("out", l, 4, AT_, 2, z3, W,
                       ready=lambda kk: pe.wait_ge(u_ready, AH * ia + kk // HT + 1))

            def gla(l):
                linear("q", l, 1, KD, 4, h3, W, ready=h_ready(l))
                linear("k", l, 1, KD, 4, h3, W)
                pe.wait_ge(b_in, 16 * 5)
                for d in range(2):
                    group(bank(tile("la", l, d))[0:RANK, 0:W], [(ga14[:, k, d, :], h3[:, k, :]) for k in range(KD)]
                          ).then_inc(acc_ready, 1)
                for d in range(2):
                    moved(pe, tile("la", l, d))
                    for h in range(BH):
                        n = d * BH + h
                        mm(bank(tile("la", l, 2 + n))[:, 0:W], ga2[:, n * BDK:(n + 1) * BDK],
                           gha[:, d * W:(d + 1) * W], True, True).then_inc(acc_ready, 1)
                linear("v", l, 2, KD, 4, h3, W, tokens=True)
                linear("g", l, 2, KD, 4, h3, W)
                pe.wait_ge(kf_ready, 1)
                for n in range(2):
                    transposes(tile("state", l, n), [
                        (lambda ps, e=e: ps[:, e * P:(e + 1) * P], kf[:, (4 * n + e) * P:(4 * n + e + 1) * P])
                        for e in range(4)])
                moved_all(pe, "state", l, 2)
                for n in range(4):
                    ps = bank(tile("state", l, 2 + n))
                    for e in range(2):
                        m = 2 * n + e
                        ins = mm(ps[:, e * BDV:(e + 1) * BDV], kft3[:, m, :],
                                 gv3[:, 0, seg((m % BH) * BDV, BDV)], True, True)
                    ins.then_inc(acc_ready, 1)
                for n, level in enumerate(range(LEVELS + 1, -1, -1)):
                    fq, fk = (fqk[level % 2][:, e * BH * TC:(e + 1) * BH * TC] for e in range(2))
                    half = (level % 2) * 3 * 512
                    if level:
                        pe.wait_ge(lq_ready, n + 1)
                        pe.wait_ge(lk_ready, n + 1)
                    else:
                        pe.wait_ge(q2_ready, 1)
                    if n >= 2:
                        pe.wait_ge(att_moved, n - 1)
                    if level > LEVELS:
                        for m in range(2 * BH):
                            h, back = divmod(m, 2)
                            ins = mm(mix[:, seg(half + m * P, P)], fk[:, seg(h * NLAT + back * P, P)],
                                     fq[:, seg(h * NLAT + (1 - back) * P, P)], True, True)
                    else:
                        for m in range(BH * NT):
                            ins = mm(mix[:, seg(half + m * P, P)], (fk if level else gk)[:, seg(m * P, P)],
                                     fq[:, seg(m * P, P)], True, True)
                    ins.then_inc(att_ready, 1)
                    if 1 <= n < MOD_CHUNKS - 1:
                        mod_part(l + 1, n - 1)
                pe.wait_ge(att_moved, LEVELS + 2)
                pe.wait_ge(q0_ready, 1)
                for n in range(2 * BH):
                    h = n // 2
                    if n >= 6:
                        pe.wait_ge(o_moved, n - 5)
                    ps = mix[:, seg((3 + n) % 6 * 512, TC)]
                    v = slice(n * P, (n + 1) * P)
                    for d in range(2):
                        mm(ps[:, P:TC], gs03[:, d * BH + h, (n % 2) * P:(n % 2 + 1) * P], gq0[:, d, h, :], d == 0, False)
                    for t in (1, 2):
                        mm(ps[:, t * P:(t + 1) * P], gv3[:, t, v], gat[:, seg((h * NT + t) * P, P)], False, False)
                        mm(ps[:, t * P:(t + 1) * P], gv3[:, 3 - t, v], gax[:, seg((2 * h + 2 - t) * P, P)],
                           False, t == 2)
                    mm(ps[:, 0:P], gv3[:, 0, v], gat[:, seg(h * NT * P, P)], True, True).then_inc(o_ready, 1)
                    if n % 2 and h:
                        gla_rms(l, h - 1)
                for n in range(MOD_CHUNKS - 2, MOD_CHUNKS):
                    mod_part(l + 1, n)
                gla_rms(l, BH - 1)
                linear("out", l, 2, KD, 4, gr3, W, ready=lambda kk: pe.wait_ge(ub_ready, kk // 2 + 1))

            def gla_rms(l, h):
                pe.wait_ge(osq_ready, h + 1)
                group(bank(rmstile(l, h))[:, 0:TC], [(ones[:, :], gsq[:, 2 * h + e, :]) for e in range(2)]
                      ).then_inc(acc_ready, 1)

            def head_squares(name, l, count, sq3):
                pe.wait_ge(hones_ready, 1)
                pe.wait_ge(csq_ready, count)
                for k in range(KD):
                    mm(bank(tile(name, l, k))[:, 0:W], hones[:, :], sq3[:, k, :], True, True).then_inc(acc_ready, 1)

            def natten(l):
                linear("q", l, 2, KD, 4, h3, W, ready=h_ready(l))
                linear("k", l, 2, KD, 4, h3, W)
                head_squares("rmsq", l, 1, cqr3)
                linear("v", l, 2, KD, 4, h3, W, tokens=True)
                head_squares("rmsk", l, 2, ckr3)
                linear("g", l, 2, KD, 4, h3, W)
                pe.wait_ge(c_in, 32)
                for n in range(2):
                    transposes(tile("turn", l, n), [
                        (lambda ps, e=e: ps[:, e * P:(e + 1) * P], ckr[:, (4 * n + e) * P:(4 * n + e + 1) * P])
                        for e in range(4)])
                pe.wait_ge(qkn_ready, 2 * KD)
                for n in range(2):
                    transposes(tile("knew", l, n), [
                        (lambda ps, e=e: ps[:, e * P:(e + 1) * P], ck3[:, 4 * n + e, 0:P]) for e in range(4)])

                def scores(h):
                    k, r = h // 2, slice(64 * (h % 2), 64 * (h % 2) + 64)
                    if h:
                        pe.wait_ge(cx_ready, h)
                    mm(mix[:, 0:P], cq3[r, k, 0:P], ck3[r, k, 0:P], True, True)
                    for q in (1, 2):
                        ps = mix[:, seg(q * 512, TC)]
                        qt = cq3[r, k, seg(TOK[q], P)]
                        mm(ps[:, 0:NLAT], qt, ck3[r, k, LAT:W], True, False)
                        mm(ps[:, 0:NLAT], ident[:, :], cb4[:, q - 1, h, :], False, True)
                        ins = mm(ps[:, NLAT:TC], qt, ckc[r, k * P:(k + 1) * P], True, True)
                    ins.then_inc(cs_ready, 1)

                def turn(h):
                    pe.wait_ge(cpn_ready, h + 1)
                    if h:
                        pe.wait_ge(cpt_ready, h)
                    for b in range(7):
                        ins = nc.tensor.transpose(mix[:, seg(3 * 512 + b * P, P)], cp[h % 2][:, b * P:(b + 1) * P],
                                                  ident[:, :])
                    ins.then_inc(ct_ready, 1)

                def values(h):
                    pe.wait_ge(cpt_ready, h + 1)
                    k, r = h // 2, slice(64 * (h % 2), 64 * (h % 2) + 64)
                    t = tile(f"attn{k}", l)
                    ps = acc[t % 2]
                    if h % 2 == 0:
                        bank(t)
                    hv = slice(h * CDH, (h + 1) * CDH)
                    pt = cpt[h % 2]
                    mm(ps[r, 0:P], cv3[:, 0, hv], pt[:, 0:P], True, True)
                    for b, v in enumerate((cv3[:, 1, hv], cv3[:, 2, hv], cvc[:, hv])):
                        both = pt[:, P:896].rearrange("p (q b t) -> p q b t", q=2, b=3)[:, :, b, :]
                        ins = mm(ps[r, P:TC].rearrange("p (q t) -> p q t", q=2), v, both, b == 0, b == 2)
                    if h % 2:
                        ins.then_inc(acc_ready, 1)

                moved_all(pe, "turn", l, 2)
                pe.wait_ge(bias_ready, 1)
                scores(0)
                for h in range(CH):
                    if h + 1 < CH:
                        scores(h + 1)
                    turn(h)
                    if h:
                        values(h - 1)
                    if h and h % 2 == 0:
                        mod_part(l + 1, h // 2 - 1)
                values(CH - 1)
                mod_part(l + 1, KD - 1)
                linear("out", l, 2, KD, 4, cg3, W, ready=lambda kk: moved(pe, tile(f"attn{kk}", l)))

            moved(pe, tile("vec", 0, 1))
            for l, kind in enumerate(KINDS):
                if l == 0:
                    mod_part(0, 0)
                    mod_part(0, 1)
                    fold_start(0)
                    for h in range(AH):
                        fold(0, h)
                        if h < AH - 1:
                            mod_part(0, 2 * h + 2)
                            mod_part(0, 2 * h + 3)
                norm(l)
                if kind == 0 and l:
                    fold_start(l)
                    for h in range(AH):
                        fold(l, h)
                [mlstm, gla, natten][kind](l)
            moved_all(pe, "out", DEPTH - 1, 8)
            for n in range(2 * NT):
                transposes(tile("store", 0, n), [
                    (lambda ps, e=e: ps[:, e * P:(e + 1) * P],
                     y3[:, 4 * (n % 2) + e, seg(TOK[n // 2], P)]) for e in range(4)])

        @block.scalar
        def _(act):
            steps = [0]

            def link(ins):
                steps[0] += 1
                ins.then_inc(act_step, 1)
                act.wait_ge(act_step, steps[0])

            def ready(n):
                act.wait_ge(acc_ready, n + 1)
                return acc[n % 2]

            def move(n, out, src=lambda ps: ps, func=ACT.Copy, **kw_):
                nc.scalar.activation(out, src(ready(n)), func, **kw_).then_inc(acc_moved[n % 2], 1)

            def pair_loop(t0, count, step):
                with act.Fori(0, count // 2) as it:
                    for e in range(2):
                        act.wait_ge(acc_ready, it * 2 + (t0 + e + 1))
                        step(it, e, acc[(t0 + e) % 2]).then_inc(acc_moved[(t0 + e) % 2], 1)

            act.wait_ge(const_dve, 1)

            rows(act, V_NORM, i["norm_g"])
            rows(act, V_BMOD, i["b_mod"])
            rows(act, V_CW, i["a_conv_w"])
            rows(act, V_CB, i["a_conv_b"])
            rows(act, V_OG, i["a_out_g"])
            rows(act, V_CTX, i["c_ctx"])
            rows(act, V_C, i["c"])
            act.dma_start(m0_all[:, :], i["state_mlstm_m"].rearrange("a j d h -> a (j d h)").to_broadcast([P, 16])
                          ).then_inc(late_in, 16)
            for n, w in enumerate((i["a_b_ig"], i["a_b_fg"], i["state_mlstm_m"][0])):
                for d in range(2):
                    act.dma_start(rowp[32 * d:32 * d + AH, 2 * n:2 * n + 2], w[:, d].rearrange("j h -> h j"),
                                  allow_slow_non_contiguous=True).then_inc(late_in, 16)

            move(tile("vec", 0, 0), vec[:, :])
            move(tile("vec", 0, 1), sc.rearrange("p (k r) -> p r k", r=2),
                 lambda ps: ps[:, V_CTX - 2 * P:V_CTX - 2 * P + 16].rearrange("p (r k) -> p r k", r=2), ACT.Silu)
            for n in range(2 * NT):
                k0 = 4 * (n % 2)
                move(tile("load", 0, n), y3[:, k0:k0 + 4, seg(TOK[n // 2], P)],
                     lambda ps: ps[:, :].rearrange("p (e t) -> p e t", e=4))

            def fold_start(l):
                for t in range(2):
                    ps = ready(tile("fold", l, t))
                    nc.scalar.copy(wg3[:, :, 8 * t:8 * t + 8].rearrange("p f n -> p n f"),
                                   ps[:, 0:384].rearrange("p (n f) -> p n f", n=8))
                    move(tile("fold", l, t), wt4[:, 96 * t:96 * t + 96], lambda ps: ps[:, 384:480])

            def mod_part(l, n):
                if l == DEPTH:
                    return
                move(tile(f"modrow{n}", l), mst[:, seg(n % 2 * MC, MC)], lambda ps: ps[0:2, 0:MC])
                for m in range(max(n - 1, 0), n + (n == MOD_CHUNKS - 1)):
                    move(tile(f"modcol{m}", l), modr[:, seg(6 * m, 6)], lambda ps: ps[:, 0:6])

            def norm(l):
                if l:
                    t0 = tile("out", l - 1)
                    with act.Fori(0, KD // 2) as it:
                        for e in range(2):
                            act.wait_ge(acc_moved[(t0 + e) % 2], it + ((t0 + e) // 2 + 1))
                            nc.scalar.activation(hT[:, bass.ds(it * (2 * W) + e * W, W)],
                                                 y[:, bass.ds(it * (2 * W) + e * W, W)], ACT.Square
                                                 ).then_inc(sq_ready, 1)
                else:
                    moved_all(act, "load", 0, 6)
                    for k in range(KD):
                        nc.scalar.activation(h3[:, k, :], y3[:, k, :], ACT.Square).then_inc(sq_ready, 1)
                for n, (c0, c1) in enumerate(HALVES):
                    move(tile("norm", l, n), rstd[:, c0:c1], lambda ps: ps[:, 0:c1 - c0], ACT.Sqrt, bias=eps[:, 0:1])
                act.wait_ge(mod_ready, l + 1)
                for k in range(KD):
                    act.wait_ge(hraw_ready, KD * l + k + 1)
                    nc.scalar.activation(h3[:, k, LAT:W], h3[:, k, LAT:W], ACT.Identity,
                                         scale=mod_col(1, k, 1), bias=mod_col(0, k, 1)).then_inc(h_lat, 1)

            def qkv(l, h, part):
                tiles = qkv_tiles(l, h)
                if part != 1:
                    for e in range(HT):
                        move(tiles[e], aq3[:, e, :], lambda ps: ps[:, 0:W], scale=ADH ** -0.5)
                if part != 0:
                    for e in range(HT):
                        move(tiles[4 + e], ak3[:, e, :], lambda ps: ps[:, 0:W])
                    for e in range(NT):
                        move(tiles[8 + e], vtok3[:, e, :])
                    move(tiles[11], ktok[:, :])

            def head(l, h):
                ia = A_BEFORE[l]
                H = AH * ia + h
                act.wait_ge(bcast_ready, H + 1)
                for d in range(2):
                    nc.scalar.activation(wi[d][:, :], mix[:, seg((2 + d) * 512 + P, NLAT)], ACT.Exp, scale=-1.0,
                                         bias=m0_all[:, (ia * 2 + d) * AH + h:(ia * 2 + d) * AH + h + 1])
                    nc.scalar.copy(fl[d][:, :], mix[:, seg((4 + d) * 512, TC)]).then_inc(w_ready, 1)
                for d in range(2):
                    act.wait_ge(e_ready, 2 * H + d + 1)
                    nc.scalar.activation(pm[d][:, :], pm[d][:, :], ACT.Exp, scale=-1.0).then_inc(x_ready, 1)
                mod_part(l + 1, 2 * h)
                for q in range(4):
                    if 2 * H + q // 2:
                        act.wait_ge(cst_out[q % 2], 16 * (2 * H + q // 2))
                    for e in range(2):
                        move(headtile(l, h, N_ST + 2 * q + e), cst[q % 2][:, e * ADH:(e + 1) * ADH])
                if h:
                    act.wait_ge(nst_out, 16 * H)
                else:
                    act.wait_ge(m_out, 32 * (ia + 1))
                move(headtile(l, h, N_N), nst[:, :], lambda ps: ps[0:2, :])
                for e in range(HT):
                    v = V_SKIP + ia * AT_ + HT * h + e
                    ins = nc.scalar.mul(xc3[:, HT * h + e, :], xc3[:, HT * h + e, :], vec[:, v:v + 1])
                ins.then_inc(sk_ready, 1)
                mod_part(l + 1, 2 * h + 1)
                if H:
                    act.wait_ge(u_ready, H)
                for e in range(HT):
                    act.wait_ge(num_ready, HT * H + e + 1)
                    ps = mix[:, seg((2 + e) * 512, W)]
                    nc.scalar.copy(h3[:, e, 0:P], ps[:, 0:P])
                    nc.scalar.copy(h3[:, e, LAT:W], ps[:, LAT:W]).then_inc(hs_moved, 1)

            def head_norm(l, h):
                for e in range(HT):
                    if e < HT - 1:
                        act.wait_ge(cen_ready, (HT - 1) * (AH * A_BEFORE[l] + h) + e + 1)
                    else:
                        moved(act, headtile(l, h, N_MEAN))
                    nc.scalar.activation(h3[:, HT + e, :], h3[:, e, :], ACT.Square).then_inc(lnsq_ready, 1)
                move(sqtile(l, h), rstd[:, :], lambda ps: ps[:, 0:W], ACT.Sqrt, bias=eps[:, 0:1])

            def mlstm(l):
                ia = A_BEFORE[l]
                pair_loop(tile("xm", l), AT_, lambda it, e, ps: nc.scalar.copy(
                    xm[:, bass.ds(it * (2 * (W + 2)) + (e * (W + 2) + 1), W)], ps[:, 0:W]))
                t0 = tile("z", l)
                with act.Fori(0, AT_ // 2) as it:
                    for e in range(2):
                        act.wait_ge(acc_ready, it * 2 + (t0 + e + 1))
                        nc.scalar.activation(z[:, bass.ds(it * (2 * W) + e * W, W)], acc[(t0 + e) % 2][:, 0:W],
                                             ACT.Silu).then_inc(acc_moved[(t0 + e) % 2], 1)
                        act.wait_ge(conv_step, it * 6 + 3 * (AT_ * ia + e + 1))
                        tmp = xc[:, bass.ds(it * (2 * W) + e * W, W)]
                        nc.scalar.activation(tmp, tmp, ACT.Silu).then_inc(xc_ready, 1)
                act.wait_ge(late_in, 16 * LATE)
                ps = ready(tile("gate", l, 0))
                nc.scalar.copy(grow[:, 0:P], ps[0:16, 0:P])
                move(tile("gate", l, 0), grow[:, P:TC], lambda ps: ps[0:16, LAT:W])
                move(tile("gate", l, 1), r_ig, lambda ps: ps[0:64, 0:TC], ACT.Identity, bias=rowp[:, ia:ia + 1])
                move(tile("gate", l, 2), r_x, lambda ps: ps[0:64, 0:TC], ACT.Identity, bias=rowp[:, 2 + ia:3 + ia])
                moved(act, tile("gate", l, 2))
                link(nc.scalar.activation(r_t, r_x, ACT.Abs))
                link(nc.scalar.activation(r_t, r_t, ACT.Exp, scale=-1.0))
                nc.scalar.activation(r_t, r_t, ACT.Ln, bias=1.0).then_inc(lse_ready, 1)
                qkv(l, 0, 2)
                act.wait_ge(rows_ready, ia + 1)
                nc.scalar.activation(r_fl[:, :], r_b[:, :], ACT.Exp, scale=-1.0)
                nc.scalar.activation(r_ws[:, 0:P], r_ws[:, 0:P], ACT.Exp).then_inc(rows_exp, 1)
                move(tile("cols", l), cols[:, :], lambda ps: ps[:, 0:256])
                for h in range(AH):
                    head(l, h)
                    if h < AH - 1:
                        qkv(l, h + 1, 0)
                    head_norm(l, h)
                    if h < AH - 1:
                        qkv(l, h + 1, 1)

            def both_sequences(n, out, **kw_):
                ps = ready(n)
                nc.scalar.activation(out[:, 0:P], ps[:, 0:P], ACT.Identity, **kw_)
                move(n, out[:, P:TC], lambda ps: ps[:, LAT:W], ACT.Identity, **kw_)

            def token_values(l, v3_, first=0, end=6):
                for n in range(first, end):
                    move(tile("v", l, n), v3_[:, n % NT, (n // NT) * 512:(n // NT + 1) * 512])

            def gate_path(l, t):
                pair_loop(tile("g", l), KD, lambda it, e, ps: nc.scalar.activation(
                    t[:, bass.ds(it * (2 * W) + e * W, W)], ps[:, 0:W], ACT.Silu))

            def gla(l):
                for h in range(BH):
                    both_sequences(tile("q", l, h), gq3[:, h, :], scale=BDK ** -0.5)
                for h in range(BH):
                    both_sequences(tile("k", l, h), gk3[:, h, :])
                for d in range(2):
                    move(tile("la", l, d), gha[:, d * W:(d + 1) * W], lambda ps: ps[0:RANK, 0:W])
                for n in range(2 * BH):
                    both_sequences(tile("la", l, 2 + n), dx[0][:, n * TC:(n + 1) * TC], bias=vec[:, V_BA + n:V_BA + n + 1])
                moved_all(act, "la", l, 10)
                link(nc.scalar.activation(dx[1][:, :], dx[0][:, :], ACT.Abs))
                token_values(l, gv3, 0, 2)
                link(nc.scalar.activation(dx[1][:, :], dx[1][:, :], ACT.Exp, scale=-1.0))
                token_values(l, gv3, 2, 3)
                nc.scalar.activation(dx[1][:, :], dx[1][:, :], ACT.Ln, bias=1.0).then_inc(xla_ready, 1)
                token_values(l, gv3, 3, 6)
                act.wait_ge(kd_ready, 1)
                nc.scalar.activation(kf[:, :], kf[:, :], ACT.Exp, scale=1.0 / B_TAU).then_inc(ke_ready, 1)

                def states():
                    for n in range(2):
                        move(tile("state", l, n), kft[:, n * 512:(n + 1) * 512])
                    for n in range(4):
                        move(tile("state", l, 2 + n), gst[:, n * 512:(n + 1) * 512])

                for n, level in enumerate(range(LEVELS + 1, 0, -1)):
                    tc = BH * (NLAT if level > LEVELS else TC)
                    half = 2 ** (level - 1)
                    fq, fk, df, db = (t[level % 2][:, e * BH * TC:e * BH * TC + tc].rearrange(
                        "p (b s t) -> p b s t", s=2, t=half) for t in (fqk, dx) for e in range(2))
                    act.wait_ge(dist_ready, n + 1)
                    if n >= 2:
                        act.wait_ge(att_ready, n - 1)
                    nc.scalar.activation(fq[:, :, 1], df[:, :, 1], ACT.Exp, scale=1.0 / B_TAU)
                    nc.scalar.activation(fq[:, :, 0], db[:, :, 0], ACT.Exp, scale=1.0 / B_TAU)
                    nc.scalar.activation(fk[:, :, 0], df[:, :, 0], ACT.Exp, scale=-1.0 / B_TAU)
                    nc.scalar.activation(fk[:, :, 1], db[:, :, 1], ACT.Exp, scale=-1.0 / B_TAU).then_inc(fac_ready, 1)
                    if n == 0:
                        gate_path(l, gr)
                    if n == 1:
                        states()
                    if n >= 2:
                        mod_part(l + 1, n - 2)
                act.wait_ge(att_ready, LEVELS)
                nc.scalar.mul(fqk[0][:, 0:BH * TC], gq[:, :], 2.0).then_inc(q2_ready, 1)
                nc.scalar.activation(gq0, gb4[:, :, :, P:TC], ACT.Exp, scale=1.0 / B_TAU).then_inc(q0e_ready, 1)
                act.wait_ge(gst_out, 16)
                for n in range(2 * BH):
                    act.wait_ge(o_ready, n + 1)
                    nc.scalar.copy(go3[:, n, :], mix[:, seg((3 + n) % 6 * 512, TC)]).then_inc(o_moved, 1)
                    if n % 2:
                        h = n // 2
                        act.wait_ge(o_moved, n + 1)
                        nc.scalar.activation(gsq[:, n - 1:n + 1, :], go3[:, n - 1:n + 1, :], ACT.Square,
                                             scale=BDV ** -0.5).then_inc(osq_ready, 1)
                        if h:
                            rms(l, h - 1)
                for n in range(MOD_CHUNKS - 2, MOD_CHUNKS):
                    mod_part(l + 1, n)
                rms(l, BH - 1)

            def rms(l, h):
                if h:
                    act.wait_ge(ub_ready, h)
                move(rmstile(l, h), rstd[:, 0:TC], lambda ps: ps[:, 0:TC], ACT.Sqrt, bias=eps[:, 0:1])

            def natten(l):
                def query_tile(it, e, ps):
                    nc.scalar.copy(cq[:, bass.ds(it * (2 * W) + e * W, LAT)], ps[:, 0:LAT])
                    return nc.scalar.copy(
                        cq[:, bass.ds(it * (2 * W) + (e * W + LAT), NLAT)].rearrange("p (q t) -> p q t", q=2),
                        ps[:, LAT:W].rearrange("p (q t) -> p q t", q=2)[:, :, ::-1])

                for s, (name, x) in enumerate((("q", cq), ("k", ck))):
                    pair_loop(tile(name, l), KD, query_tile if s == 0 else lambda it, e, ps: nc.scalar.copy(
                        ck[:, bass.ds(it * (2 * W) + e * W, W)], ps[:, 0:W]))
                    if s == 0:
                        moved_all(act, name, l, KD)
                        nc.scalar.activation(cqr[:, :], x, ACT.Square).then_inc(csq_ready, 1)
                for k in range(KD):
                    move(tile("rmsq", l, k), cqr3[:, k, :], lambda ps: ps[:, 0:W], ACT.Sqrt, bias=eps[:, 0:1])
                moved_all(act, "k", l, KD)
                nc.scalar.activation(ckrt[:, :], ck, ACT.Square).then_inc(csq_ready, 1)
                token_values(l, cv3)
                for k in range(KD):
                    move(tile("rmsk", l, k), ckr3[:, k, :], lambda ps: ps[:, 0:W], ACT.Sqrt, bias=eps[:, 0:1])
                gate_path(l, cg)
                for n in range(2):
                    move(tile("turn", l, n), ckc[:, n * 512:(n + 1) * 512])
                for n in range(2):
                    move(tile("knew", l, n), knt[:, n * 512:(n + 1) * 512])

                def exps(h):
                    s = h % 2
                    act.wait_ge(mx_ready, h + 1)
                    if h >= 2:
                        act.wait_ge(ct_ready, h - 1)
                    for q, (c, n) in enumerate(((0, P), (P, TC), (P + TC, TC))):
                        ins = nc.scalar.activation(cp[s][:, seg(c, n)], mix[:, seg(q * 512, n)], ACT.Exp,
                                                   bias=cst_[s][:, q:q + 1], accum_out=cst_[s][:, 3 + q:4 + q])
                    ins.then_inc(cx_ready, 1)

                def turned(h):
                    act.wait_ge(ct_ready, h + 1)
                    nc.scalar.copy(cpt[h % 2], mix[:, seg(3 * 512, 896)]).then_inc(cpt_ready, 1)

                for h in range(CH):
                    exps(h)
                    if h:
                        turned(h - 1)
                    if h >= 3 and h % 2:
                        mod_part(l + 1, h // 2 - 1)
                turned(CH - 1)
                mod_part(l + 1, KD - 1)

            for l, kind in enumerate(KINDS):
                if l == 0:
                    mod_part(0, 0)
                    mod_part(0, 1)
                    fold_start(0)
                    for n in range(2, MOD_CHUNKS):
                        mod_part(0, n)
                norm(l)
                if kind == 0 and l:
                    fold_start(l)
                [mlstm, gla, natten][kind](l)
            done_before(act, DEPTH - 1)
            for n in range(2 * NT):
                move(tile("store", 0, n), XIN[n // 2][:, (n % 2) * 512:(n % 2 + 1) * 512])

        @block.vector
        def _(dve):
            steps = [0]

            def link(ins):
                steps[0] += 1
                ins.then_inc(dve_step, 1)
                dve.wait_ge(dve_step, steps[0])

            tt = nc.vector.tensor_tensor
            stt = nc.vector.scalar_tensor_tensor

            for t, x in ((vrow[:, :], 0.0), (rowp[:, :], 0.0), (eps[:, :], EPS), (ones[:, :], 1.0),
                         (ones_d[:, :], 1.0 / D), (ones_h[:, :], 1.0 / ADH),
                         (y3[:, :, NCTX:LAT], 0.0)):
                ins = nc.vector.memset(t, x)
            ins.then_inc(const_dve, 1)

            def mod_vectors(l):
                for n in (MOD_CHUNKS - 2, MOD_CHUNKS - 1):
                    moved(dve, tile(f"modcol{n}", l))
                if l:
                    dve.wait_ge(h_lat, KD * l)
                    moved_all(dve, "out", l - 1, 8)
                link(tt(modv.rearrange("p (c r) -> p c r", r=2), modr.rearrange("p (c r) -> p c r", r=2),
                        vec[:, V_BMOD + 24 * l:V_BMOD + 24 * l + 24].unsqueeze(2).to_broadcast([P, 24, 2]), ALU.add))
                scale = modv[:, 16:32].rearrange("p (k r) -> p k r", r=2)
                stt(scale, scale, 1.0, vec[:, V_NORM + 8 * l:V_NORM + 8 * l + 8].unsqueeze(2).to_broadcast([P, KD, 2]),
                    ALU.add, ALU.mult).then_inc(mod_ready, 1)

            def norm(l):
                for n in range(2):
                    moved(dve, tile("norm", l, n))
                inv = mix[:, 0:W]
                link(nc.vector.reciprocal(inv, rstd[:, :]))
                dve.wait_ge(mod_ready, l + 1)
                for k in range(KD + 1):
                    if k < KD:
                        tt(h3[:, k, :], y3[:, k, :], inv, ALU.mult).then_inc(hraw_ready, 1)
                    if k:
                        dve.wait_ge(hraw_ready, KD * l + k)
                        nc.vector.tensor_scalar(h3[:, k - 1, 0:P], h3[:, k - 1, 0:P], mod_col(1, k - 1, 0),
                                                mod_col(0, k - 1, 0), ALU.mult, ALU.add).then_inc(h_ctx, 1)

            def residual(l):
                t0 = tile("out", l)
                with dve.Fori(0, KD // 2) as it:
                    for e in range(2):
                        ps = acc[(t0 + e) % 2]
                        dve.wait_ge(acc_ready, it * 2 + (t0 + e + 1))
                        for r, (c, n) in enumerate(((0, NCTX), (LAT, NLAT))):
                            yc = y[:, bass.ds(it * (2 * W) + (e * W + c), n)]
                            ins = stt(yc, ps[:, seg(c, n)], modv[:, bass.ds(it * 4 + (2 * (2 * KD + e) + r), 1)], yc,
                                      ALU.mult, ALU.add)
                        ins.then_inc(acc_moved[(t0 + e) % 2], 1)

            def block_diagonal(l, h):
                w5 = wt4.rearrange("p (m o f) -> p m f o", m=3, o=4)
                for m in range(3):
                    ins = tt(bd4[:, m].rearrange("p e (b o) -> p e b o", o=4),
                             w5[:, m, HT * h:HT * h + HT, :].unsqueeze(2).to_broadcast([P, HT, 32, 4]),
                             mask4.unsqueeze(1).unsqueeze(3).to_broadcast([P, HT, 32, 4]), ALU.mult)
                ins.then_inc(bd_ready, 1)

            def prepare(l):
                done_before(dve, l - 1)
                for t in (xm3[:, :, 0:1], xm3[:, :, W + 1:W + 2], gsel, r_ab[:, :], r_m[:, :]):
                    ins = nc.vector.memset(t, 0.0)
                link(ins)
                dve.wait_ge(const_made, CONSTS)
                for x in range(4):
                    ins = nc.vector.tensor_copy(
                        gspread[:, seg(x * P, P)].rearrange("p (b y) -> p b y", y=4),
                        ident.rearrange("p (b y) -> p b y", y=4)[:, :, x:x + 1].to_broadcast([P, P // 4, 4]))
                ins.then_inc(spread_made, 1)
                nc.vector.tensor_copy(gsel.rearrange("p (n c) -> p n c", c=32)[:, :, 0:AH],
                                      ident[0:16, 0:16].rearrange("p (n c) -> p n c", c=AH)).then_inc(gsel_ready, 1)
                dve.wait_ge(mask_ready, A_BEFORE[l] + 1)
                for t in range(2):
                    moved(dve, tile("fold", l, t))
                w5 = wt4.rearrange("p (m o f) -> p m f o", m=3, o=4)
                for n in range(12):
                    x, m = divmod(n, 3)
                    t = tile(f"fold{x}", l, m)
                    g_ = g4[:, :, m // 2, :]
                    out = g_ if x == 0 and m != 1 else rd[n % 2][:, 0:256].rearrange("p (f n) -> p f n", n=16)
                    dve.wait_ge(acc_ready, t + 1)
                    tt(out, acc[t % 2][:, 0:256].rearrange("p (f n) -> p f n", n=16),
                       w5[:, m, :, x].unsqueeze(2).to_broadcast([P, AT_, 16]), ALU.mult).then_inc(acc_moved[t % 2], 1)
                    if x or m == 1:
                        moved(dve, t)
                        ins = tt(g_, g_, out, ALU.add)
                        if n < 11:
                            link(ins)
                ins.then_inc(gfold_ready, 1)

            def conv(l):
                ia = A_BEFORE[l]
                t0 = tile("xm", l)
                with dve.Fori(0, AT_ // 2) as it:
                    for e in range(2):
                        def x(shift):
                            return xm[:, bass.ds(it * (2 * (W + 2)) + (e * (W + 2) + shift), W)]

                        def w(row):
                            return vec[:, bass.ds(it * 2 + (row + e), 1)]

                        out = xc[:, bass.ds(it * (2 * W) + e * W, W)]
                        n = 3 * (AT_ * ia + e)
                        dve.wait_ge(acc_moved[(t0 + e) % 2], it + ((t0 + e) // 2 + 1))
                        nc.vector.tensor_scalar(out, x(1), w(V_CW + (3 * ia + 1) * AT_), w(V_CB + ia * AT_),
                                                ALU.mult, ALU.add).then_inc(conv_step, 1)
                        dve.wait_ge(conv_step, it * 6 + (n + 1))
                        stt(out, x(0), w(V_CW + 3 * ia * AT_), out, ALU.mult, ALU.add).then_inc(conv_step, 1)
                        dve.wait_ge(conv_step, it * 6 + (n + 2))
                        stt(out, x(2), w(V_CW + (3 * ia + 2) * AT_), out, ALU.mult, ALU.add).then_inc(conv_step, 1)

            DIRS = ((0, slice(0, AH)), (1, slice(32, 32 + AH)))

            def gate_rows(l):
                ia = A_BEFORE[l]
                for t_, x in ((r_keep, 1.0), (r_ones, 1.0), (r_ws, 0.0)):
                    ins = nc.vector.memset(t_, x)
                link(ins)
                nc.vector.memset(r_keep[0:AH, P:P + 1], 0.0)
                nc.vector.memset(r_keep[32:32 + AH, P - 1:P], 0.0)
                dve.wait_ge(lse_ready, ia + 1)
                dve.wait_ge(late_in, 16 * LATE)
                link(stt(r_x, r_x, 0.0, r_t, ALU.min, ALU.subtract))
                for d, r in DIRS:
                    way = slice(None, None, -1) if d else slice(None)
                    ins = nc.vector.tensor_tensor_scan(r_b[r, way], r_keep[r, way], r_x[r, way], 0.0, ALU.mult, ALU.add)
                link(ins)
                for d, r in DIRS:
                    ins = tt(r_a[r, :], r_ig[r, :], r_b[r, :], ALU.subtract)
                link(ins)
                for d, r in DIRS:
                    for first, n, start in ((0, NCTX, 0.0), (NCTX, NLAT, rowp[r, 4 + ia:5 + ia])):
                        way = slice(first + n - 1, first - 1 if first else None, -1) if d else seg(first, n)
                        ins = nc.vector.tensor_tensor_scan(r_m[r, way], r_ones[r, way], r_a[r, way], start,
                                                           ALU.mult, ALU.max)
                link(ins)
                for d, r in DIRS:
                    tt(r_b[r, :], r_b[r, :], r_m[r, :], ALU.add)
                    end = 0 if d else P - 1
                    ins = nc.vector.tensor_scalar(r_ws[r, 0:P], r_a[r, 0:P], r_m[r, end:end + 1], None, ALU.subtract)
                ins.then_inc(rows_ready, 1)

            def head(l, h):
                ia = A_BEFORE[l]
                H = AH * ia + h
                moved(dve, tile("cols", l))
                dve.wait_ge(bcast_ready, H + 1)
                for d, mask in enumerate((mask_f, mask_b)):
                    dve.wait_ge(w_ready, 2 * H + d + 1)
                    m = mix[:, seg((2 + d) * 512, TC)]
                    for t, (c, n, m0) in enumerate(((0, P, P), (P, NLAT, P), (P, NLAT, 0))):
                        a = cols[:, t * 64 + 32 * d + h:t * 64 + 32 * d + h + 1]
                        ins = stt(pm[d][:, seg((0, P, TC)[t], n)], m[:, seg(c, n)], a, mask[:, seg(m0, n)],
                                  ALU.subtract, ALU.max)
                    ins.then_inc(e_ready, 1)
                t = headtile(l, h, N_QN)
                dve.wait_ge(acc_ready, t + 1)
                for d in range(2):
                    ins = tt(rd[d][:, P:TC], wi[d][:, :], acc[t % 2][:, d * NLAT:(d + 1) * NLAT], ALU.mult)
                ins.then_inc(acc_moved[t % 2], 1)
                dve.wait_ge(s_ready, H + 1)
                for d in range(2):
                    dve.wait_ge(x_ready, 2 * H + d + 1)
                    tt(pm[d][:, 0:TC], pm[d][:, 0:TC], mix[:, 0:TC], ALU.mult)
                    tt(pm[d][:, TC:640], pm[d][:, TC:640], mix[:, 512:512 + NLAT], ALU.mult).then_inc(p_ready, 1)
                for d in range(2):
                    den = mix[:, seg((2 + d) * 512, TC)]
                    dve.wait_ge(den_ready, 2 * H + d + 1)
                    stt(fl[d][:, 0:P], den[:, 0:P], -1.0, fl[d][:, 0:P], ALU.mult, ALU.max)
                    ins = tt(rd[d][:, P:TC], den[:, P:TC], rd[d][:, P:TC], ALU.add)
                link(ins)
                for d in range(2):
                    ins = stt(fl[d][:, P:TC], rd[d][:, P:TC], -1.0, fl[d][:, P:TC], ALU.mult, ALU.max)
                link(ins)
                for d in range(2):
                    tt(rd[d][:, 0:P], mix[:, seg((2 + d) * 512, P)], fl[d][:, 0:P], ALU.max)
                    ins = tt(rd[d][:, P:TC], rd[d][:, P:TC], fl[d][:, P:TC], ALU.max)
                link(ins)
                for d in range(2):
                    link(nc.vector.reciprocal(rd[d][:, :], rd[d][:, :]))
                    link(tt(wi[d][:, :], wi[d][:, :], rd[d][:, P:TC], ALU.mult))
                    tt(qs3[d], aq3[:, :, LAT:W], wi[d].unsqueeze(1).to_broadcast([P, HT, NLAT]), ALU.mult
                       ).then_inc(qs_ready, 1)
                dve.wait_ge(p_ready, 2 * H + 2)
                for d in range(2):
                    tt(pm[d][:, 0:P], pm[d][:, 0:P], rd[d][:, 0:P], ALU.mult)
                    both = pm[d][:, P:640].rearrange("p (s t) -> p s t", s=2)
                    ins = tt(both, both, rd[d][:, P:TC].unsqueeze(1).to_broadcast([P, 2, NLAT]), ALU.mult)
                link(ins)
                tt(pm[0][:, :], pm[0][:, :], pm[1][:, :], ALU.add).then_inc(a_ready, 1)
                if h < AH - 1:
                    block_diagonal(l, h + 1)
                hs = h3[:, 0:HT, :]
                t = headtile(l, h, N_MEAN)
                dve.wait_ge(acc_ready, t + 1)
                for e in range(HT):
                    tt(h3[:, e, :], h3[:, e, :], acc[t % 2][:, 0:W], ALU.subtract
                       ).then_inc(cen_ready if e < HT - 1 else acc_moved[t % 2], 1)
                dve.wait_ge(cen_ready, (HT - 1) * (H + 1))
                moved(dve, t)
                moved(dve, sqtile(l, h))
                link(nc.vector.reciprocal(rstd[:, :], rstd[:, :]))
                link(tt(hs, hs, rstd.unsqueeze(1).to_broadcast([P, HT, W]), ALU.mult))
                dve.wait_ge(sk_ready, H + 1)
                for e in range(HT):
                    v = V_OG + ia * AT_ + HT * h + e
                    ins = stt(h3[:, e, :], h3[:, e, :], vec[:, v:v + 1], xc3[:, HT * h + e, :], ALU.mult, ALU.add)
                link(ins)
                zh = z3[:, HT * h:HT * h + HT, :]
                tt(zh, zh, hs, ALU.mult).then_inc(u_ready, 1)

            def mlstm(l):
                conv(l)
                block_diagonal(l, 0)
                gate_rows(l)
                for h in range(AH):
                    head(l, h)

            def gla(l):
                copy = nc.vector.tensor_copy
                done_before(dve, l - 1)
                for d in range(2):
                    ins = nc.vector.memset(keep[d], 1.0)
                link(ins)
                nc.vector.memset(keep[0][:, P:P + 1], 0.0)
                nc.vector.memset(keep[1][:, P - 1:P], 0.0)
                dve.wait_ge(gmask_ready, 1)
                link(tt(gxor, gxor, gxs, ALU.bitwise_xor))
                for level in range(LEVELS):
                    ins = nc.vector.tensor_scalar(gmask[:, level * P:(level + 1) * P], gxor, float(2 ** level), None,
                                                  ALU.is_lt)
                link(ins)
                dve.wait_ge(xla_ready, 1)
                link(stt(dx[0], dx[0], 0.0, dx[1], ALU.min, ALU.subtract))
                for n in range(2 * BH):
                    d = n // BH
                    c = n * TC
                    way = slice(c + TC - 1, c - 1 if c else None, -1) if d else seg(c, TC)
                    ins = nc.vector.tensor_tensor_scan(gb[:, way], keep[d][:, ::-1] if d else keep[d],
                                                       dx[0][:, way], 0.0, ALU.mult, ALU.add)
                link(ins)
                for d in range(2):
                    end = 0 if d else P - 1
                    ins = tt(kf[:, d * 512:(d + 1) * 512].rearrange("p (h t) -> p h t", h=BH),
                             gb4[:, d, :, end:end + 1].to_broadcast([P, BH, P]), gb4[:, d, :, 0:P], ALU.subtract)
                ins.then_inc(kd_ready, 1)

                def distance(n, level):
                    if n >= 2:
                        dve.wait_ge(fac_ready, n - 1)
                    size = 2 ** level
                    for d in range(2):
                        if level > LEVELS:
                            src = gb4[:, d, :, P:TC]
                            tc = BH * NLAT
                        else:
                            src = gb[:, d * BH * TC:(d + 1) * BH * TC].rearrange("p (b t) -> p b t", t=size)
                            tc = BH * TC
                        mid = size // 2 - 1 + d
                        ins = tt(dx[level % 2][:, d * BH * TC:d * BH * TC + tc].rearrange("p (b t) -> p b t", t=size),
                                 src, src[:, :, mid:mid + 1].to_broadcast([P, tc // size, size]), ALU.subtract)
                    ins.then_inc(dist_ready, 1)

                def attention(n, level):
                    dve.wait_ge(att_ready, n + 1)
                    if n:
                        dve.wait_ge(att_moved, n)
                    half = (level % 2) * 3 * 512
                    if level > LEVELS:
                        ins = copy(gax, mix[:, seg(half, 2 * BH * P)])
                    elif level == LEVELS:
                        ins = copy(gat, mix[:, seg(half, BH * TC)])
                    else:
                        ins = nc.vector.copy_predicated(
                            gat.rearrange("p (n t) -> p n t", t=P),
                            gmask[:, level * P:(level + 1) * P].unsqueeze(1).to_broadcast([P, BH * NT, P]),
                            mix[:, seg(half, BH * TC)].rearrange("p (n t) -> p n t", t=P))
                    ins.then_inc(att_moved, 1)

                distance(0, LEVELS + 1)
                dve.wait_ge(ke_ready, 1)
                for d in range(2):
                    kd = kf[:, d * 512:(d + 1) * 512].rearrange("p (h t) -> p h t", h=BH)
                    ins = tt(kd, kd, gk3[:, :, 0:P], ALU.mult)
                ins.then_inc(kf_ready, 1)
                for n, level in enumerate(range(LEVELS + 1, 0, -1)):
                    if level > 1:
                        distance(n + 1, level - 1)
                    dve.wait_ge(fac_ready, n + 1)
                    if level > LEVELS:
                        f = fqk[level % 2][:, 0:BH * NLAT].rearrange("p (h t) -> p h t", h=BH)
                        tt(f, f, gq3[:, :, P:TC], ALU.mult).then_inc(lq_ready, 1)
                    else:
                        f = fqk[level % 2][:, 0:BH * TC]
                        tt(f, f, gq, ALU.mult).then_inc(lq_ready, 1)
                    if n:
                        attention(n - 1, level + 1)
                attention(LEVELS, 1)
                attention(LEVELS + 1, 0)
                dve.wait_ge(q0e_ready, 1)
                for d in range(2):
                    ins = tt(gq0[:, d], gq0[:, d], gq3[:, :, P:TC], ALU.mult)
                ins.then_inc(q0_ready, 1)
                for h in range(BH):
                    moved(dve, rmstile(l, h))
                    link(nc.vector.reciprocal(rstd[:, 0:TC], rstd[:, 0:TC]))
                    for e in range(2):
                        n = 2 * h + e
                        ins = stt(go3[:, n, :], go3[:, n, :], vec[:, V_BOG + n:V_BOG + n + 1], rstd[:, 0:TC],
                                  ALU.mult, ALU.mult)
                    link(ins)
                    for c, w, g in ((0, P, 0), (P, NLAT, LAT)):
                        r_ = gr3[:, 2 * h:2 * h + 2, seg(g, w)]
                        ins = tt(r_, r_, go3[:, 2 * h:2 * h + 2, seg(c, w)], ALU.mult)
                    ins.then_inc(ub_ready, 1)

            def natten(l):
                done_before(dve, l - 1)
                link(nc.vector.memset(hones, 0.0))
                nc.vector.memset(hones[0:CDH, 0:CDH], 1.0 / CDH)
                link(nc.vector.memset(hones[CDH:P, CDH:P], 1.0 / CDH))
                nc.vector.tensor_scalar(cqg, vec[:, V_QG:V_QG + 1], CDH ** -0.5, None, ALU.mult).then_inc(hones_ready, 1)
                dve.wait_ge(hones_ready, 1)
                for name, x3, r3, gain in (("rmsq", cq3, cqr3, cqg), ("rmsk", ck3, ckr3, vec[:, V_KG:V_KG + 1])):
                    for k in range(KD):
                        moved(dve, tile(name, l, k))
                        link(nc.vector.reciprocal(r3[:, k, :], r3[:, k, :]))
                        stt(x3[:, k, :], x3[:, k, :], gain, r3[:, k, :], ALU.mult, ALU.mult).then_inc(qkn_ready, 1)

                def maxima(h):
                    st_ = cst_[h % 2]
                    dve.wait_ge(cs_ready, h + 1)
                    for q, n in enumerate((P, TC, TC)):
                        ins = nc.vector.tensor_reduce(st_[:, q:q + 1], mix[:, seg(q * 512, n)], AX, ALU.max)
                    link(ins)
                    nc.vector.tensor_scalar(st_[:, 0:3], st_[:, 0:3], -1.0, None, ALU.mult).then_inc(mx_ready, 1)

                def normalise(h):
                    st_ = cst_[h % 2]
                    dve.wait_ge(cx_ready, h + 1)
                    link(nc.vector.reciprocal(st_[:, 3:6], st_[:, 3:6]))
                    for q, (c, n) in enumerate(((0, P), (P, TC), (P + TC, TC))):
                        ins = nc.vector.tensor_scalar(cp[h % 2][:, seg(c, n)], cp[h % 2][:, seg(c, n)],
                                                      st_[:, 3 + q:4 + q], None, ALU.mult)
                    ins.then_inc(cpn_ready, 1)

                def gated(k):
                    t = tile(f"attn{k}", l)
                    dve.wait_ge(acc_ready, t + 1)
                    g_ = cg3[:, k, 0:P]
                    tt(g_, g_, acc[t % 2][:, 0:P], ALU.mult)
                    g_ = cg3[:, k, LAT:W].rearrange("p (q t) -> p q t", q=2)
                    ins = tt(g_, g_, acc[t % 2][:, P:TC].rearrange("p (q t) -> p q t", q=2)[:, :, ::-1], ALU.mult)
                    ins.then_inc(acc_moved[t % 2], 1)

                maxima(0)
                for h in range(CH):
                    normalise(h)
                    if h + 1 < CH:
                        maxima(h + 1)
                    if h and h % 2 == 0:
                        gated(h // 2 - 1)
                gated(KD - 1)

            for l, kind in enumerate(KINDS):
                if l == 0:
                    prepare(0)
                mod_vectors(l)
                norm(l)
                if kind == 0 and l:
                    prepare(l)
                [mlstm, gla, natten][kind](l)
                residual(l)

        @block.gpsimd
        def _(pool):
            steps = [0]

            def link(ins):
                steps[0] += 1
                ins.then_inc(pool_step, 1)
                pool.wait_ge(pool_step, steps[0])

            def select(t, pattern, base, mult, fill, op=ALU.is_ge):
                return nc.gpsimd.affine_select(out=t, in_=t, pattern=pattern, compare_op=op, fill=fill,
                                               base=base, channel_multiplier=mult)

            link(nc.gpsimd.memset(ident[:, :], 0.0))
            select(ident[:, :], [[-1, P]], 0, 1, 1.0, ALU.not_equal).then_inc(const_made, 1)

            def mlstm(l):
                ia = A_BEFORE[l]
                j = ia
                done_before(pool, l - 1)
                for n, w in enumerate((i["a_w_ig"], i["a_w_fg"])):
                    for d in range(2):
                        pool.dma_start(wg_rows[:, seg((2 * n + d) * 512, 512)],
                                       w[j, d].rearrange("(f q) h -> f (q h)", q=P)).then_inc(fold_in, 16)
                for n, w in enumerate((i["a_wq"], i["a_wk"], i["a_wv"])):
                    pool.dma_start(wt_rows[:, seg(n * 512, 512)],
                                   w[j].rearrange("(f b) x o -> f (b x o)", b=32)).then_inc(fold_in, 16)
                for t, x in ((mask_f[:, 0:P], BIG), (mask_f[:, P:TC], 0.0), (mask_b[:, 0:2 * P], 0.0),
                             (mask_b[:, 2 * P:TC], BIG), (mask4[:, :], 1.0)):
                    ins = nc.gpsimd.memset(t, x)
                link(ins)
                select(mask_f[:, P:2 * P], [[1, P]], 0, -1, BIG)
                select(mask_b[:, P:2 * P], [[-1, P]], 0, 1, BIG)
                link(select(mask4[:, :], [[-4, 32]], 0, 1, 0.0))
                select(mask4[:, :], [[4, 32]], 3, -1, 0.0).then_inc(mask_ready, 1)
                pool.wait_ge(rows_ready, ia + 1)
                for d in range(2):
                    col = 0 if d else P - 1
                    pool.dma_start(o["new_m"][0, j, d].rearrange("(h x) -> h x", x=1),
                                   r_b[32 * d:32 * d + AH, col:col + 1]).then_inc(m_out, 16)
                moved(pool, tile("cols", l))
                for h in range(AH):
                    moved(pool, qkv_tiles(l, h)[11])
                    for d in range(2):
                        nc.gpsimd.tensor_scalar(kw[d][:, :], ktok[:, :], cols[:, seg(192 + 32 * d + h, 1)], None,
                                                ALU.mult).then_inc(kw_ready, 1)
                    for q in range(4):
                        for e in range(2):
                            moved(pool, headtile(l, h, N_ST + 2 * q + e))
                        dst = o["new_C"][0, j, q // 2, h].rearrange("(k p) n -> p k n", p=P)
                        pool.dma_start(dst[:, 2 * (q % 2):2 * (q % 2) + 2, :],
                                       cst[q % 2].rearrange("p (k n) -> p k n", k=2)).then_inc(cst_out[q % 2], 16)
                    moved(pool, headtile(l, h, N_N))
                    pool.dma_start(o["new_n"][0, j, :, h], nst[:, :]).then_inc(nst_out, 16)

            def gla(l):
                done_before(pool, l - 1)
                for d in range(2):
                    pool.dma_start(ga14[:, :, d, :], i["b_w_a1"][0, d].rearrange("(k p) n -> p k n", p=P)).then_inc(b_in, 16)
                    pool.dma_start(ga2[:, seg(d * BH * BDK, BH * BDK)], i["b_w_a2"][0, d]).then_inc(b_in, 16)
                pool.dma_start(gs03, i["state_gla_S"][0, 0].rearrange("d h k v -> k (d h) v")).then_inc(b_in, 16)
                nc.gpsimd.iota(gxor, [[1, P]], base=0, channel_multiplier=0)
                nc.gpsimd.iota(gxs, [[0, P]], base=0, channel_multiplier=1).then_inc(gmask_ready, 1)
                for n, level in enumerate(range(LEVELS + 1, 0, -1)):
                    pool.wait_ge(fac_ready, n + 1)
                    f = fqk[level % 2][:, BH * TC:2 * BH * TC]
                    if level > LEVELS:
                        f = f[:, 0:BH * NLAT].rearrange("p (h t) -> p h t", h=BH)
                        nc.gpsimd.tensor_tensor(f, f, gk3[:, :, P:TC], ALU.mult).then_inc(lk_ready, 1)
                    else:
                        nc.gpsimd.tensor_tensor(f, f, gk, ALU.mult).then_inc(lk_ready, 1)
                    if n == 2:
                        for m in range(2, 6):
                            moved(pool, tile("state", l, m))
                        pool.dma_start(o["new_S"][0, 0].rearrange("d h k v -> k (d h) v"),
                                       gst.rearrange("p (n v) -> p n v", v=BDV)).then_inc(gst_out, 16)

            def natten(l):
                done_before(pool, l - 1)
                for t, name in ((ckr, "cache_na_k"), (cvc, "cache_na_v")):
                    pool.dma_start(t.rearrange("p (h c) -> p h c", h=CH), i[name][0, 0].rearrange("h t c -> t h c")
                                   ).then_inc(c_in, 16)
                link(nc.gpsimd.memset(zrow, 0.0))
                for h in range(CH):
                    pool.dma_start(zrow[7 * h:7 * h + 7, GW - WINW:GW - WINW + 31], i["c_rpb"][0, h, 4:11, :]
                                   ).then_inc(rpb_in, 16)
                pool.wait_ge(rpb_in, 16 * CH)
                pool.dma_start(rpb_rows, zrow).then_inc(rpb_out, 16)
                pool.wait_ge(rpb_out, 16)
                for r in range(ROWS):
                    for kr in range(ROWS):
                        src = bass.AP(tensor=rpb_rows.tensor, offset=(kr - r + 3) * P,
                                      ap=[[1, GW], [7 * P, CH], [1, GW]])
                        pool.dma_start(cb4[seg(GW * (1 - r % 2), GW), r // 2, :, kr * GW:(kr + 1) * GW], src
                                       ).then_inc(bias_in, 16)
                link(nc.gpsimd.memset(cwin, 0.0))
                for half in range(2):
                    p = seg(GW * half, GW)
                    link(select(cwin[p, 0:GW - WINW], [[1, GW - WINW]], WINW // 2 - (GW - 1), 1, -BIG))
                    ins = select(cwin[p, WINW:GW], [[-1, GW - WINW]], GW - 1 + WINW // 2 - 1 - WINW, -1, -BIG)
                link(ins)
                pool.wait_ge(bias_in, 16 * ROWS * ROWS)
                both = cb.rearrange("p (n c) -> p n c", c=GW)
                nc.gpsimd.tensor_tensor(both, both, cwin.unsqueeze(1).to_broadcast([P, 2 * CH * ROWS, GW]), ALU.add
                                        ).then_inc(bias_ready, 1)
                moved_all(pool, "v", l, 6)
                pool.dma_start(o["new_v"][0, 0].rearrange("h t c -> t h c"),
                               cv3[:, 0, :].rearrange("p (h c) -> p h c", h=CH)).then_inc(kv_out, 16)
                moved_all(pool, "knew", l, 2)
                pool.dma_start(o["new_k"][0, 0].rearrange("h t c -> t h c"),
                               knt.rearrange("p (h c) -> p h c", h=CH)).then_inc(kv_out, 16)

            for l, kind in enumerate(KINDS):
                [mlstm, gla, natten][kind](l)
            done_before(pool, DEPTH - 1)


_INS = ["x_prompt", "x_sample", "state_mlstm_C", "state_mlstm_n", "state_mlstm_m", "state_gla_S", "cache_na_k",
        "cache_na_v", "c", "c_ctx", "norm_g", "w_mod", "b_mod", "a_w_in", "a_conv_w", "a_conv_b", "a_wq", "a_wk",
        "a_wv", "a_w_ig", "a_b_ig", "a_w_fg", "a_b_fg", "a_out_g", "a_skip", "a_w_out", "b_w_in", "b_w_a1",
        "b_w_a2", "b_b_a", "b_out_g", "b_w_out", "c_w_in", "c_q_g", "c_k_g", "c_rpb", "c_w_out"]
_OUTS = {"y_prompt": (1, 128, 1024), "y_sample": (1, 256, 1024), "new_C": (1, 2, 2, 4, 512, 512),
         "new_n": (1, 2, 2, 4, 512), "new_m": (1, 2, 2, 4), "new_S": (1, 1, 2, 4, 128, 256),
         "new_k": (1, 1, 16, 128, 64), "new_v": (1, 1, 16, 128, 64)}


def kernel(**inputs):
    import numpy as _np
    import concourse.bacc as _bacc
    from concourse import mybir as _mybir
    from concourse.bass_utils import run_bass_kernel_spmd as _run

    nc = _bacc.Bacc("TRN2", target_bir_lowering=False, num_devices=1)
    arrays, ins, outs = {}, {}, {}
    for name in _INS:
        a = _np.ascontiguousarray(inputs[name])
        arrays[f"in_{name}"] = a
        ins[name] = nc.dram_tensor(f"in_{name}", a.shape, _mybir.dt.from_np(a.dtype), kind="ExternalInput").ap()
    for name, shape in _OUTS.items():
        outs[name] = nc.dram_tensor(f"out_{name}", shape, _mybir.dt.float32, kind="ExternalOutput").ap()
    trunk(nc, ins, outs)
    r = _run(nc, [arrays], core_ids=[0])
    return tuple(r.results[0][f"out_{name}"] for name in _OUTS)
```
